# Optimizing a Trainium2 kernel written in Bass

```python
import jax, jax.numpy as jnp
from jax import lax
import numpy as np

D_MODEL = 1024
BATCH = 1
SEQ = 512
DEPTH = 1

HEAD_DIM = 64
N_HEADS_SB = 8
N_HEADS_FOX = 8
D_SB = N_HEADS_SB * HEAD_DIM
D_FOX = N_HEADS_FOX * HEAD_DIM
D_MIX = D_SB + D_FOX
D_IN = 3 * D_SB + 3 * D_FOX + N_HEADS_FOX
D_FF = 2816
D_PLE = 256
BLOCK_Q = 128
EPS = 1e-6
FFN_RES_WEIGHT = 0.5
FORGET_BIAS_INIT = 3.0

kernel_name = "hybrid_stickbreak_fox_macaron_block"

def rms_norm(x, g):
    xf = x.astype(jnp.float32)
    y = xf * lax.rsqrt(jnp.mean(xf * xf, axis=-1, keepdims=True) + EPS)
    return (y * g.astype(jnp.float32)).astype(x.dtype)

def swiglu(h, w_gate, w_up, w_down):
    return (jax.nn.silu(h @ w_gate) * (h @ w_up)) @ w_down

def split_heads(t, n_heads):
    b, s, _ = t.shape
    return t.reshape(b, s, n_heads, HEAD_DIM).transpose(0, 2, 1, 3)

def merge_heads(t):
    b, h, s, d = t.shape
    return t.transpose(0, 2, 1, 3).reshape(b, s, h * d)

def stick_breaking_block(q_blk, k_pre, v_pre, q_start):
    n_q = q_blk.shape[2]
    n_k = k_pre.shape[2]
    z = jnp.einsum('bhqd,bhkd->bhqk', q_blk.astype(jnp.float32), k_pre.astype(jnp.float32)) * (HEAD_DIM ** -0.5)
    t_idx = q_start + jnp.arange(n_q)[:, None]
    s_idx = jnp.arange(n_k)[None, :]
    causal = s_idx < t_idx
    log_1m_beta = jnp.where(causal, jax.nn.log_sigmoid(-z), 0.0)
    tail = lax.cumsum(log_1m_beta, axis=3, reverse=True) - log_1m_beta
    a = jnp.where(causal, jnp.exp(jax.nn.log_sigmoid(z) + tail), 0.0)
    return jnp.einsum('bhqk,bhkd->bhqd', a, v_pre.astype(jnp.float32))

def forgetting_block(q_blk, k_pre, v_pre, fcum_q, fcum_k, q_start):
    n_q = q_blk.shape[2]
    n_k = k_pre.shape[2]
    logits = jnp.einsum('bhqd,bhkd->bhqk', q_blk.astype(jnp.float32), k_pre.astype(jnp.float32)) * (HEAD_DIM ** -0.5)
    logits = logits + fcum_q[..., :, None] - fcum_k[..., None, :]
    t_idx = q_start + jnp.arange(n_q)[:, None]
    s_idx = jnp.arange(n_k)[None, :]
    logits = jnp.where(s_idx <= t_idx, logits, -jnp.inf)
    w = jax.nn.softmax(logits, axis=-1)
    return jnp.einsum('bhqk,bhkd->bhqd', w, v_pre.astype(jnp.float32))

def token_mixer(h, w_in, b_forget, sb_group_g, fox_group_g, w_out):
    b, s, _ = h.shape
    proj = h @ w_in
    o = np.cumsum([0, D_SB, D_SB, D_SB, D_FOX, D_FOX, D_FOX, N_HEADS_FOX])
    q_sb = split_heads(proj[..., o[0]:o[1]], N_HEADS_SB)
    k_sb = split_heads(proj[..., o[1]:o[2]], N_HEADS_SB)
    v_sb = split_heads(proj[..., o[2]:o[3]], N_HEADS_SB)
    q_fx = split_heads(proj[..., o[3]:o[4]], N_HEADS_FOX)
    k_fx = split_heads(proj[..., o[4]:o[5]], N_HEADS_FOX)
    v_fx = split_heads(proj[..., o[5]:o[6]], N_HEADS_FOX)
    f_logit = proj[..., o[6]:o[7]].astype(jnp.float32) + b_forget.astype(jnp.float32)
    fcum = lax.cumsum(jax.nn.log_sigmoid(f_logit), axis=1).transpose(0, 2, 1)

    outs_sb, outs_fx = [], []
    for i in range(s // BLOCK_Q):
        s0 = i * BLOCK_Q
        s1 = s0 + BLOCK_Q
        outs_sb.append(stick_breaking_block(q_sb[:, :, s0:s1], k_sb[:, :, :s1], v_sb[:, :, :s1], s0))
        outs_fx.append(forgetting_block(q_fx[:, :, s0:s1], k_fx[:, :, :s1], v_fx[:, :, :s1],
                                        fcum[:, :, s0:s1], fcum[:, :, :s1], s0))
    o_sb = merge_heads(jnp.concatenate(outs_sb, axis=2))
    o_fx = merge_heads(jnp.concatenate(outs_fx, axis=2))
    merged = jnp.concatenate([rms_norm(o_sb, sb_group_g), rms_norm(o_fx, fox_group_g)], axis=-1)
    return merged.astype(h.dtype) @ w_out

def setup_inputs(seed: int = 0) -> dict:
    key = jax.random.key(seed)
    ks = iter(jax.random.split(key, 32))

    def dense(shape, fan_in):
        return jax.random.normal(next(ks), (DEPTH,) + shape, jnp.float32) * (fan_in ** -0.5)

    def gain(dim):
        return 1.0 + 0.02 * jax.random.normal(next(ks), (DEPTH, dim), jnp.float32)

    inp = {}
    inp["x"] = jax.random.normal(next(ks), (BATCH, SEQ, D_MODEL), jnp.float32)
    inp["p"] = jax.random.normal(next(ks), (DEPTH, BATCH, SEQ, D_PLE), jnp.float32)
    inp["ffn1_pre_g"] = gain(D_MODEL)
    inp["ffn1_w_gate"] = dense((D_MODEL, D_FF), D_MODEL)
    inp["ffn1_w_up"] = dense((D_MODEL, D_FF), D_MODEL)
    inp["ffn1_w_down"] = dense((D_FF, D_MODEL), D_FF)
    inp["ffn1_post_g"] = gain(D_MODEL)
    inp["mix_pre_g"] = gain(D_MODEL)
    inp["w_in"] = dense((D_MODEL, D_IN), D_MODEL)
    inp["b_forget"] = FORGET_BIAS_INIT + 0.5 * jax.random.normal(next(ks), (DEPTH, N_HEADS_FOX), jnp.float32)
    inp["sb_group_g"] = gain(D_SB)
    inp["fox_group_g"] = gain(D_FOX)
    inp["w_out"] = dense((D_MIX, D_MODEL), D_MIX)
    inp["mix_post_g"] = gain(D_MODEL)
    inp["ffn2_pre_g"] = gain(D_MODEL)
    inp["ffn2_w_gate"] = dense((D_MODEL, D_FF), D_MODEL)
    inp["ffn2_w_up"] = dense((D_MODEL, D_FF), D_MODEL)
    inp["ffn2_w_down"] = dense((D_FF, D_MODEL), D_FF)
    inp["ffn2_post_g"] = gain(D_MODEL)
    inp["ple_pre_g"] = gain(D_MODEL)
    inp["w_ple_gate"] = dense((D_MODEL, D_MODEL), D_MODEL)
    inp["w_ple_proj"] = dense((D_PLE, D_MODEL), D_PLE)
    inp["ple_post_g"] = gain(D_MODEL)
    return inp

def reference(x, p, ffn1_pre_g, ffn1_w_gate, ffn1_w_up, ffn1_w_down, ffn1_post_g,
              mix_pre_g, w_in, b_forget, sb_group_g, fox_group_g, w_out, mix_post_g,
              ffn2_pre_g, ffn2_w_gate, ffn2_w_up, ffn2_w_down, ffn2_post_g,
              ple_pre_g, w_ple_gate, w_ple_proj, ple_post_g):
    for i in range(DEPTH):
        f1 = swiglu(rms_norm(x, ffn1_pre_g[i]), ffn1_w_gate[i], ffn1_w_up[i], ffn1_w_down[i])
        x = x + FFN_RES_WEIGHT * rms_norm(f1, ffn1_post_g[i])
        m = token_mixer(rms_norm(x, mix_pre_g[i]), w_in[i], b_forget[i],
                        sb_group_g[i], fox_group_g[i], w_out[i])
        x = x + rms_norm(m, mix_post_g[i])
        f2 = swiglu(rms_norm(x, ffn2_pre_g[i]), ffn2_w_gate[i], ffn2_w_up[i], ffn2_w_down[i])
        x = x + FFN_RES_WEIGHT * rms_norm(f2, ffn2_post_g[i])
        gate = jax.nn.sigmoid(rms_norm(x, ple_pre_g[i]) @ w_ple_gate[i])
        e = gate * (p[i] @ w_ple_proj[i])
        x = x + rms_norm(e, ple_post_g[i])
    return x


_drawn_inputs = setup_inputs


def setup_inputs(seed=0):
    import zlib

    import numpy as np

    out = dict(_drawn_inputs(seed))
    spreads = {}
    factors = {'ffn1_pre_g': 3.938,
     'ffn1_post_g': 5.565,
     'mix_pre_g': 3.333,
     'sb_group_g': 23.919,
     'fox_group_g': 24.442,
     'mix_post_g': 12.32,
     'ffn2_pre_g': 24.019,
     'ffn2_post_g': 37.685,
     'ple_pre_g': 33.9,
     'ple_post_g': 24.111}
    for name, (base, spread) in spreads.items():
        noise = np.random.default_rng([zlib.crc32(name.encode()), seed]).standard_normal(out[name].shape)
        drawn = base * np.exp(spread * noise) if base else spread * noise
        out[name] = __import__('jax').numpy.asarray(drawn.astype(out[name].dtype))
    for name, factor in factors.items():
        out[name] = (out[name] * factor).astype(out[name].dtype)
    return out
```

```python
import concourse.bass as bass
from concourse import mybir
from contextlib import ExitStack

P = 128
SEQ = 512
D = 1024
DC = D // P
FF = 2816
FC = FF // P
HEADS = 8
HD = 64
TILES = HEADS // 2
D_PLE = 256
TB = SEQ // P
EPS = 1e-6
MASKED = -1e30

GAINS = [("ffn1_pre_g", 8), ("ffn1_post_g", 8), ("mix_pre_g", 8), ("sb_group_g", 4), ("fox_group_g", 4),
         ("mix_post_g", 8), ("ffn2_pre_g", 8), ("ffn2_post_g", 8), ("ple_pre_g", 8), ("ple_post_g", 8)]
GAIN_AT = {}
GAIN_ROWS = 0
for _name, _rows in GAINS:
    GAIN_AT[_name] = GAIN_ROWS
    GAIN_ROWS += _rows

SLOTS = 4
STEP_UNITS = 8
STEPS = FC // 2
UP_UNITS = STEPS * STEP_UNITS
DOWN_UNITS = 2 * FC
TILE_UNITS = 12
OUT_UNITS = 16
PLE_UNITS = 20
U_UP = [0, UP_UNITS + DOWN_UNITS + TILES * TILE_UNITS + OUT_UNITS]
U_DOWN = [u + UP_UNITS for u in U_UP]
U_MIX = U_DOWN[0] + DOWN_UNITS
U_OUT = U_MIX + TILES * TILE_UNITS
U_PLE = U_DOWN[1] + DOWN_UNITS
UNITS = U_PLE + PLE_UNITS

Z_AT = {0: (0, 0, 512), 1: (1, 0, 384), 3: (1, 384, 128), 2: (2, 0, 256)}
Z_BANKS = [[0], [1, 3], [2]]
Z_W = [512, 512, 256]
Z_COLS = sum(Z_W)
L_AT = {3: (0, 0, 512), 2: (1, 0, 384), 0: (1, 384, 128), 1: (2, 0, 256)}

N_FFN1_PRE, N_FFN1_POST, N_MIX_PRE, N_SB, N_FOX, N_MIX_POST, N_FFN2_PRE, N_FFN2_POST, N_PLE_PRE, N_PLE_POST = range(10)


def build(nc, t, out):
    f32, f32r = mybir.dt.float32, mybir.dt.float32r
    ALU, ACT, AX = mybir.AluOpType, mybir.ActivationFunctionType, mybir.AxisListType.X
    MUL, ADD, SUB, MAX, MIN = ALU.mult, ALU.add, ALU.subtract, ALU.max, ALU.min

    def ds(start, size):
        return bass.ds(start, size)

    with ExitStack() as ctx:
        def sb(name, shape, dt=f32):
            return ctx.enter_context(nc.sbuf_tensor(name, shape, dt))

        def sem(name):
            return ctx.enter_context(nc.semaphore(name))

        def plain(ap):
            return ap.bitcast(f32)

        xT = sb("xT", [P, DC, SEQ])
        xg = sb("xg", [P, 2, DC, SEQ], f32r)
        big = sb("big", [P, 2 * FC, SEQ], f32r)
        w_raw = sb("w_raw", [P, SLOTS, 4 * P])
        w_r = sb("w_r", [P, 2, SLOTS, 4 * P], f32r)
        scratch = sb("scratch", [P, 6912])
        acc = sb("acc", [P, 2, SEQ])
        sq = sb("sq", [P, 2, SEQ])
        rms = sb("rms", [P, 2, SEQ])
        gains = sb("gains", [P, GAIN_ROWS])
        ident = sb("ident", [P, P])
        ones = sb("ones", [P, P])
        const_r = sb("const_r", [P, 5, P], f32r)
        f4 = sb("f4", [P, SEQ], f32r)
        pick = sb("pick", [P, 2, HEADS])
        b_col = sb("b_col", [HEADS, 1])
        eps_col = sb("eps_col", [P, 1])
        stat = sb("stat", [P, 4, TB])

        ident_r, tri_r, full_r, mask_sb, mask_fx = (const_r[:, i, :] for i in range(5))
        h_hi, h_lo = big[:, 0:FC, :], big[:, FC:2 * FC, :]
        H = [h_hi, h_lo]
        qk = {n: [big[:, 2 * i + p, :] for p in range(2)] for i, n in enumerate(["q_sb", "k_sb", "q_fx", "k_fx"])}
        v_r = {n: [big[:, 8 + 2 * i + p, :] for p in range(2)] for i, n in enumerate(["v_sb", "v_fx"])}
        aug = [big[:, 12 + i, :] for i in range(2)]
        wf_r = [big[:, 14:16, :], big[:, 16:18, :]]
        oT = [big[:, 18:26, :], big[:, 26:34, :]]

        wide = big[:, 34:44, :].rearrange("p r n -> p (r n)").rearrange("p (i n) -> p i n", n=Z_COLS)
        sp_r = [wide[:, i, :] for i in range(2)]
        pt_r = [wide[:, 2 + i, :] for i in range(2)]
        pT_r = [big[:, 0:2, :], big[:, 2:4, :]]
        gu = [scratch[:, i * SEQ:(i + 1) * SEQ] for i in range(4)]
        y0 = scratch[:, 2048:2560]
        y_sb = scratch[:, 2560:6656].rearrange("p (c n) -> p c n", n=SEQ)
        x_in = scratch[:, 2560:6656].rearrange("p (b n) -> p b n", n=D)
        p_in = scratch[:, 2560:3584].rearrange("p (b n) -> p b n", n=D_PLE)
        x_out = scratch[:, 0:2048].rearrange("p (b n) -> p b n", n=SEQ)
        hold = scratch[:, 0:3072].rearrange("p (c n) -> p c n", n=SEQ)
        el = scratch[:, 3072:4352]
        spf = scratch[:, 4352:5632]
        pr = scratch[:, 5632:6912]
        wf_raw = scratch[:, 6656:6720].rearrange("p (k n) -> p k n", n=HEADS)
        gains_in = scratch[0:GAIN_ROWS, 1536:1536 + P]
        const_in = scratch[:, 0:5 * P].rearrange("p (i n) -> p i n", n=P)
        scan_ones = el[0:HEADS, 0:SEQ]
        fz, fa, fl = (spf[0:HEADS, 0:SEQ], spf[0:HEADS, SEQ:2 * SEQ], pr[0:HEADS, 0:SEQ])
        outs = [gu[0], gu[1], y0, acc[:, 1, :]] + [y_sb[:, i, :] for i in range(4)]

        bank = [ctx.enter_context(nc.psum_tensor(f"bank{i}", [P, SEQ], f32)) for i in range(8)]
        Z, O_BANK, G_BANK, L_BANKS, T_BANK = bank[0:3], bank[3], bank[4], [bank[5], bank[6]], bank[7]

        gains_loaded, b_loaded, x_loaded, wf_loaded, p_loaded, stored = map(sem, (
            "gains_loaded", "b_loaded", "x_loaded", "wf_loaded", "p_loaded", "stored"))
        raw_loaded = [sem(f"raw_loaded{i}") for i in range(SLOTS)]
        w_hi, w_lo, w_used = sem("w_hi"), sem("w_lo"), sem("w_used")
        zeroed, consts, const_hi = sem("zeroed"), sem("consts"), sem("const_hi")
        gains_t, gains_ready, x_t = sem("gains_t"), sem("gains_ready"), sem("x_t")
        x_ready, xg_hi, xg_lo = sem("x_ready"), sem("xg_hi"), sem("xg_lo")
        squared, acc_zero, added, summed, ln_done, rms_ready = map(sem, (
            "squared", "acc_zero", "added", "summed", "ln_done", "rms_ready"))
        gate_out, up_out, silu_done, h_f, h_hi_s, h_lo_s = map(sem, (
            "gate_out", "up_out", "silu_done", "h_full", "h_hi", "h_lo"))
        y_done, y0_copied, y_scaled = sem("y_done"), sem("y0_copied"), sem("y_scaled")
        wf_zero, wf_hi, wf_lo, f_done, f_step, f_act, f4_ready = map(sem, (
            "wf_zero", "wf_hi", "wf_lo", "f_done", "f_step", "f_act", "f4_ready"))
        hold_ready, qk_hi, qk_lo, v_t, v_hi, v_lo = map(sem, (
            "hold_ready", "qk_hi", "qk_lo", "v_t", "v_hi", "v_lo"))
        z_done, absz, exp_z, lnz, sp_full, sp_hi, sp_lo, tri_done, a_exp, a_hi, a_lo = map(sem, (
            "z_done", "absz", "exp_z", "lnz", "sp_full", "sp_hi", "sp_lo", "tri_done", "a_exp", "a_hi", "a_lo"))
        aug_ready, l_done, neg_max, p_exp, rcp, p_scaled, pt_done, pt_hi, pt_lo = map(sem, (
            "aug_ready", "l_done", "neg_max", "p_exp", "rcp", "p_scaled", "pt_done", "pt_hi", "pt_lo"))
        o_done, o_hi, o_out = sem("o_done"), sem("o_hi"), sem("o_out")
        y_half, y_out = sem("y_half"), sem("y_out")
        p_t, p_hi, p_lo = sem("p_t"), sem("p_hi"), sem("p_lo")
        g_out, sig_done, e_out = sem("g_out"), sem("sig_done"), sem("e_out")
        out_t, out_copied = sem("out_t"), sem("out_copied")

        block = ctx.enter_context(nc.Block())

        @block.sync
        def _(sp):
            sp.dma_start(x_in, t["x"][0].rearrange("(b p) d -> p b d", p=P)).then_inc(x_loaded, 16)
            for name, rows in GAINS:
                sp.dma_start(gains_in[GAIN_AT[name]:GAIN_AT[name] + rows, :],
                             t[name][0].rearrange("(c p) -> c p", p=P)).then_inc(gains_loaded, 16)
            w_in = t["w_in"][0].rearrange("(k p) n -> p k n", p=P)
            sp.dma_start(b_col[:, :], t["b_forget"][0].rearrange("(h o) -> h o", o=1)).then_inc(b_loaded, 16)
            sp.dma_start(wf_raw, w_in[:, :, 6 * 512:6 * 512 + HEADS]).then_inc(wf_loaded, 16)

            def load_unit(u, slot, src, k):
                if not isinstance(u, int) or u >= SLOTS:
                    sp.wait_ge(w_lo, u - SLOTS + 1)
                dst = w_raw[:, slot, :].rearrange("p (k n) -> p k n", k=k)
                sp.dma_start(dst, src).then_inc(raw_loaded[slot], 16)

            def load_up(f):
                w = [t[f"ffn{f + 1}_w_{kind}"][0].rearrange("(k p) n -> p k n", p=P) for kind in ("gate", "up")]

                def step(s):
                    for q in range(4):
                        for kind in range(2):
                            j = 2 * q + kind
                            load_unit(U_UP[f] + STEP_UNITS * s + j, j % SLOTS,
                                      w[kind][:, 2 * q:2 * q + 2, ds(s * 256, 256)], 2)
                step(0)
                with sp.Fori(1, STEPS) as s:
                    step(s)

            def load_down(f):
                w = t[f"ffn{f + 1}_w_down"][0].rearrange("(k p) n -> p k n", p=P)
                with sp.Fori(0, STEPS) as s:
                    for j in range(4):
                        load_unit(U_DOWN[f] + 4 * s + j, j,
                                  w[:, ds(2 * s + j // 2, 1), 512 * (j % 2):512 * (j % 2) + 512], 1)

            load_up(0)
            load_down(0)
            for j in range(TILE_UNITS):
                kh, c = divmod(j, 6)
                load_unit(U_MIX + j, j % SLOTS, w_in[:, 4 * kh:4 * kh + 4, 512 * c:512 * c + P], 4)
            with sp.Fori(1, TILES) as tile:
                for j in range(TILE_UNITS):
                    c, kh = divmod(j, 2)
                    load_unit(U_MIX + TILE_UNITS * tile + j, j % SLOTS,
                              w_in[:, 4 * kh:4 * kh + 4, ds(512 * c + tile * P, P)], 4)
            w_out = t["w_out"][0].rearrange("(k p) n -> p k n", p=P)
            with sp.Fori(0, 4) as i:
                for q in range(4):
                    load_unit(U_OUT + 4 * i + q, q, w_out[:, 2 * q:2 * q + 2, ds(256 * i, 256)], 2)
            load_up(1)
            sp.wait_ge(x_ready, 3 * DC)
            sp.dma_start(p_in, t["p"][0, 0].rearrange("(b p) d -> p b d", p=P)).then_inc(p_loaded, 16)
            load_down(1)
            w_pg = t["w_ple_gate"][0].rearrange("(k p) n -> p k n", p=P)
            w_pp = t["w_ple_proj"][0].rearrange("(k p) n -> p k n", p=P)
            for i in range(4):
                for q in range(5):
                    u = 5 * i + q
                    src = w_pg[:, 2 * q:2 * q + 2, 256 * i:256 * i + 256] if q < 4 else w_pp[:, :, 256 * i:256 * i + 256]
                    load_unit(U_PLE + u, u % SLOTS, src, 2)
            for c in range(2):
                for b in range(TB):
                    sp.wait_ge(out_copied, TB * c + b + 1)
                    sp.dma_start(out[0, b * P:(b + 1) * P, 512 * c:512 * c + 512], outs[TB * c + b]).then_inc(stored, 16)
            sp.wait_ge(stored, 16 * 2 * TB)

        @block.gpsimd
        def _(pool):
            n = [0]

            def settle(ins):
                n[0] += 1
                ins.then_inc(zeroed, 1)

            settle(pool.memset(ident[:, :], 0.0))
            settle(pool.memset(const_in[:, 0, :], 0.0))
            settle(pool.memset(const_in[:, 1, :], -1.0))
            settle(pool.memset(const_in[:, 3, :], 0.0))
            settle(pool.memset(const_in[:, 4, :], 0.0))
            settle(pool.memset(pick[:, :, :], 0.0))
            pool.memset(const_in[:, 2, :], -1.0).then_inc(consts, 1)
            pool.memset(ones[:, :], 1.0).then_inc(consts, 1)
            pool.memset(eps_col[:, :], EPS).then_inc(consts, 1)
            pool.memset(plain(f4[:, :]), 0.0).then_inc(consts, 1)
            pool.wait_ge(zeroed, n[0])

            def select(m, sign, op, fill, base=0):
                return pool.affine_select(out=m, in_=m, compare_op=op, fill=fill, base=base,
                                          pattern=[[-sign, m.shape[-1]]], channel_multiplier=sign)
            select(ident[:, :], 1, ALU.not_equal, 1.0).then_inc(consts, 1)
            select(const_in[:, 0, :], 1, ALU.not_equal, 1.0).then_inc(consts, 1)
            select(const_in[:, 1, :], 1, ALU.is_ge, 0.0).then_inc(consts, 1)
            select(const_in[:, 3, :], -1, ALU.is_gt, MASKED).then_inc(consts, 1)
            select(const_in[:, 4, :], 1, ALU.is_ge, MASKED).then_inc(consts, 1)
            for i in range(4):
                if i % 2:
                    pool.wait_ge(consts, 9 + i)
                select(pick[:, i // 2, :], 1, ALU.not_equal, 1.0, base=-32 * i).then_inc(consts, 1)
            pool.wait_ge(w_used, U_MIX)
            for p in range(2):
                pool.memset(plain(wf_r[p]), 0.0).then_inc(wf_zero, 1)

        CONSTS = 13

        def w_slot(p, slot, first, size=P):
            return w_r[:, p, slot, first:first + size]

        @block.scalar
        def _(act):
            def split_hi(u, slot, after=None):
                if after is not None:
                    act.wait_ge(w_used, after)
                if isinstance(u, int):
                    act.wait_ge(raw_loaded[slot], 16 * (u // SLOTS + 1))
                else:
                    act.wait_ge(raw_loaded[slot], u)
                act.activation(w_slot(0, slot, 0, 4 * P), w_raw[:, slot, :], ACT.Copy).then_inc(w_hi, 1)

            def ahead(base, i, stride, j):
                slot = (base + j) % SLOTS
                if isinstance(i, int):
                    u = base + stride * i + j
                    if u + SLOTS < UNITS:
                        split_hi(u + SLOTS, u % SLOTS, after=u + 1)
                else:
                    split_hi(16 * ((base + j) // SLOTS + 2) + i * (4 * stride), slot, after=base + j + 1 + stride * i)

            def square(n, m, src, dst=None, also=0):
                at = 8 * n + m if isinstance(m, int) else m + 8 * n
                if not isinstance(at, int) or at >= 2:
                    act.wait_ge(added, at - 1)

            def squares(at, src, rows=slice(0, P), par=0):
                if not isinstance(at, int) or at >= 2:
                    act.wait_ge(added, at - 1)
                act.activation(sq[rows, par, :], src, ACT.Square).then_inc(squared, 1)

            def factor(n, slot, s_bank, count):
                act.wait_ge(summed, n + 1)
                act.activation(rms[:, slot, :], s_bank[:, :], ACT.Ln, bias=eps_col[:, :], scale=1.0 / count).then_inc(ln_done, 1)
                act.wait_ge(ln_done, n + 1)
                act.activation(rms[:, slot, :], rms[:, slot, :], ACT.Exp, scale=-0.5).then_inc(rms_ready, 1)

            def prep(stage, n, gain, used):
                g = GAIN_AT[gain]
                if used:
                    act.wait_ge(w_used, used)
                for k in range(DC):
                    act.wait_ge(x_ready, DC * stage + k + 1)
                    act.activation(xg[:, 0, k, :], xT[:, k, :], ACT.Copy, scale=gains[:, g + k:g + k + 1]).then_inc(xg_hi, 1)
                    squares(8 * n + k, xT[:, k, :], par=k % 2)

            def up(f, pre_bank):
                n = N_FFN1_PRE if f == 0 else N_FFN2_PRE

                def step(s, first=False):
                    for j in range(STEP_UNITS):
                        ahead(U_UP[f], s, STEP_UNITS, j)
                        if first and j == 5:
                            factor(n, 0, pre_bank, D)
                    for a in range(2):
                        at = 2 * s + (2 * STEPS * f + a + 1)
                        act.wait_ge(gate_out, at)
                        act.activation(gu[a], gu[a], ACT.Silu).then_inc(silu_done, 1)
                    for a in range(2):
                        at = 2 * s + (2 * STEPS * f + a + 1)
                        act.wait_ge(h_f, at)
                        act.activation(H[0][:, ds(2 * s + a, 1), :], gu[2 + a].unsqueeze(1), ACT.Copy).then_inc(h_hi_s, 1)
                step(0, first=True)
                with act.Fori(1, STEPS) as s:
                    step(s)

            def down(f):
                n = N_FFN1_POST if f == 0 else N_FFN2_POST
                with act.Fori(0, STEPS - 1) as s:
                    for j in range(4):
                        ahead(U_DOWN[f], s, 4, j)
                for j in range(4):
                    ahead(U_DOWN[f], STEPS - 1, 4, j)
                    if j in (1, 2):
                        for m in range(4 * j - 4, 4 * j):
                            if m % 4 == 3:
                                act.wait_ge(w_used, U_DOWN[f] + DOWN_UNITS - 1 + m // 4)
                            else:
                                act.wait_ge(y_done, 6 * f + m - m // 4 + 1)
                            squares(8 * n + m, bank[(m + 4) % 8][:, :], par=m % 2)
                factor(n, 0, bank[4], D)

            def mixer_start():
                for j in range(TILE_UNITS):
                    ahead(U_MIX, 0, TILE_UNITS, j)
                    if j == 3:
                        act.wait_ge(wf_zero, 2)
                        act.activation(wf_r[0].rearrange("p a (k n) -> p (a k) n", n=P)[:, :, 0:HEADS], wf_raw,
                                       ACT.Copy).then_inc(wf_hi, 1)
                    if j == 8:
                        factor(N_MIX_PRE, 0, bank[7], D)
                act.wait_ge(f4_ready, 1)
                act.wait_ge(b_loaded, 16)
                act.activation(fa, fz, ACT.Abs, bias=b_col[:, :]).then_inc(f_act, 1)
                act.wait_ge(f_act, 1)
                act.activation(fa, fa, ACT.Exp, scale=-1.0).then_inc(f_act, 1)
                act.wait_ge(f_act, 2)
                act.activation(fa, fa, ACT.Ln, bias=1.0).then_inc(f_act, 1)
                act.wait_ge(f_step, 4)
                act.activation(f4[0:HEADS, :], fl, ACT.Copy).then_inc(f_act, 1)
                act.wait_ge(f_act, 4)
                act.activation(f4[64:64 + HEADS, :], plain(f4[0:HEADS, :]), ACT.Copy, scale=-1.0).then_inc(f_act, 1)
                act.wait_ge(f_step, 5)
                act.activation(f4[96:96 + HEADS, :], plain(f4[32:32 + HEADS, :]), ACT.Copy, scale=-1.0).then_inc(f_act, 1)

            def mixer_tile(j, more):
                act.wait_ge(hold_ready, 6 * j + 6)
                act.wait_ge(o_done, 4 * j + 1)
                for i, (name, c) in enumerate((("q_sb", 0), ("k_sb", 1), ("q_fx", 3), ("k_fx", 4))):
                    act.activation(qk[name][0], hold[:, c, :], ACT.Copy).then_inc(qk_hi, 1)
                for i, (name, b) in enumerate((("v_sb", T_BANK), ("v_fx", L_BANKS[0]))):
                    act.wait_ge(v_t, 2 * j + i + 1)
                    act.activation(v_r[name][0], b[:, :], ACT.Copy).then_inc(v_hi, 1)
                for hh in range(2):
                    hd = 2 * j + hh
                    rows = slice(HD * hh, HD * hh + HD)

                    def unit(x):
                        if more:
                            ahead(U_MIX + TILE_UNITS, j, TILE_UNITS, 6 * hh + x)
                    for b in range(3):
                        e = el[:, 512 * b:512 * b + Z_W[b]]
                        act.wait_ge(z_done, 3 * hd + b + 1)
                        act.activation(e, Z[b][:, 0:Z_W[b]], ACT.Abs).then_inc(absz, 1)
                        act.wait_ge(absz, 3 * hd + b + 1)
                        act.activation(e, e, ACT.Exp, scale=-1.0).then_inc(exp_z, 1)
                        act.wait_ge(exp_z, 3 * hd + b + 1)
                        act.activation(e, e, ACT.Ln, bias=1.0).then_inc(lnz, 1)
                    for b in range(3):
                        c = slice(512 * b, 512 * b + Z_W[b])
                        act.wait_ge(sp_full, 3 * hd + b + 1)
                        act.activation(sp_r[0][:, c], spf[:, c], ACT.Copy).then_inc(sp_hi, 1)
                    unit(0)
                    unit(1)
                    act.wait_ge(tri_done, hd + 1)
                    for b in range(3):
                        c = slice(512 * b, 512 * b + Z_W[b])
                        act.activation(el[:, c], Z[b][:, 0:Z_W[b]], ACT.Exp).then_inc(a_exp, 1)
                        act.wait_ge(a_exp, 3 * hd + b + 2)
                        act.activation(sp_r[0][:, c], el[:, c], ACT.Copy).then_inc(a_hi, 1)

                    def softmax_exp(i, b):
                        lb, at, w = L_AT[b]
                        src = L_BANKS[lb % 2][:, at:at + w]
                        first = 512 * lb + at
                        act.wait_ge(neg_max, 4 * hd + (1, 3, 3, 4)[i])
                        act.activation(pr[:, first:first + w], src, ACT.Exp, bias=stat[:, 0, b:b + 1],
                                       accum_out=stat[:, 1, b:b + 1]).then_inc(p_exp, 1)
                    for i, b in enumerate((3, 2, 0)):
                        softmax_exp(i, b)
                    unit(2)
                    unit(3)

                    def out_hi(kind, gain):
                        act.wait_ge(o_done, 2 * hd + kind + 2)
                        g = gains[rows, ds(GAIN_AT[gain] + j, 1)]
                        act.activation(oT[0][rows, ds(j + 4 * kind, 1), :], O_BANK[rows, :].unsqueeze(1), ACT.Copy,
                                       scale=g).then_inc(o_hi, 1)
                        squares(8 * N_SB + 2 * hd + kind, O_BANK[rows, :], rows, kind)
                    out_hi(0, "sb_group_g")
                    softmax_exp(3, 1)
                    unit(4)
                    for b in range(3):
                        c = slice(512 * b, 512 * b + Z_W[b])
                        act.wait_ge(pt_done, 3 * hd + b + 1)
                        act.activation(pt_r[0][:, c], (T_BANK, L_BANKS[1], L_BANKS[0])[b][:, 0:Z_W[b]],
                                       ACT.Copy).then_inc(pt_hi, 1)
                    unit(5)
                    out_hi(1, "fox_group_g")

            act.wait_ge(consts, CONSTS)
            act.activation(const_r[:, :, :], const_in, ACT.Copy).then_inc(const_hi, 1)
            for u in range(SLOTS):
                split_hi(u, u)
            act.wait_ge(gains_ready, 2)
            prep(0, N_FFN1_PRE, "ffn1_pre_g", None)
            up(0, bank[7])
            down(0)
            prep(1, N_MIX_PRE, "mix_pre_g", U_DOWN[0])
            mixer_start()
            act.sem_inc(a_exp, 1)
            act.preload_act_table_set("natural_log_exp_and_others")
            with act.Fori(0, TILES - 1) as j:
                mixer_tile(j, True)
            mixer_tile(TILES - 1, False)

            def out_pair(i):
                for q in range(4):
                    ahead(U_OUT, i, 4, q)
                    if q == 2 and isinstance(i, int) and i == 0:
                        factor(N_SB, 0, bank[6], D // 2)
                        factor(N_FOX, 1, bank[7], D // 2)
                for a in range(2):
                    act.wait_ge(y_out, 2 * i + a + 1)
                    squares(8 * N_MIX_POST + 2 * i + a, y_sb[:, ds(2 * i + a, 1), :].squeeze(1), par=a)
            out_pair(0)
            with act.Fori(1, 4) as i:
                out_pair(i)
            factor(N_MIX_POST, 0, bank[0], D)
            prep(2, N_FFN2_PRE, "ffn2_pre_g", U_OUT)
            up(1, bank[7])
            down(1)
            prep(3, N_PLE_PRE, "ple_pre_g", U_DOWN[1])
            for c in range(2):
                act.wait_ge(p_t, c + 1)
                act.activation(pT_r[0][:, c, :], bank[5 + c][:, :], ACT.Copy).then_inc(p_hi, 1)
            for i in range(4):
                for q in range(5):
                    ahead(U_PLE, i, 5, q)
                    if i == 0 and q == 3:
                        factor(N_PLE_PRE, 0, bank[7], D)
                for a in range(2):
                    act.wait_ge(g_out, 2 * i + a + 1)
                    act.activation(gu[a], gu[a], ACT.Sigmoid).then_inc(sig_done, 1)
                for a in range(2):
                    act.wait_ge(e_out, 2 * i + a + 1)
                    squares(8 * N_PLE_POST + 2 * i + a, y_sb[:, 2 * i + a, :], par=a)
            factor(N_PLE_POST, 0, bank[0], D)

        @block.vector
        def _(dve):
            def split_lo(u):
                pass

            def lo_of(at, slot):
                dve.wait_ge(w_hi, at)
                dve.tensor_tensor(w_slot(1, slot, 0, 4 * P), w_raw[:, slot, :], plain(w_slot(0, slot, 0, 4 * P)),
                                  SUB).then_inc(w_lo, 1)

            def ahead(base, i, stride, j):
                if isinstance(i, int) and base + stride * i + j + SLOTS >= UNITS:
                    return
                slot = (base + j + (stride * i if isinstance(i, int) else 0)) % SLOTS
                lo_of(base + j + SLOTS + 1 + stride * i, slot)

            zeros = [0]

            def zero_acc(n, slot):
                if n:
                    dve.wait_ge(summed, n)
                dve.memset(acc[:, slot, :], 0.0).then_inc(acc_zero, 1)

            def add(n_zero, at, slot=0, rows=slice(0, P), par=0):
                dve.wait_ge(acc_zero, n_zero)
                dve.wait_ge(squared, at + 1)
                if not isinstance(at, int) or at:
                    dve.wait_ge(added, at)
                dve.tensor_tensor(acc[rows, slot, :], acc[rows, slot, :], sq[rows, par, :], ADD).then_inc(added, 1)

            def prep(stage, n, gain):
                g = GAIN_AT[gain]
                for k in range(DC):
                    dve.wait_ge(xg_hi, DC * stage + k + 1)
                    dve.scalar_tensor_tensor(xg[:, 1, k, :], xT[:, k, :], gains[:, g + k:g + k + 1],
                                             plain(xg[:, 0, k, :]), MUL, SUB).then_inc(xg_lo, 1)
                    add(n + 1, 8 * n + k, par=k % 2)

            def into_x(stage, n, gain, source, pre):
                g = GAIN_AT[gain]
                dve.wait_ge(rms_ready, n + 1)
                if pre:
                    pre_n, pre_gain = pre
                    zero_acc(pre_n, 0)
                    pg = GAIN_AT[pre_gain]

                def low(k):
                    dve.wait_ge(xg_hi, DC * stage + k + 1)
                    dve.scalar_tensor_tensor(xg[:, 1, k, :], xT[:, k, :], gains[:, pg + k:pg + k + 1],
                                             plain(xg[:, 0, k, :]), MUL, SUB).then_inc(xg_lo, 1)
                for m in range(DC):
                    tmp = gu[2 + m % 2]
                    at = DC * (stage - 1) + m + 1
                    dve.scalar_tensor_tensor(tmp, source(m), gains[:, g + m:g + m + 1], rms[:, 0, :], MUL, MUL)\
                       .then_inc(y_scaled, 1)
                    dve.wait_ge(y_scaled, at)
                    dve.tensor_tensor(xT[:, m, :], xT[:, m, :], tmp, ADD).then_inc(x_ready, 1)
                    if pre and m:
                        low(m - 1)
                        if m > 1:
                            add(pre_n + 1, 8 * pre_n + m - 2, par=m % 2)
                if pre:
                    low(DC - 1)
                    add(pre_n + 1, 8 * pre_n + DC - 2, par=0)
                    add(pre_n + 1, 8 * pre_n + DC - 1, par=1)

            def up(f):
                n = N_FFN1_PRE if f == 0 else N_FFN2_PRE

                def step(s, st, first=False):
                    for j in range(STEP_UNITS):
                        ahead(U_UP[f], s, STEP_UNITS, j)
                    banks = bank[4 * st:4 * st + 4]
                    if first:
                        dve.wait_ge(rms_ready, n + 1)
                    done = U_UP[f] + STEP_UNITS + STEP_UNITS * s
                    dve.wait_ge(w_used, done)
                    for a in range(2):
                        dve.tensor_tensor(gu[a], banks[a][:, :], rms[:, 0, :], MUL).then_inc(gate_out, 1)
                    for a in range(2):
                        dve.tensor_tensor(gu[2 + a], banks[2 + a][:, :], rms[:, 0, :], MUL).then_inc(up_out, 1)
                    for a in range(2):
                        at = 2 * s + (2 * STEPS * f + a + 1)
                        dve.wait_ge(silu_done, at)
                        dve.wait_ge(up_out, at)
                        dve.tensor_tensor(gu[2 + a], gu[a], gu[2 + a], MUL).then_inc(h_f, 1)
                    for a in range(2):
                        at = 2 * s + (2 * STEPS * f + a + 1)
                        dve.wait_ge(h_hi_s, at)
                        dve.tensor_tensor(H[1][:, ds(2 * s + a, 1), :], gu[2 + a].unsqueeze(1),
                                          plain(H[0][:, ds(2 * s + a, 1), :]), SUB).then_inc(h_lo_s, 1)
                step(0, 0, first=True)
                with dve.Fori(0, STEPS // 2) as s2:
                    step(2 * s2 + 1, 1)
                    step(2 * s2 + 2, 0)

            def down(f):
                n = N_FFN1_POST if f == 0 else N_FFN2_POST
                with dve.Fori(0, STEPS - 1) as s:
                    for j in range(4):
                        ahead(U_DOWN[f], s, 4, j)
                zero_acc(n, 0)
                for j in range(4):
                    ahead(U_DOWN[f], STEPS - 1, 4, j)
                    if j in (1, 2):
                        for m in range(4 * j - 4, 4 * j):
                            add(n + 1, 8 * n + m, par=m % 2)
                            if m == 0:
                                dve.tensor_copy(y0, bank[4][:, :]).then_inc(y0_copied, 1)

            def hold_tile_column(c, src, at):
                scale = HD ** -0.5 if c in (0, 3) else 1.0
                dve.scalar_tensor_tensor(hold[:, c, :], src, scale, rms[:, 0, :], MUL, MUL).then_inc(hold_ready, 1)

            def mixer_start():
                for j in range(TILE_UNITS):
                    ahead(U_MIX, 0, TILE_UNITS, j)
                    if j == 3:
                        dve.wait_ge(wf_hi, 1)
                        cols = [w.rearrange("p a (k n) -> p (a k) n", n=P)[:, :, 0:HEADS] for w in wf_r]
                        dve.tensor_tensor(cols[1], wf_raw, plain(cols[0]), SUB).then_inc(wf_lo, 1)
                dve.memset(scan_ones, 1.0).then_inc(f_step, 1)
                dve.wait_ge(rms_ready, N_MIX_PRE + 1)
                for c in range(6):
                    dve.wait_ge(w_used, U_MIX + 7 + c)
                    hold_tile_column(c, bank[c][:, :], 0)
                dve.wait_ge(f_done, 1)
                dve.tensor_tensor(fz, bank[6][0:HEADS, :], rms[0:HEADS, 0, :], MUL).then_inc(f4_ready, 1)
                dve.wait_ge(f4_ready, 1)
                dve.wait_ge(f_act, 3)
                dve.tensor_scalar(fz, fz, b_col[:, :], 0.0, ADD, MIN).then_inc(f_step, 1)
                dve.wait_ge(f_step, 2)
                dve.tensor_tensor(fz, fz, fa, SUB).then_inc(f_step, 1)
                dve.wait_ge(f_step, 3)
                dve.tensor_tensor_scan(fl, scan_ones, fz, 0.0, MUL, ADD).then_inc(f_step, 1)
                dve.wait_ge(f_act, 4)
                dve.wait_ge(f_step, 4)
                dve.tensor_tensor(f4[32:32 + HEADS, :], fl, plain(f4[0:HEADS, :]), SUB).then_inc(f_step, 1)
                dve.wait_ge(f_act, 6)
                dve.wait_ge(summed, N_SB)
                dve.memset(acc[:, 0, :], 0.0).then_inc(acc_zero, 1)
                dve.memset(acc[:, 1, :], 0.0).then_inc(acc_zero, 1)

            def mixer_tile(j, more):
                for i, (name, c) in enumerate((("q_sb", 0), ("k_sb", 1), ("q_fx", 3), ("k_fx", 4))):
                    dve.wait_ge(qk_hi, 4 * j + i + 1)
                    dve.tensor_tensor(qk[name][1], hold[:, c, :], plain(qk[name][0]), SUB).then_inc(qk_lo, 1)
                for i, (name, b) in enumerate((("v_sb", T_BANK), ("v_fx", L_BANKS[0]))):
                    dve.wait_ge(v_hi, 2 * j + i + 1)
                    dve.tensor_tensor(v_r[name][1], b[:, :], plain(v_r[name][0]), SUB).then_inc(v_lo, 1)
                for hh in range(2):
                    hd = 2 * j + hh
                    rows = slice(HD * hh, HD * hh + HD)

                    def unit(x):
                        if more:
                            ahead(U_MIX + TILE_UNITS, j, TILE_UNITS, 6 * hh + x)

                    def project_out(g):
                        if more:
                            dve.wait_ge(w_used, U_MIX + TILE_UNITS + 6 * hh + 2 * g + 2 + TILE_UNITS * j)
                            hold_tile_column(3 * hh + g, G_BANK[:, :], 0)
                    for b in range(3):
                        c = slice(512 * b, 512 * b + Z_W[b])
                        dve.wait_ge(lnz, 3 * hd + b + 1)
                        dve.scalar_tensor_tensor(spf[:, c], Z[b][:, 0:Z_W[b]], 0.0, el[:, c], MAX, ADD).then_inc(sp_full, 1)
                    for b in range(3):
                        c = slice(512 * b, 512 * b + Z_W[b])
                        dve.wait_ge(sp_hi, 3 * hd + b + 1)
                        dve.tensor_tensor(sp_r[1][:, c], spf[:, c], plain(sp_r[0][:, c]), SUB).then_inc(sp_lo, 1)
                    for i in range(2):
                        dve.tensor_scalar(aug[i], plain(f4[:, :]), pick[:, i, ds(hd, 1)], pick[:, 1 - i, ds(hd, 1)],
                                          MUL, ADD).then_inc(aug_ready, 1)
                    unit(0)
                    unit(1)
                    project_out(0)

                    def softmax_max(b):
                        lb, at, w = L_AT[b]
                        dve.reduce_max(stat[:, 0, b:b + 1], L_BANKS[lb % 2][:, at:at + w], AX, negate=True).then_inc(neg_max, 1)
                    dve.wait_ge(l_done, 3 * hd + 1)
                    softmax_max(3)
                    dve.wait_ge(l_done, 3 * hd + 2)
                    softmax_max(2)
                    softmax_max(0)
                    for b in range(3):
                        c = slice(512 * b, 512 * b + Z_W[b])
                        dve.wait_ge(a_hi, 3 * hd + b + 1)
                        dve.tensor_tensor(sp_r[1][:, c], el[:, c], plain(sp_r[0][:, c]), SUB).then_inc(a_lo, 1)

                    def normalise(i, b):
                        lb, at, w = L_AT[b]
                        c = slice(512 * lb + at, 512 * lb + at + w)
                        dve.wait_ge(p_exp, 4 * hd + i + 1)
                        dve.reciprocal(stat[:, 2, b:b + 1], stat[:, 1, b:b + 1]).then_inc(rcp, 1)
                        dve.wait_ge(rcp, 4 * hd + i + 1)
                        dve.tensor_scalar(pr[:, c], pr[:, c], stat[:, 2, b:b + 1], None, MUL).then_inc(p_scaled, 1)
                    for i, b in enumerate((3, 2, 0)):
                        normalise(i, b)
                    unit(2)
                    unit(3)
                    project_out(1)

                    def out_lo(kind, gain):
                        at = 8 * N_SB + 2 * hd + kind
                        dve.wait_ge(o_hi, 2 * hd + kind + 1)
                        dve.wait_ge(squared, at + 1)
                        dve.scalar_tensor_tensor(oT[1][rows, ds(j + 4 * kind, 1), :].squeeze(1), O_BANK[rows, :],
                                                 gains[rows, ds(GAIN_AT[gain] + j, 1)],
                                                 plain(oT[0][rows, ds(j + 4 * kind, 1), :].squeeze(1)), MUL, SUB).then_inc(o_out, 1)
                        add(N_FOX + 1, at, slot=kind, rows=rows, par=kind)
                    out_lo(0, "sb_group_g")
                    dve.wait_ge(l_done, 3 * hd + 3)
                    softmax_max(1)
                    normalise(3, 1)
                    unit(4)
                    for b in range(3):
                        c = slice(512 * b, 512 * b + Z_W[b])
                        dve.wait_ge(pt_hi, 3 * hd + b + 1)
                        dve.tensor_tensor(pt_r[1][:, c], (T_BANK, L_BANKS[1], L_BANKS[0])[b][:, 0:Z_W[b]],
                                          plain(pt_r[0][:, c]), SUB).then_inc(pt_lo, 1)
                    unit(5)
                    project_out(2)
                    out_lo(1, "fox_group_g")

            dve.wait_ge(gains_t, 1)
            dve.tensor_copy(gains[:, :], bank[0][:, 0:GAIN_ROWS]).then_inc(gains_ready, 1)
            dve.wait_ge(gains_ready, 1)
            post = gains[:, GAIN_AT["ffn1_post_g"]:GAIN_AT["ffn1_post_g"] + DC]
            dve.tensor_scalar(post, post, 0.5, None, MUL)
            post = gains[:, GAIN_AT["ffn2_post_g"]:GAIN_AT["ffn2_post_g"] + DC]
            dve.tensor_scalar(post, post, 0.5, None, MUL).then_inc(gains_ready, 1)
            for u in range(SLOTS):
                lo_of(u + 1, u)
            zero_acc(0, 0)
            for k in range(DC):
                dve.wait_ge(x_t, k + 1)
                dve.tensor_copy(xT[:, k, :], bank[k][:, :]).then_inc(x_ready, 1)
            prep(0, N_FFN1_PRE, "ffn1_pre_g")
            up(0)
            down(0)
            into_x(1, N_FFN1_POST, "ffn1_post_g", lambda m: y0 if m == 0 else bank[(m + 4) % 8][:, :],
                   (N_MIX_PRE, "mix_pre_g"))
            mixer_start()
            dve.sem_inc(o_out, 1)
            with dve.Fori(0, TILES - 1) as j:
                mixer_tile(j, True)
            mixer_tile(TILES - 1, False)
            zero_acc(N_MIX_POST, 0)

            def out_pair(i, st):
                for q in range(4):
                    ahead(U_OUT, i, 4, q)
                if isinstance(i, int) and i == 0:
                    dve.wait_ge(rms_ready, N_FOX + 1)
                dve.wait_ge(w_used, U_OUT + 4 + 4 * i)
                banks = bank[4 * st:4 * st + 4]
                for a in range(2):
                    for half in range(2):
                        dve.tensor_tensor(gu[2 * a + half], banks[2 * half + a][:, :], rms[:, half, :], MUL).then_inc(y_half, 1)
                    dve.wait_ge(y_half, 4 * i + (2 * a + 2))
                    dve.tensor_tensor(y_sb[:, ds(2 * i + a, 1), :].squeeze(1), gu[2 * a], gu[2 * a + 1], ADD).then_inc(y_out, 1)
                for a in range(2):
                    add(N_MIX_POST + 1, 8 * N_MIX_POST + 2 * i + a, par=a)
            out_pair(0, 0)
            with dve.Fori(0, 1) as i:
                out_pair(2 * i + 1, 1)
                out_pair(2 * i + 2, 0)
            out_pair(3, 1)
            into_x(2, N_MIX_POST, "mix_post_g", lambda m: y_sb[:, m, :], (N_FFN2_PRE, "ffn2_pre_g"))
            up(1)
            down(1)
            into_x(3, N_FFN2_POST, "ffn2_post_g", lambda m: y0 if m == 0 else bank[(m + 4) % 8][:, :],
                   (N_PLE_PRE, "ple_pre_g"))
            for c in range(2):
                dve.wait_ge(p_hi, c + 1)
                dve.tensor_tensor(pT_r[1][:, c, :], bank[5 + c][:, :], plain(pT_r[0][:, c, :]), SUB).then_inc(p_lo, 1)
            zero_acc(N_PLE_POST, 0)
            for i in range(4):
                for q in range(5):
                    ahead(U_PLE, i, 5, q)
                banks = bank[4 * (i % 2):4 * (i % 2) + 4]
                if i == 0:
                    dve.wait_ge(rms_ready, N_PLE_PRE + 1)
                dve.wait_ge(w_used, U_PLE + 5 * i + 5)
                for a in range(2):
                    dve.tensor_tensor(gu[a], banks[a][:, :], rms[:, 0, :], MUL).then_inc(g_out, 1)
                for a in range(2):
                    dve.wait_ge(sig_done, 2 * i + a + 1)
                    dve.tensor_tensor(y_sb[:, 2 * i + a, :], banks[2 + a][:, :], gu[a], MUL).then_inc(e_out, 1)
                for a in range(2):
                    add(N_PLE_POST + 1, 8 * N_PLE_POST + 2 * i + a, par=a)
            into_x(4, N_PLE_POST, "ple_post_g", lambda m: y_sb[:, m, :], None)
            for i in range(2 * TB):
                dve.wait_ge(out_t, i + 1)
                dve.tensor_copy(outs[i], bank[i][:, :]).then_inc(out_copied, 1)

        @block.tensor
        def _(pe):
            def product(dst, w_hi_ap, w_lo_ap, m_hi, m_lo, start, stop):
                pe.matmul(dst, w_hi_ap, m_hi, start=start, stop=False, skip_group_check=True)
                pe.matmul(dst, w_lo_ap, m_hi, start=False, stop=False, skip_group_check=True)
                return pe.matmul(dst, w_hi_ap, m_lo, start=False, stop=stop, skip_group_check=True)

            def blocks(dst, slot, col, m_hi, m_lo, start, stop):
                return product(dst, w_slot(0, slot, col), w_slot(1, slot, col), m_hi, m_lo, start, stop)

            def sum_rows(n, s_bank, slot=0):
                pe.wait_ge(added, 8 * n + 8)
                pe.matmul(s_bank[:, :], ones[:, :], acc[:, slot, :], start=True, stop=True).then_inc(summed, 1)

            def up(f, stage):
                n = N_FFN1_PRE if f == 0 else N_FFN2_PRE

                def step(s, st, number):
                    for q in range(4):
                        for kind in range(2):
                            j = 2 * q + kind
                            pe.wait_ge(w_lo, U_UP[f] + j + 1 + STEP_UNITS * s)
                            if number == 1 and j == 0:
                                pe.wait_ge(ln_done, n + 1)
                            if number >= 2 and q == 0:
                                pe.wait_ge(up_out, 2 * STEPS * f + 2 * s - 2)
                            for kk in range(2):
                                k = 2 * q + kk
                                if number == 0:
                                    pe.wait_ge(xg_lo, DC * stage + k + 1)
                                for a in range(2):
                                    last = blocks(bank[4 * st + 2 * kind + a][:, :], j % SLOTS, 256 * kk + P * a,
                                                  xg[:, 0, k, :], xg[:, 1, k, :], k == 0, k == DC - 1)
                            last.then_inc(w_used, 1)
                            if number == 0 and j == 5:
                                sum_rows(n, bank[7])
                step(0, 0, 0)
                step(1, 1, 1)
                with pe.Fori(0, STEPS // 2 - 1) as s2:
                    step(2 * s2 + 2, 0, 2)
                    step(2 * s2 + 3, 1, 2)
                step(STEPS - 1, 0, 2)

            def down(f):
                n = N_FFN1_POST if f == 0 else N_FFN2_POST

                def step(s, first=False, final=False):
                    for j in range(4):
                        c, half = divmod(j, 2)
                        pe.wait_ge(w_lo, U_DOWN[f] + j + 1 + 4 * s)
                        if half == 0:
                            pe.wait_ge(h_lo_s, 2 * STEPS * f + c + 1 + 2 * s)
                        if first and c == 0:
                            pe.wait_ge(up_out, 2 * STEPS * f + 20 + 2 * half)
                        for mm in range(4):
                            m = 4 * half + mm
                            hid = [x[:, ds(2 * s + c, 1), :].squeeze(1) for x in H]
                            last = blocks(bank[(m + 4) % 8][:, :], j, P * mm, hid[0], hid[1],
                                          first and c == 0, final and c == 1)
                            if final and c == 1 and mm < 3:
                                last.then_inc(y_done, 1)
                        last.then_inc(w_used, 1)
                step(0, first=True)
                with pe.Fori(1, STEPS - 1) as s:
                    step(s)
                step(STEPS - 1, final=True)
                pe.wait_ge(y0_copied, f + 1)
                sum_rows(n, bank[4])

            def z_region(c):
                b, at, w = Z_AT[c]
                return b, at, w

            def mixer_start():
                for j in range(TILE_UNITS):
                    kh, c = divmod(j, 6)
                    pe.wait_ge(w_lo, U_MIX + j + 1)
                    for kk in range(4):
                        k = 4 * kh + kk
                        pe.wait_ge(xg_lo, DC + k + 1)
                        last = blocks(bank[c][:, :], j % SLOTS, P * kk, xg[:, 0, k, :], xg[:, 1, k, :], k == 0, k == DC - 1)
                    last.then_inc(w_used, 1)
                    if j == 8:
                        sum_rows(N_MIX_PRE, bank[7])
                pe.wait_ge(wf_lo, 1)
                wf = [w.rearrange("p a (k n) -> p (a k) n", n=P) for w in wf_r]
                for k in range(DC):
                    last = product(bank[6][:, :], wf[0][:, k, :], wf[1][:, k, :], xg[:, 0, k, :], xg[:, 1, k, :],
                                   k == 0, k == DC - 1)
                last.then_inc(f_done, 1)

            def mixer_tile(j, more):
                pe.wait_ge(hold_ready, 6 * j + 6)
                pe.wait_ge(rms_ready, N_MIX_PRE + 1)
                for i, (c, b) in enumerate(((2, T_BANK), (5, L_BANKS[0]))):
                    for s in range(TB):
                        last = pe.transpose(b[:, s * P:(s + 1) * P], hold[:, c, s * P:(s + 1) * P], ident[:, :])
                    last.then_inc(v_t, 1)
                for hh in range(2):
                    hd = 2 * j + hh
                    rows = slice(HD * hh, HD * hh + HD)

                    def project(g, halves=(0, 1)):
                        if not more:
                            return
                        for kh in halves:
                            x = 6 * hh + 2 * g + kh
                            pe.wait_ge(w_lo, U_MIX + TILE_UNITS + x + 1 + TILE_UNITS * j)
                            if kh == 0:
                                pe.wait_ge(hold_ready, 6 + 3 * hh + g + 6 * j)
                            for kk in range(4):
                                k = 4 * kh + kk
                                last = blocks(G_BANK[:, :], x % SLOTS, P * kk, xg[:, 0, k, :], xg[:, 1, k, :],
                                              k == 0, k == DC - 1)
                            last.then_inc(w_used, 1)

                    if hh == 0:
                        pe.wait_ge(qk_lo, 4 * j + 2)
                    pe.wait_ge(a_exp, 3 * hd + 1)
                    kt, qt = qk["k_sb"], qk["q_sb"]
                    for b in range(3):
                        for c in Z_BANKS[b]:
                            _, at, w = Z_AT[c]
                            dst = Z[b][:, at:at + w]
                            product(dst, kt[0][rows, c * P:(c + 1) * P], kt[1][rows, c * P:(c + 1) * P],
                                    qt[0][rows, c * P:SEQ], qt[1][rows, c * P:SEQ], at == 0, False)
                            last = pe.matmul(Z[b][:, at:at + P], ident_r, mask_sb, start=False, stop=True, skip_group_check=True)
                        last.then_inc(z_done, 1)
                    project(0)
                    pe.wait_ge(sp_lo, 3 * hd + 3)
                    for c in range(TB):
                        b, at, w = Z_AT[c]
                        for jc in range(c, TB):
                            jb, jat, jw = Z_AT[jc]
                            off = at + (jc - c) * P
                            lhs = tri_r if jc == c else full_r
                            for part in range(2):
                                last = pe.matmul(Z[b][:, off:off + jw], lhs, sp_r[part][:, 512 * jb + jat:512 * jb + jat + jw],
                                                 start=False, stop=(jc == TB - 1 and part == 1), skip_group_check=True)
                    last.then_inc(tri_done, 1)

                    def logits(b):
                        lb, at, w = L_AT[b]
                        lbank = L_BANKS[lb % 2]
                        dst = lbank[:, at:at + w]
                        qf, kf = qk["q_fx"], qk["k_fx"]
                        product(dst, qf[0][rows, b * P:(b + 1) * P], qf[1][rows, b * P:(b + 1) * P],
                                kf[0][rows, 0:w], kf[1][rows, 0:w], at == 0, False)
                        pe.matmul(dst, aug[0][:, b * P:(b + 1) * P], aug[1][:, 0:w], start=False, stop=False, skip_group_check=True)
                        return pe.matmul(lbank[:, at + b * P:at + (b + 1) * P], ident_r, mask_fx, start=False, stop=True,
                                         skip_group_check=True)
                    if hh == 0:
                        pe.wait_ge(qk_lo, 4 * j + 4)
                        pe.wait_ge(v_lo, 2 * j + 2)
                    pe.wait_ge(aug_ready, 2 * hd + 2)
                    logits(3).then_inc(l_done, 1)
                    logits(2)
                    logits(0).then_inc(l_done, 1)
                    project(1)

                    def weigh(v, a):
                        for c in range(TB):
                            b, at, w = Z_AT[c]
                            first = 512 * b + at
                            last = product(O_BANK[:, c * P:SEQ], v[0][:, c * P:(c + 1) * P], v[1][:, c * P:(c + 1) * P],
                                           a[0][:, first:first + w], a[1][:, first:first + w], c == 0, c == TB - 1)
                        last.then_inc(o_done, 1)
                    pe.wait_ge(a_lo, 3 * hd + 3)
                    pe.wait_ge(o_out, 2 * hd + 1)
                    weigh(v_r["v_sb"], sp_r)
                    pe.wait_ge(p_exp, 4 * hd + 1)
                    logits(1).then_inc(l_done, 1)
                    project(2, (0,))
                    pe.wait_ge(p_scaled, 4 * hd + 4)
                    for b in range(3):
                        tbank = (T_BANK, L_BANKS[1], L_BANKS[0])[b]
                        for c in Z_BANKS[b]:
                            _, at, w = Z_AT[c]
                            for q in range(c, TB):
                                lb, lat, _ = L_AT[q]
                                first = 512 * lb + lat + c * P
                                last = pe.transpose(tbank[:, at + (q - c) * P:at + (q - c + 1) * P],
                                                    pr[:, first:first + P], ident[:, :])
                        last.then_inc(pt_done, 1)
                    project(2, (1,))
                    pe.wait_ge(pt_lo, 3 * hd + 3)
                    pe.wait_ge(o_out, 2 * hd + 2)
                    weigh(v_r["v_fx"], pt_r)

            pe.wait_ge(consts, CONSTS)
            pe.wait_ge(gains_loaded, 16 * len(GAINS))
            pe.transpose(bank[0][:, 0:GAIN_ROWS], gains_in, ident[0:GAIN_ROWS, 0:GAIN_ROWS]).then_inc(gains_t, 1)
            pe.wait_ge(x_loaded, 16)
            for k in (1, 2, 3, 4, 5, 6, 7, 0):
                pass
            for k in range(DC):
                if k == 0:
                    pe.wait_ge(gains_ready, 1)
                for b in range(TB):
                    last = pe.transpose(bank[k][:, b * P:(b + 1) * P], x_in[:, b, k * P:(k + 1) * P], ident[:, :])
                last.then_inc(x_t, 1)
            pe.wait_ge(const_hi, 1)
            pe.wait_ge(x_ready, DC)
            up(0, 0)
            down(0)
            pe.wait_ge(x_ready, 2 * DC)
            mixer_start()
            pe.sem_inc(o_done, 1)
            with pe.Fori(0, TILES - 1) as j:
                mixer_tile(j, True)
            mixer_tile(TILES - 1, False)

            def out_pair(i, st, number):
                for q in range(4):
                    pe.wait_ge(w_lo, U_OUT + q + 1 + 4 * i)
                    if number >= 2 and q == 0:
                        pe.wait_ge(y_out, 2 * i - 2)
                    if number == 1 and q == 0:
                        pe.wait_ge(ln_done, N_FOX + 1)
                    for kk in range(2):
                        k = 2 * q + kk
                        for a in range(2):
                            last = blocks(bank[4 * st + 2 * (q // 2) + a][:, :], q, 256 * kk + P * a,
                                          oT[0][:, k, :], oT[1][:, k, :], k % 4 == 0, k % 4 == 3)
                    last.then_inc(w_used, 1)
                    if number == 0 and q == 2:
                        sum_rows(N_SB + 1 - 0, None) if False else None
                        pe.wait_ge(added, 8 * N_FOX + 8)
                        pe.matmul(bank[6][:, :], ones[:, :], acc[:, 0, :], start=True, stop=True).then_inc(summed, 1)
                        pe.matmul(bank[7][:, :], ones[:, :], acc[:, 1, :], start=True, stop=True).then_inc(summed, 1)
            pe.wait_ge(o_out, 2 * HEADS + 1)
            for i in range(4):
                out_pair(i, i % 2, i)
            sum_rows(N_MIX_POST, bank[0])
            up(1, 2)
            down(1)
            pe.wait_ge(p_loaded, 16)
            pe.wait_ge(x_ready, 3 * DC + DC)
            for c in range(2):
                for b in range(TB):
                    last = pe.transpose(bank[5 + c][:, b * P:(b + 1) * P], p_in[:, b, c * P:(c + 1) * P], ident[:, :])
                last.then_inc(p_t, 1)
            for i in range(4):
                for q in range(5):
                    u = 5 * i + q
                    pe.wait_ge(w_lo, U_PLE + u + 1)
                    if i >= 2 and q == 0:
                        pe.wait_ge(e_out, 2 * i - 2)
                    if i == 1 and q == 0:
                        pe.wait_ge(ln_done, N_PLE_PRE + 1)
                        pe.wait_ge(p_lo, 2)
                    if i == 0 and q == 4:
                        pe.wait_ge(p_lo, 2)
                    for kk in range(2):
                        k = 2 * q + kk if q < 4 else kk
                        if i == 0 and q < 4:
                            pe.wait_ge(xg_lo, 3 * DC + k + 1)
                        for a in range(2):
                            if q < 4:
                                last = blocks(bank[4 * (i % 2) + a][:, :], u % SLOTS, 256 * kk + P * a,
                                              xg[:, 0, k, :], xg[:, 1, k, :], k == 0, k == DC - 1)
                            else:
                                last = blocks(bank[4 * (i % 2) + 2 + a][:, :], u % SLOTS, 256 * kk + P * a,
                                              pT_r[0][:, k, :], pT_r[1][:, k, :], k == 0, k == 1)
                    last.then_inc(w_used, 1)
                    if i == 0 and q == 3:
                        sum_rows(N_PLE_PRE, bank[7])
            sum_rows(N_PLE_POST, bank[0])
            for c in range(2):
                for b in range(TB):
                    if b == 0:
                        pe.wait_ge(x_ready, 4 * DC + 4 * c + 4)
                    for k in range(4 * c, 4 * c + 4):
                        last = pe.transpose(bank[TB * c + b][:, (k % 4) * P:(k % 4 + 1) * P], xT[:, k, b * P:(b + 1) * P],
                                            ident[:, :])
                    last.then_inc(out_t, 1)


NAMES = ["x", "p", "ffn1_pre_g", "ffn1_w_gate", "ffn1_w_up", "ffn1_w_down", "ffn1_post_g", "mix_pre_g", "w_in",
         "b_forget", "sb_group_g", "fox_group_g", "w_out", "mix_post_g", "ffn2_pre_g", "ffn2_w_gate", "ffn2_w_up",
         "ffn2_w_down", "ffn2_post_g", "ple_pre_g", "w_ple_gate", "w_ple_proj", "ple_post_g"]


def kernel(**inputs):
    import numpy as np
    import concourse.bacc as bacc
    from concourse.bass_utils import run_bass_kernel_spmd

    nc = bacc.Bacc("TRN2", target_bir_lowering=False, num_devices=1)
    arrays, tensors = {}, {}
    for name in NAMES:
        arrays[f"in_{name}"] = np.ascontiguousarray(inputs[name])
        tensors[name] = nc.dram_tensor(f"in_{name}", arrays[f"in_{name}"].shape, mybir.dt.float32, kind="ExternalInput").ap()
    out = nc.dram_tensor("out_x", (1, SEQ, D), mybir.dt.float32, kind="ExternalOutput").ap()
    build(nc, tensors, out)
    result = run_bass_kernel_spmd(nc, [arrays], core_ids=[0])
    return result.results[0]["out_x"]
```

```python
import concourse.bass as bass
from concourse import mybir
from contextlib import ExitStack

P = 128
SEQ = 512
D = 1024
DC = D // P
FF = 2816
FC = FF // P
HEADS = 8
HD = 64
TILES = HEADS // 2
D_PLE = 256
TB = SEQ // P
EPS = 1e-6
MASKED = -1e30

GAINS = [("ffn1_pre_g", 8), ("ffn1_post_g", 8), ("mix_pre_g", 8), ("sb_group_g", 4), ("fox_group_g", 4),
         ("mix_post_g", 8), ("ffn2_pre_g", 8), ("ffn2_post_g", 8), ("ple_pre_g", 8), ("ple_post_g", 8)]
GAIN_AT = {}
GAIN_ROWS = 0
for _name, _rows in GAINS:
    GAIN_AT[_name] = GAIN_ROWS
    GAIN_ROWS += _rows

SLOTS = 4
STEP_UNITS = 8
STEPS = FC // 2
UP_UNITS = STEPS * STEP_UNITS
DOWN_UNITS = 2 * FC
TILE_UNITS = 12
OUT_UNITS = 16
EARLY = 6
TAIL_STEPS = 2
BODY_STEPS = STEPS - TAIL_STEPS
TAIL_UNITS = 4 * TAIL_STEPS
PLE_UNITS = 20
U_UP = [0, UP_UNITS + DOWN_UNITS + TILES * TILE_UNITS + OUT_UNITS]
U_DOWN = [u + UP_UNITS for u in U_UP]
U_MIX = U_DOWN[0] + DOWN_UNITS
U_OUT = U_MIX + TILES * TILE_UNITS
UNITS = U_DOWN[1] + DOWN_UNITS
MIX_FIRST = [(0, 0), (0, 1), (1, 0), (1, 1), (0, 2), (1, 2), (2, 0), (2, 1), (2, 2), (3, 0), (3, 1), (3, 2)]
MIX_BANK = [5, 6, 7, 4, 0, 1]

Z_AT = {0: (0, 0, 512), 1: (1, 0, 384), 3: (1, 384, 128), 2: (2, 0, 256)}
Z_BANKS = [[0], [1, 3], [2]]
Z_W = [512, 512, 256]
Z_COLS = sum(Z_W)
L_AT = {3: (0, 0, 512), 2: (1, 0, 384), 0: (1, 384, 128), 1: (2, 0, 256)}

PROJ_BANK = [5, 6, 7, 4] * 2
GATE_BANK = [4, 5, 6, 7] * 2
XT_BANK = [1, 2, 3, 0] * 2

N_FFN1_PRE, N_FFN1_POST, N_MIX_PRE, N_SB, N_FOX, N_MIX_POST, N_FFN2_PRE, N_FFN2_POST, N_PLE_PRE = range(9)


def build(nc, t, out):
    f32, f32r = mybir.dt.float32, mybir.dt.float32r
    ALU, ACT, AX = mybir.AluOpType, mybir.ActivationFunctionType, mybir.AxisListType.X
    MUL, ADD, SUB, MAX, MIN = ALU.mult, ALU.add, ALU.subtract, ALU.max, ALU.min

    def ds(start, size):
        return bass.ds(start, size)

    with ExitStack() as ctx:
        def sb(name, shape, dt=f32):
            return ctx.enter_context(nc.sbuf_tensor(name, shape, dt))

        def sem(name):
            return ctx.enter_context(nc.semaphore(name))

        def plain(ap):
            return ap.bitcast(f32)

        xT = sb("xT", [P, DC, SEQ])
        xg = sb("xg", [P, 2, DC, SEQ], f32r)
        big = sb("big", [P, 2 * FC, SEQ], f32r)
        w_raw = sb("w_raw", [P, SLOTS, 4 * P])
        w_r = sb("w_r", [P, 2, SLOTS, 4 * P], f32r)
        scratch = sb("scratch", [P, 6912])
        acc = sb("acc", [P, 2, SEQ])
        sq = sb("sq", [P, 2, SEQ])
        rms = sb("rms", [P, 2, SEQ])
        gains = sb("gains", [P, GAIN_ROWS])
        ident = sb("ident", [P, P])
        ones = sb("ones", [P, P])
        const_r = sb("const_r", [P, 5, P], f32r)
        f4 = sb("f4", [P, SEQ], f32r)
        pick = sb("pick", [P, 2, HEADS])
        b_col = sb("b_col", [HEADS, 1])
        eps_col = sb("eps_col", [P, 1])
        stat = sb("stat", [P, 4, TB])
        cols = sb("cols", [P, 4, TB])

        ident_r, tri_r, full_r, mask_sb, mask_fx = (const_r[:, i, :] for i in range(5))
        h_hi, h_lo = big[:, 0:FC, :], big[:, FC:2 * FC, :]
        H = [h_hi, h_lo]
        qk = {n: [big[:, 2 * i + p, :] for p in range(2)] for i, n in enumerate(["q_sb", "k_sb", "q_fx", "k_fx"])}
        v_r = {n: [big[:, 8 + 2 * i + p, :] for p in range(2)] for i, n in enumerate(["v_sb", "v_fx"])}
        aug = [big[:, 12 + i, :] for i in range(2)]
        wf_r = [big[:, 14:16, :], big[:, 16:18, :]]
        oT = [big[:, 18:26, :], big[:, 26:34, :]]

        wide = big[:, 34:44, :].rearrange("p r n -> p (r n)").rearrange("p (i n) -> p i n", n=Z_COLS)
        sp_r = [wide[:, i, :] for i in range(2)]
        pt_r = [wide[:, 2 + i, :] for i in range(2)]
        w_ple = [big[:, 0:PLE_UNITS, :], big[:, FC:FC + PLE_UNITS, :]]
        pT_r = [xg[:, i, DC - 2:DC, :] for i in range(2)]
        gu = [scratch[:, i * SEQ:(i + 1) * SEQ] for i in range(4)]
        y_low = scratch[:, 2048:4096].rearrange("p (c n) -> p c n", n=SEQ)
        ple_raw = gu[0:2]
        sig = gu
        g_post = scratch[:, 2048:3072]
        p_in = scratch[:, 5120:6144].rearrange("p (b n) -> p b n", n=D_PLE)
        pT = [scratch[:, 4096 + i * SEQ:4096 + (i + 1) * SEQ] for i in range(2)]
        e_tok = [w_raw[:, i, :] for i in range(TB)] + [scratch[:, 4096 + i * SEQ:4096 + (i + 1) * SEQ] for i in range(TB)]
        y_sb = scratch[:, 2560:6656].rearrange("p (c n) -> p c n", n=SEQ)
        x_in = scratch[:, 2560:6656].rearrange("p (b n) -> p b n", n=D)
        hold = scratch[:, 0:3072].rearrange("p (c n) -> p c n", n=SEQ)
        el = scratch[:, 3072:4352]
        spf = scratch[:, 4352:5632]
        pr = scratch[:, 5632:6912]
        wf_raw = scratch[:, 6656:6720].rearrange("p (k n) -> p k n", n=HEADS)
        gains_in = scratch[0:GAIN_ROWS, 1536:1536 + P]
        const_in = scratch[:, 0:5 * P].rearrange("p (i n) -> p i n", n=P)
        scan_ones = el[0:HEADS, 0:SEQ]
        fz, fa, fl = (spf[0:HEADS, 0:SEQ], spf[0:HEADS, SEQ:2 * SEQ], pr[0:HEADS, 0:SEQ])

        bank = [ctx.enter_context(nc.psum_tensor(f"bank{i}", [P, SEQ], f32)) for i in range(8)]
        Z, O_BANK, G_BANK, L_BANKS, T_BANK = bank[0:3], bank[3], bank[4], [bank[5], bank[6]], bank[7]

        gains_loaded, b_loaded, wf_loaded, p_loaded = map(sem, ("gains_loaded", "b_loaded", "wf_loaded", "p_loaded"))
        x_loaded = [sem(f"x_loaded{i}") for i in range(2)]
        raw_loaded = [sem(f"raw_loaded{i}") for i in range(SLOTS)]
        raw_loaded_2nd = [sem(f"raw_loaded_2nd{i}") for i in range(SLOTS)]
        w_hi, w_lo, w_used = sem("w_hi"), sem("w_lo"), sem("w_used")
        zeroed, consts, const_hi = sem("zeroed"), sem("consts"), sem("const_hi")
        gains_t, gains_ready, x_t = sem("gains_t"), sem("gains_ready"), sem("x_t")
        x_ready, xg_hi, xg_lo = sem("x_ready"), sem("xg_hi"), sem("xg_lo")
        squared, acc_zero, added, summed, ln_done, rms_ready = map(sem, (
            "squared", "acc_zero", "added", "summed", "ln_done", "rms_ready"))
        gate_out, up_out, silu_done, h_f, h_hi_s, h_lo_s = map(sem, (
            "gate_out", "up_out", "silu_done", "h_full", "h_hi", "h_lo"))
        y_done, y_copied, y_scaled = sem("y_done"), sem("y_copied"), sem("y_scaled")
        wf_zero, wf_hi, wf_lo, f_done, f_step, f_act, f4_ready = map(sem, (
            "wf_zero", "wf_hi", "wf_lo", "f_done", "f_step", "f_act", "f4_ready"))
        hold_ready, qk_hi, qk_lo, v_t, v_hi, v_lo = map(sem, (
            "hold_ready", "qk_hi", "qk_lo", "v_t", "v_hi", "v_lo"))
        z_done, absz, exp_z, lnz, sp_full, sp_hi, sp_lo, tri_done, a_exp, a_hi, a_lo = map(sem, (
            "z_done", "absz", "exp_z", "lnz", "sp_full", "sp_hi", "sp_lo", "tri_done", "a_exp", "a_hi", "a_lo"))
        aug_ready, l_done, neg_max, p_exp, rcp, p_scaled, pt_done, pt_hi, pt_lo = map(sem, (
            "aug_ready", "l_done", "neg_max", "p_exp", "rcp", "p_scaled", "pt_done", "pt_hi", "pt_lo"))
        o_done, o_hi, o_out = sem("o_done"), sem("o_hi"), sem("o_out")
        y_half, y_out = sem("y_half"), sem("y_out")
        p_t, p_copied, p_hi, p_lo = sem("p_t"), sem("p_copied"), sem("p_hi"), sem("p_lo")
        ple_loaded = [sem(f"ple_loaded{i}") for i in range(2)]
        ple_hi, ple_lo, g_post_loaded = sem("ple_hi"), sem("ple_lo"), sem("g_post_loaded")
        e_done, e_copied, gate_done, sig_done, e_out, e_squared, eg_out = map(sem, (
            "e_done", "e_copied", "gate_done", "sig_done", "e_out", "e_squared", "eg_out"))
        pre_ln, pre_ready, post_sum, post_ln, post_ready = map(sem, (
            "pre_ln", "pre_ready", "post_sum", "post_ln", "post_ready"))
        xt_done, out_ready = sem("xt_done"), sem("out_ready")
        out_stored = [sem(f"out_stored{i}") for i in range(4)]

        block = ctx.enter_context(nc.Block())

        @block.sync
        def _(sp):
            x_rows = t["x"][0].rearrange("(b p) d -> p b d", p=P)
            for half in range(2):
                c = slice(512 * half, 512 * half + 512)
                sp.dma_start(x_in[:, :, c], x_rows[:, :, c]).then_inc(x_loaded[half], 16)
            w_in = t["w_in"][0].rearrange("(k p) n -> p k n", p=P)
            def load_unit(u, slot, src, k):
                if not isinstance(u, int) or u >= SLOTS:
                    sp.wait_ge(w_lo, u - SLOTS + 1)
                dst = w_raw[:, slot, :].rearrange("p (k n) -> p k n", k=k)
                sp.dma_start(dst, src).then_inc(raw_loaded[slot], 16)

            def load_up(f):
                w = [t[f"ffn{f + 1}_w_{kind}"][0].rearrange("(k p) n -> p k n", p=P) for kind in ("gate", "up")]

                def step(s):
                    for q in range(4):
                        for kind in range(2):
                            j = 2 * q + kind
                            load_unit(U_UP[f] + STEP_UNITS * s + j, j % SLOTS,
                                      w[kind][:, 2 * q:2 * q + 2, ds(s * 256, 256)], 2)
                step(0)
                with sp.Fori(1, STEPS) as s:
                    step(s)

            w_pg = t["w_ple_gate"][0].rearrange("(k p) n -> p k n", p=P)
            w_pp = t["w_ple_proj"][0].rearrange("(k p) n -> p k n", p=P)

            def load_ple(i, slot, src):
                if not isinstance(i, int) or i >= 2:
                    sp.wait_ge(ple_lo, i - 1)
                sp.dma_start(ple_raw[slot].unsqueeze(1), src).then_inc(ple_loaded[slot], 16)

            def load_gates(step):
                for i in range(2):
                    load_ple(2 * step + i, i, w_pg[:, ds(step - 2, 1), 512 * i:512 * i + 512])

            def load_down(f):
                w = t[f"ffn{f + 1}_w_down"][0].rearrange("(k p) n -> p k n", p=P)

                def step(s):
                    for j in range(4):
                        load_unit(U_DOWN[f] + 4 * s + j, j,
                                  w[:, ds(2 * s + j // 2, 1), 512 * (j % 2):512 * (j % 2) + 512], 1)
                if f == 0:
                    with sp.Fori(0, BODY_STEPS) as s:
                        step(s)
                else:
                    step(0)
                    sp.wait_ge(h_lo_s, 4 * STEPS)
                    for s in range(1, 3):
                        for i in range(2):
                            load_ple(2 * s - 2 + i, i, w_pp[:, i:i + 1, 512 * (s - 1):512 * s])
                        step(s)
                    with sp.Fori(3, BODY_STEPS) as s:
                        load_gates(s - 1)
                        step(s)
                    load_gates(BODY_STEPS - 1)
                for j in range(TAIL_UNITS):
                    half, c = divmod(j, 2 * TAIL_STEPS)
                    u = U_DOWN[f] + 4 * BODY_STEPS + j
                    load_unit(u, u % SLOTS, w[:, 2 * BODY_STEPS + c:2 * BODY_STEPS + c + 1, 512 * half:512 * half + 512], 1)

            load_up(0)
            sp.dma_start(b_col[:, :], t["b_forget"][0].rearrange("(h o) -> h o", o=1)).then_inc(b_loaded, 16)
            sp.dma_start(wf_raw, w_in[:, :, 6 * 512:6 * 512 + HEADS]).then_inc(wf_loaded, 16)
            load_down(0)
            w_six = w_in[:, :, 0:6 * 512].rearrange("p k (c n) -> p k c n", n=512)
            for j, (kp, cp) in enumerate(MIX_FIRST):
                u = U_MIX + j
                sp.wait_ge(w_lo, u - SLOTS + 1)
                for k, loaded in enumerate((raw_loaded, raw_loaded_2nd)):
                    sp.dma_start(w_raw[:, u % SLOTS, 256 * k:256 * k + 256].rearrange("p (c n) -> p c n", c=2),
                                 w_six[:, 2 * kp + k, 2 * cp:2 * cp + 2, 0:P]).then_inc(loaded[u % SLOTS], 16)
            with sp.Fori(1, TILES) as tile:
                for j in range(TILE_UNITS):
                    c, kh = divmod(j, 2)
                    load_unit(U_MIX + TILE_UNITS * tile + j, j % SLOTS,
                              w_in[:, 4 * kh:4 * kh + 4, ds(512 * c + tile * P, P)], 4)
            w_out = t["w_out"][0].rearrange("(k p) n -> p k n", p=P)
            with sp.Fori(0, 4) as i:
                for q in range(4):
                    load_unit(U_OUT + 4 * i + q, q, w_out[:, 2 * q:2 * q + 2, ds(256 * i, 256)], 2)
            load_up(1)
            sp.wait_ge(x_ready, 3 * DC)
            sp.dma_start(p_in, t["p"][0, 0].rearrange("(b p) d -> p b d", p=P)).then_inc(p_loaded, 16)
            load_down(1)
            load_gates(BODY_STEPS)
            sp.wait_ge(x_ready, 4 * DC)
            sp.dma_start(g_post, t["ple_post_g"][0].partition_broadcast(P)).then_inc(g_post_loaded, 16)
            for r in range(2 * TB):
                b, half = divmod(r, 2)
                sp.wait_ge(out_ready, r + 1)
                sp.dma_start(out[0, b * P:(b + 1) * P, 512 * half:512 * half + 512], sig[r % 4]).then_inc(out_stored[r % 4], 16)
            for i in range(4):
                sp.wait_ge(out_stored[i], 32)

        @block.gpsimd
        def _(pool):
            n = [0]

            def settle(ins):
                n[0] += 1
                ins.then_inc(zeroed, 1)

            settle(pool.memset(ident[:, :], 0.0))
            settle(pool.memset(const_in[:, 0, :], 0.0))
            settle(pool.memset(const_in[:, 1, :], -1.0))
            settle(pool.memset(const_in[:, 3, :], 0.0))
            settle(pool.memset(const_in[:, 4, :], 0.0))
            settle(pool.memset(pick[:, :, :], 0.0))
            pool.memset(const_in[:, 2, :], -1.0).then_inc(consts, 1)
            pool.memset(ones[:, :], 1.0).then_inc(consts, 1)
            pool.memset(eps_col[:, :], EPS).then_inc(consts, 1)
            pool.memset(plain(f4[:, :]), 0.0).then_inc(consts, 1)
            pool.wait_ge(zeroed, n[0])

            def select(m, sign, op, fill, base=0):
                return pool.affine_select(out=m, in_=m, compare_op=op, fill=fill, base=base,
                                          pattern=[[-sign, m.shape[-1]]], channel_multiplier=sign)
            select(ident[:, :], 1, ALU.not_equal, 1.0).then_inc(consts, 1)
            select(const_in[:, 0, :], 1, ALU.not_equal, 1.0).then_inc(consts, 1)
            select(const_in[:, 1, :], 1, ALU.is_ge, 0.0).then_inc(consts, 1)
            select(const_in[:, 3, :], -1, ALU.is_gt, MASKED).then_inc(consts, 1)
            select(const_in[:, 4, :], 1, ALU.is_ge, MASKED).then_inc(consts, 1)
            for i in range(4):
                if i % 2:
                    pool.wait_ge(consts, 9 + i)
                select(pick[:, i // 2, :], 1, ALU.not_equal, 1.0, base=-32 * i).then_inc(consts, 1)

            def add_squares(n):
                if n:
                    pool.wait_ge(summed, n)
                pool.memset(acc[:, 0, :], 0.0).then_inc(acc_zero, 1)
                pool.wait_ge(acc_zero, n + 1)
                for k in range(DC):
                    at = 8 * n + k
                    pool.wait_ge(squared, at + 1)
                    if at:
                        pool.wait_ge(added, at)
                    pool.tensor_tensor(acc[:, 0, :], acc[:, 0, :], sq[:, k % 2, :], ADD).then_inc(added, 1)
            add_squares(N_FFN1_PRE)
            pool.wait_ge(w_used, U_MIX)
            for p in range(2):
                pool.memset(plain(wf_r[p]), 0.0).then_inc(wf_zero, 1)
            for n in (N_MIX_PRE, N_FFN2_PRE, N_PLE_PRE):
                add_squares(n)

        CONSTS = 13

        def w_slot(p, slot, first, size=P):
            return w_r[:, p, slot, first:first + size]

        @block.scalar
        def _(act):
            def split_hi(u, slot, after=None):
                if after is not None:
                    act.wait_ge(w_used, after)
                if isinstance(u, int):
                    act.wait_ge(raw_loaded[slot], 16 * (u // SLOTS + 1))
                    if U_MIX <= u < U_MIX + TILE_UNITS:
                        act.wait_ge(raw_loaded_2nd[slot], 16 * ((u - U_MIX) // SLOTS + 1))
                else:
                    act.wait_ge(raw_loaded[slot], u)
                act.activation(w_slot(0, slot, 0, 4 * P), w_raw[:, slot, :], ACT.Copy).then_inc(w_hi, 1)

            def ahead(base, i, stride, j):
                slot = (base + j) % SLOTS
                if isinstance(i, int):
                    u = base + stride * i + j
                    if u + SLOTS < UNITS:
                        split_hi(u + SLOTS, u % SLOTS, after=u + 1)
                else:
                    split_hi(16 * ((base + j) // SLOTS + 2) + i * (4 * stride), slot, after=base + j + 1 + stride * i)

            def squares(at, src, rows=slice(0, P), par=0):
                if not isinstance(at, int) or at >= 2:
                    act.wait_ge(added, at - 1)
                act.activation(sq[rows, par, :], src, ACT.Square).then_inc(squared, 1)

            def factor(n, slot, s_bank, count):
                act.wait_ge(summed, n + 1)
                act.activation(rms[:, slot, :], s_bank[:, :], ACT.Ln, bias=eps_col[:, :], scale=1.0 / count).then_inc(ln_done, 1)
                act.wait_ge(ln_done, n + 1)
                act.activation(rms[:, slot, :], rms[:, slot, :], ACT.Exp, scale=-0.5).then_inc(rms_ready, 1)

            def prep(stage, n, gain, used, between=None):
                g = GAIN_AT[gain]
                if used:
                    act.wait_ge(w_used, used)
                for k in range(DC):
                    act.wait_ge(x_ready, DC * stage + k + 1)
                    act.activation(xg[:, 0, k, :], xT[:, k, :], ACT.Copy, scale=gains[:, g + k:g + k + 1]).then_inc(xg_hi, 1)
                    squares(8 * n + k, xT[:, k, :], par=k % 2)
                    if between:
                        between(k)

            def up(f, pre_bank):
                n = N_FFN1_PRE if f == 0 else N_FFN2_PRE

                def step(s, first=False, p_copy=False):
                    for j in range(EARLY if first else 0, STEP_UNITS):
                        ahead(U_UP[f], s, STEP_UNITS, j)
                        if p_copy and j == 5:
                            for c in range(2):
                                act.wait_ge(p_t, c + 1)
                                act.activation(pT[c], bank[6 + c][:, :], ACT.Copy).then_inc(p_copied, 1)
                        if first and j == 6:
                            factor(n, 0, pre_bank, D)
                    for a in range(2):
                        at = 2 * s + (2 * STEPS * f + a + 1)
                        act.wait_ge(gate_out, at)
                        act.activation(gu[a], gu[a], ACT.Silu).then_inc(silu_done, 1)
                    for a in range(2):
                        at = 2 * s + (2 * STEPS * f + a + 1)
                        act.wait_ge(h_f, at)
                        act.activation(H[0][:, ds(2 * s + a, 1), :], gu[2 + a].unsqueeze(1), ACT.Copy).then_inc(h_hi_s, 1)
                step(0, first=True)
                with act.Fori(1, STEPS - 1) as s:
                    step(s)
                step(STEPS - 1, p_copy=f == 1)

            def split_ple(i, slot, used):
                act.wait_ge(w_used, used)
                act.wait_ge(ple_loaded[slot], 8 * (i - slot) + 16)
                act.activation(w_ple[0][:, ds(i, 1), :], ple_raw[slot].unsqueeze(1), ACT.Copy).then_inc(ple_hi, 1)

            def down(f):
                n = N_FFN1_POST if f == 0 else N_FFN2_POST
                base = U_DOWN[f] + 4 * BODY_STEPS
                act.preload_act_table_set("natural_log_exp_and_others")

                def step(s):
                    if f == 1:
                        for i in range(2):
                            split_ple(2 * s - 2 + i, i, U_DOWN[f] + 4 * s)
                    for j in range(4):
                        ahead(U_DOWN[f], s, 4, j)
                for j in range(4):
                    ahead(U_DOWN[f], 0, 4, j)
                if f == 1:
                    act.wait_ge(p_copied, 2)
                    act.wait_ge(w_used, U_DOWN[1])
                    for c in range(2):
                        act.activation(pT_r[0][:, c, :], pT[c], ACT.Copy).then_inc(p_hi, 1)
                with act.Fori(1, BODY_STEPS) as s:
                    step(s)
                if f == 1:
                    for i in range(2):
                        split_ple(2 * BODY_STEPS - 2 + i, i, base)
                for j in range(4):
                    ahead(base, 0, 4, j)
                for m in range(4):
                    if m == 3:
                        act.wait_ge(w_used, base + 4)
                    else:
                        act.wait_ge(y_done, 6 * f + m + 1)
                    squares(8 * n + m, bank[m + 4][:, :], par=m % 2)
                for j in range(4, 7):
                    ahead(base, 0, 4, j)
                if f == 1:
                    for i in range(2):
                        split_ple(PLE_UNITS - 2 + i, i, base + 6)
                for m in range(4, 8):
                    if m == 7:
                        act.wait_ge(w_used, base + 8)
                    else:
                        act.wait_ge(y_done, 6 * f + m)
                    squares(8 * n + m, bank[m - 4][:, :], par=m % 2)
                ahead(base, 0, 4, 7)
                factor(n, 0, bank[4], D)

            def qk_split(tile, kind):
                act.wait_ge(hold_ready, 6 * tile + 3 * kind + 2)
                for name, c in ((("q_sb", 0), ("k_sb", 1)), (("q_fx", 3), ("k_fx", 4)))[kind]:
                    act.activation(qk[name][0], hold[:, c, :], ACT.Copy).then_inc(qk_hi, 1)

            def v_split(tile, kind):
                act.wait_ge(v_t, 2 * tile + kind + 1)
                act.activation(v_r[("v_sb", "v_fx")[kind]][0], (T_BANK, O_BANK)[kind][:, :], ACT.Copy).then_inc(v_hi, 1)

            def mixer_start():
                for j in range(EARLY, 9):
                    ahead(U_MIX, 0, TILE_UNITS, j)
                    if j == EARLY:
                        act.wait_ge(wf_zero, 2)
                        act.wait_ge(wf_loaded, 16)
                        act.activation(wf_r[0].rearrange("p a (k n) -> p (a k) n", n=P)[:, :, 0:HEADS], wf_raw,
                                       ACT.Copy).then_inc(wf_hi, 1)
                factor(N_MIX_PRE, 0, bank[2], D)
                act.wait_ge(f4_ready, 1)
                act.wait_ge(b_loaded, 16)
                act.activation(fa, fz, ACT.Abs, bias=b_col[:, :]).then_inc(f_act, 1)
                act.wait_ge(f_act, 1)
                act.activation(fa, fa, ACT.Exp, scale=-1.0).then_inc(f_act, 1)
                act.wait_ge(f_act, 2)
                act.activation(fa, fa, ACT.Ln, bias=1.0).then_inc(f_act, 1)
                act.wait_ge(f_step, 4)
                act.activation(f4[0:HEADS, :], fl, ACT.Copy).then_inc(f_act, 1)
                act.wait_ge(f_act, 4)
                act.activation(f4[64:64 + HEADS, :], plain(f4[0:HEADS, :]), ACT.Copy, scale=-1.0).then_inc(f_act, 1)
                act.wait_ge(f_step, 5)
                act.activation(f4[96:96 + HEADS, :], plain(f4[32:32 + HEADS, :]), ACT.Copy, scale=-1.0).then_inc(f_act, 1)
                ahead(U_MIX, 0, TILE_UNITS, 9)
                qk_split(0, 0)
                ahead(U_MIX, 0, TILE_UNITS, 10)
                ahead(U_MIX, 0, TILE_UNITS, 11)
                v_split(0, 0)
                qk_split(0, 1)

            def mixer_tile(j, more):
                for hh in range(2):
                    hd = 2 * j + hh
                    rows = slice(HD * hh, HD * hh + HD)

                    def unit(x):
                        if more:
                            ahead(U_MIX + TILE_UNITS, j, TILE_UNITS, 6 * hh + x)
                    for b in range(3):
                        e = el[:, 512 * b:512 * b + Z_W[b]]
                        act.wait_ge(z_done, 3 * hd + b + 1)
                        act.activation(e, Z[b][:, 0:Z_W[b]], ACT.Abs).then_inc(absz, 1)
                        act.wait_ge(absz, 3 * hd + b + 1)
                        act.activation(e, e, ACT.Exp, scale=-1.0).then_inc(exp_z, 1)
                        act.wait_ge(exp_z, 3 * hd + b + 1)
                        act.activation(e, e, ACT.Ln, bias=1.0).then_inc(lnz, 1)
                    for b in range(3):
                        c = slice(512 * b, 512 * b + Z_W[b])
                        act.wait_ge(sp_full, 3 * hd + b + 1)
                        act.activation(sp_r[0][:, c], spf[:, c], ACT.Copy).then_inc(sp_hi, 1)
                    if hh == 0:
                        v_split(j, 1)

                    def softmax_exp(i, b):
                        lb, at, w = L_AT[b]
                        src = L_BANKS[lb % 2][:, at:at + w]
                        first = 512 * lb + at
                        act.wait_ge(neg_max, 4 * hd + (1, 3, 3, 4)[i])
                        act.activation(pr[:, first:first + w], src, ACT.Exp, bias=stat[:, 0, b:b + 1],
                                       accum_out=stat[:, 1, b:b + 1]).then_inc(p_exp, 1)
                    for i, b in enumerate((3, 2, 0)):
                        softmax_exp(i, b)
                    unit(0)
                    unit(1)
                    act.wait_ge(tri_done, hd + 1)
                    for b in range(3):
                        c = slice(512 * b, 512 * b + Z_W[b])
                        act.activation(el[:, c], Z[b][:, 0:Z_W[b]], ACT.Exp).then_inc(a_exp, 1)
                        act.wait_ge(a_exp, 3 * hd + b + 2)
                        act.activation(sp_r[0][:, c], el[:, c], ACT.Copy).then_inc(a_hi, 1)
                    softmax_exp(3, 1)
                    unit(2)
                    unit(3)
                    if hh == 1 and more:
                        qk_split(j + 1, 0)
                        qk_split(j + 1, 1)

                    def out_hi(kind, gain):
                        act.wait_ge(o_done, 2 * hd + kind + 2)
                        g = gains[rows, ds(GAIN_AT[gain] + j, 1)]
                        act.activation(oT[0][rows, ds(j + 4 * kind, 1), :], O_BANK[rows, :].unsqueeze(1), ACT.Copy,
                                       scale=g).then_inc(o_hi, 1)
                        squares(8 * N_SB + 2 * hd + kind, O_BANK[rows, :], rows, kind)
                    out_hi(0, "sb_group_g")
                    for b in range(3):
                        c = slice(512 * b, 512 * b + Z_W[b])
                        act.wait_ge(pt_done, 3 * hd + b + 1)
                        act.activation(pt_r[0][:, c], (T_BANK, L_BANKS[1], L_BANKS[0])[b][:, 0:Z_W[b]],
                                       ACT.Copy).then_inc(pt_hi, 1)
                    unit(4)
                    if hh == 1 and more:
                        v_split(j + 1, 0)
                    unit(5)
                    out_hi(1, "fox_group_g")

            for name, n in GAINS:
                act.dma_start(gains_in[GAIN_AT[name]:GAIN_AT[name] + n, :],
                              t[name][0].rearrange("(c p) -> c p", p=P)).then_inc(gains_loaded, 16)
            act.wait_ge(consts, CONSTS)
            act.activation(const_r[:, :, :], const_in, ACT.Copy).then_inc(const_hi, 1)
            for u in range(SLOTS):
                split_hi(u, u)
            act.wait_ge(gains_ready, 2)

            def early(base, stride):
                def between(k):
                    if k >= 2:
                        ahead(base, 0, stride, k - 2)
                return between
            prep(0, N_FFN1_PRE, "ffn1_pre_g", None, early(U_UP[0], STEP_UNITS))
            up(0, bank[7])
            down(0)
            prep(1, N_MIX_PRE, "mix_pre_g", U_DOWN[0], early(U_MIX, TILE_UNITS))
            mixer_start()
            act.sem_inc(a_exp, 1)
            act.preload_act_table_set("natural_log_exp_and_others")
            with act.Fori(0, TILES - 1) as j:
                mixer_tile(j, True)
            mixer_tile(TILES - 1, False)

            def out_pair(i):
                for q in range(4):
                    ahead(U_OUT, i, 4, q)
                    if q == 2 and isinstance(i, int) and i == 0:
                        factor(N_SB, 0, bank[6], D // 2)
                        factor(N_FOX, 1, bank[7], D // 2)
                for a in range(2):
                    act.wait_ge(y_out, 2 * i + a + 1)
                    squares(8 * N_MIX_POST + 2 * i + a, y_sb[:, ds(2 * i + a, 1), :].squeeze(1), par=a)
            out_pair(0)
            with act.Fori(1, 4) as i:
                out_pair(i)
            factor(N_MIX_POST, 0, bank[0], D)
            prep(2, N_FFN2_PRE, "ffn2_pre_g", U_OUT, early(U_UP[1], STEP_UNITS))
            up(1, bank[7])
            down(1)

            def e_copy(r):
                act.wait_ge(e_done, r + 1)
                half, b = divmod(r, TB)
                act.activation(e_tok[TB * half + b], bank[PROJ_BANK[r]][:, :], ACT.Copy).then_inc(e_copied, 1)

            def e_copies(k):
                for r in (2 * k + 1, 2 * k + 2):
                    if r < 2 * TB:
                        e_copy(r)
                if k == 5:
                    act.wait_ge(e_done, 2 * TB)
            act.wait_ge(w_lo, UNITS)
            e_copy(0)
            prep(3, N_PLE_PRE, "ple_pre_g", None, e_copies)
            act.wait_ge(summed, N_PLE_PRE + 1)
            act.activation(cols[:, 0, :], bank[0][:, 0:TB], ACT.Ln, bias=eps_col[:, :], scale=1.0 / D).then_inc(pre_ln, 1)
            act.wait_ge(pre_ln, 1)
            act.activation(cols[:, 0, :], cols[:, 0, :], ACT.Exp, scale=-0.5).then_inc(pre_ready, 1)
            act.wait_ge(pre_ready, 1)
            act.wait_ge(x_ready, 4 * DC)
            act.wait_ge(ple_lo, PLE_UNITS)
            act.wait_ge(added, 8 * N_PLE_PRE + 8)
            for b in range(TB):
                for half in range(2):
                    r = 2 * b + half
                    act.wait_ge(gate_done, r + 1)
                    if r >= 4:
                        act.wait_ge(out_stored[r % 4], 16)
                    act.activation(sig[r % 4], bank[GATE_BANK[r]][:, :], ACT.Sigmoid, scale=cols[:, 0, b:b + 1]).then_inc(sig_done, 1)
                for half in range(2):
                    r = 2 * b + half
                    act.wait_ge(e_out, r + 1)
                    if r >= 2:
                        act.wait_ge(e_squared, r - 1)
                    act.activation(sq[:, half, :], e_tok[TB * half + b], ACT.Square,
                                   accum_out=cols[:, 1 + half, b:b + 1]).then_inc(e_squared, 1)
                act.wait_ge(post_sum, b + 1)
                act.activation(cols[:, 3, b:b + 1], cols[:, 3, b:b + 1], ACT.Ln, bias=eps_col[:, :], scale=1.0 / D).then_inc(post_ln, 1)
                act.wait_ge(post_ln, b + 1)
                act.activation(cols[:, 3, b:b + 1], cols[:, 3, b:b + 1], ACT.Exp, scale=-0.5).then_inc(post_ready, 1)

        @block.vector
        def _(dve):
            def lo_of(at, slot):
                dve.wait_ge(w_hi, at)
                dve.tensor_tensor(w_slot(1, slot, 0, 4 * P), w_raw[:, slot, :], plain(w_slot(0, slot, 0, 4 * P)),
                                  SUB).then_inc(w_lo, 1)

            def ahead(base, i, stride, j):
                if isinstance(i, int) and base + stride * i + j + SLOTS >= UNITS:
                    return
                slot = (base + j + (stride * i if isinstance(i, int) else 0)) % SLOTS
                lo_of(base + j + SLOTS + 1 + stride * i, slot)

            def zero_acc(n, slot):
                if n:
                    dve.wait_ge(summed, n)
                dve.memset(acc[:, slot, :], 0.0).then_inc(acc_zero, 1)

            def add(n_zero, at, slot=0, rows=slice(0, P), par=0):
                dve.wait_ge(acc_zero, n_zero)
                dve.wait_ge(squared, at + 1)
                if not isinstance(at, int) or at:
                    dve.wait_ge(added, at)
                dve.tensor_tensor(acc[rows, slot, :], acc[rows, slot, :], sq[rows, par, :], ADD).then_inc(added, 1)

            def low(stage, k, gain):
                g = GAIN_AT[gain]
                dve.wait_ge(xg_hi, DC * stage + k + 1)
                dve.scalar_tensor_tensor(xg[:, 1, k, :], xT[:, k, :], gains[:, g + k:g + k + 1],
                                         plain(xg[:, 0, k, :]), MUL, SUB).then_inc(xg_lo, 1)

            def into_x(stage, n, gain, source, pre_gain, between=None):
                g = GAIN_AT[gain]
                dve.wait_ge(rms_ready, n + 1)

                def after(k):
                    low(stage, k, pre_gain)
                    if between:
                        between(k)
                for m in range(DC):
                    tmp = gu[2 + m % 2]
                    at = DC * (stage - 1) + m + 1
                    dve.scalar_tensor_tensor(tmp, source(m), gains[:, g + m:g + m + 1], rms[:, 0, :], MUL, MUL)\
                       .then_inc(y_scaled, 1)
                    dve.wait_ge(y_scaled, at)
                    dve.tensor_tensor(xT[:, m, :], xT[:, m, :], tmp, ADD).then_inc(x_ready, 1)
                    if m:
                        after(m - 1)
                after(DC - 1)

            def early(base, stride):
                def between(k):
                    if k >= 2:
                        ahead(base, 0, stride, k - 2)
                return between

            def up(f):
                n = N_FFN1_PRE if f == 0 else N_FFN2_PRE

                def step(s, st, first=False):
                    for j in range(EARLY if first else 0, STEP_UNITS):
                        ahead(U_UP[f], s, STEP_UNITS, j)
                    banks = bank[4 * st:4 * st + 4]
                    if first:
                        dve.wait_ge(rms_ready, n + 1)
                    done = U_UP[f] + STEP_UNITS + STEP_UNITS * s
                    dve.wait_ge(w_used, done)
                    for a in range(2):
                        dve.tensor_tensor(gu[a], banks[a][:, :], rms[:, 0, :], MUL).then_inc(gate_out, 1)
                    for a in range(2):
                        dve.tensor_tensor(gu[2 + a], banks[2 + a][:, :], rms[:, 0, :], MUL).then_inc(up_out, 1)
                    for a in range(2):
                        at = 2 * s + (2 * STEPS * f + a + 1)
                        dve.wait_ge(silu_done, at)
                        dve.wait_ge(up_out, at)
                        dve.tensor_tensor(gu[2 + a], gu[a], gu[2 + a], MUL).then_inc(h_f, 1)
                    for a in range(2):
                        at = 2 * s + (2 * STEPS * f + a + 1)
                        dve.wait_ge(h_hi_s, at)
                        dve.tensor_tensor(H[1][:, ds(2 * s + a, 1), :], gu[2 + a].unsqueeze(1),
                                          plain(H[0][:, ds(2 * s + a, 1), :]), SUB).then_inc(h_lo_s, 1)
                step(0, 0, first=True)
                with dve.Fori(0, STEPS // 2) as s2:
                    step(2 * s2 + 1, 1)
                    step(2 * s2 + 2, 0)

            def ple_lo_row(i, slot):
                dve.wait_ge(ple_hi, i + 1)
                dve.tensor_tensor(w_ple[1][:, ds(i, 1), :], ple_raw[slot].unsqueeze(1), plain(w_ple[0][:, ds(i, 1), :]),
                                  SUB).then_inc(ple_lo, 1)

            def down(f):
                n = N_FFN1_POST if f == 0 else N_FFN2_POST
                base = U_DOWN[f] + 4 * BODY_STEPS
                for j in range(4):
                    ahead(U_DOWN[f], 0, 4, j)
                if f == 1:
                    for c in range(2):
                        dve.wait_ge(p_hi, c + 1)
                        dve.tensor_tensor(pT_r[1][:, c, :], pT[c], plain(pT_r[0][:, c, :]), SUB).then_inc(p_lo, 1)
                with dve.Fori(1, BODY_STEPS) as s:
                    if f == 1:
                        for i in range(2):
                            ple_lo_row(2 * s - 2 + i, i)
                    for j in range(4):
                        ahead(U_DOWN[f], s, 4, j)
                zero_acc(n, 0)
                if f == 1:
                    for i in range(2):
                        ple_lo_row(2 * BODY_STEPS - 2 + i, i)
                for j in range(4):
                    ahead(base, 0, 4, j)
                for m in range(4):
                    add(n + 1, 8 * n + m, par=m % 2)
                    dve.tensor_copy(y_low[:, m, :], bank[m + 4][:, :]).then_inc(y_copied, 1)
                for j in range(4, 7):
                    ahead(base, 0, 4, j)
                if f == 1:
                    for i in range(2):
                        ple_lo_row(PLE_UNITS - 2 + i, i)
                for m in range(4, 8):
                    add(n + 1, 8 * n + m, par=m % 2)
                ahead(base, 0, 4, 7)

            def hold_tile_column(c, src, at):
                scale = HD ** -0.5 if c in (0, 3) else 1.0
                dve.scalar_tensor_tensor(hold[:, c, :], src, scale, rms[:, 0, :], MUL, MUL).then_inc(hold_ready, 1)

            def qk_split(tile, kind):
                for i, (name, c) in enumerate(((("q_sb", 0), ("k_sb", 1)), (("q_fx", 3), ("k_fx", 4)))[kind]):
                    dve.wait_ge(qk_hi, 4 * tile + (2 * kind + i + 1))
                    dve.tensor_tensor(qk[name][1], hold[:, c, :], plain(qk[name][0]), SUB).then_inc(qk_lo, 1)

            def v_split(tile, kind):
                name = ("v_sb", "v_fx")[kind]
                dve.wait_ge(v_hi, 2 * tile + kind + 1)
                dve.tensor_tensor(v_r[name][1], (T_BANK, O_BANK)[kind][:, :], plain(v_r[name][0]), SUB).then_inc(v_lo, 1)

            def aug_rows(hd):
                for i in range(2):
                    dve.tensor_scalar(aug[i], plain(f4[:, :]), pick[:, i, ds(hd, 1)], pick[:, 1 - i, ds(hd, 1)],
                                      MUL, ADD).then_inc(aug_ready, 1)

            def mixer_start():
                for j in range(EARLY, 9):
                    ahead(U_MIX, 0, TILE_UNITS, j)
                    if j == EARLY:
                        dve.wait_ge(wf_hi, 1)
                        cols = [w.rearrange("p a (k n) -> p (a k) n", n=P)[:, :, 0:HEADS] for w in wf_r]
                        dve.tensor_tensor(cols[1], wf_raw, plain(cols[0]), SUB).then_inc(wf_lo, 1)
                dve.memset(scan_ones, 1.0).then_inc(f_step, 1)
                dve.wait_ge(rms_ready, N_MIX_PRE + 1)
                dve.memset(acc[:, 0, :], 0.0).then_inc(acc_zero, 1)
                dve.memset(acc[:, 1, :], 0.0).then_inc(acc_zero, 1)
                dve.wait_ge(f_done, 1)
                dve.tensor_tensor(fz, bank[3][0:HEADS, :], rms[0:HEADS, 0, :], MUL).then_inc(f4_ready, 1)
                dve.wait_ge(f4_ready, 1)
                dve.wait_ge(f_act, 3)
                dve.tensor_scalar(fz, fz, b_col[:, :], 0.0, ADD, MIN).then_inc(f_step, 1)
                dve.wait_ge(f_step, 2)
                dve.tensor_tensor(fz, fz, fa, SUB).then_inc(f_step, 1)
                dve.wait_ge(f_step, 3)
                dve.tensor_tensor_scan(fl, scan_ones, fz, 0.0, MUL, ADD).then_inc(f_step, 1)
                dve.wait_ge(f_act, 4)
                dve.wait_ge(f_step, 4)
                dve.tensor_tensor(f4[32:32 + HEADS, :], fl, plain(f4[0:HEADS, :]), SUB).then_inc(f_step, 1)
                for j in range(9, TILE_UNITS):
                    ahead(U_MIX, 0, TILE_UNITS, j)
                    dve.wait_ge(w_used, U_MIX + j + 1)
                    for c in (2 * (j - 9), 2 * (j - 9) + 1):
                        hold_tile_column(c, bank[MIX_BANK[c]][:, :], 0)
                    if j == 9:
                        qk_split(0, 0)
                v_split(0, 0)
                qk_split(0, 1)
                dve.wait_ge(f_act, 6)
                aug_rows(0)

            def mixer_tile(j, more):
                for hh in range(2):
                    hd = 2 * j + hh
                    rows = slice(HD * hh, HD * hh + HD)

                    def unit(x):
                        if more:
                            ahead(U_MIX + TILE_UNITS, j, TILE_UNITS, 6 * hh + x)

                    def project_out(g):
                        if more:
                            dve.wait_ge(w_used, U_MIX + TILE_UNITS + 6 * hh + 2 * g + 2 + TILE_UNITS * j)
                            hold_tile_column(3 * hh + g, G_BANK[:, :], 0)
                    for b in range(3):
                        c = slice(512 * b, 512 * b + Z_W[b])
                        dve.wait_ge(lnz, 3 * hd + b + 1)
                        dve.scalar_tensor_tensor(spf[:, c], Z[b][:, 0:Z_W[b]], 0.0, el[:, c], MAX, ADD).then_inc(sp_full, 1)
                    for b in range(3):
                        c = slice(512 * b, 512 * b + Z_W[b])
                        dve.wait_ge(sp_hi, 3 * hd + b + 1)
                        dve.tensor_tensor(sp_r[1][:, c], spf[:, c], plain(sp_r[0][:, c]), SUB).then_inc(sp_lo, 1)
                    if hh == 0:
                        v_split(j, 1)

                    def softmax_max(b):
                        lb, at, w = L_AT[b]
                        dve.reduce_max(stat[:, 0, b:b + 1], L_BANKS[lb % 2][:, at:at + w], AX, negate=True).then_inc(neg_max, 1)
                    dve.wait_ge(l_done, 3 * hd + 1)
                    softmax_max(3)
                    dve.wait_ge(l_done, 3 * hd + 2)
                    softmax_max(2)
                    softmax_max(0)

                    def normalise(i, b):
                        lb, at, w = L_AT[b]
                        c = slice(512 * lb + at, 512 * lb + at + w)
                        dve.wait_ge(p_exp, 4 * hd + i + 1)
                        dve.reciprocal(stat[:, 2, b:b + 1], stat[:, 1, b:b + 1]).then_inc(rcp, 1)
                        dve.wait_ge(rcp, 4 * hd + i + 1)
                        dve.tensor_scalar(pr[:, c], pr[:, c], stat[:, 2, b:b + 1], None, MUL).then_inc(p_scaled, 1)
                    for i, b in enumerate((3, 2, 0)):
                        normalise(i, b)
                    unit(0)
                    unit(1)
                    project_out(0)
                    dve.wait_ge(l_done, 3 * hd + 3)
                    softmax_max(1)
                    for b in range(3):
                        c = slice(512 * b, 512 * b + Z_W[b])
                        dve.wait_ge(a_hi, 3 * hd + b + 1)
                        dve.tensor_tensor(sp_r[1][:, c], el[:, c], plain(sp_r[0][:, c]), SUB).then_inc(a_lo, 1)
                    normalise(3, 1)
                    if more or hh == 0:
                        aug_rows(hd + 1)
                    unit(2)
                    unit(3)
                    project_out(1)
                    if hh == 1 and more:
                        qk_split(j + 1, 0)
                        qk_split(j + 1, 1)

                    def out_lo(kind, gain):
                        at = 8 * N_SB + 2 * hd + kind
                        dve.wait_ge(o_hi, 2 * hd + kind + 1)
                        dve.wait_ge(squared, at + 1)
                        dve.scalar_tensor_tensor(oT[1][rows, ds(j + 4 * kind, 1), :].squeeze(1), O_BANK[rows, :],
                                                 gains[rows, ds(GAIN_AT[gain] + j, 1)],
                                                 plain(oT[0][rows, ds(j + 4 * kind, 1), :].squeeze(1)), MUL, SUB).then_inc(o_out, 1)
                        add(N_FOX + 1, at, slot=kind, rows=rows, par=kind)
                    out_lo(0, "sb_group_g")
                    for b in range(3):
                        c = slice(512 * b, 512 * b + Z_W[b])
                        dve.wait_ge(pt_hi, 3 * hd + b + 1)
                        dve.tensor_tensor(pt_r[1][:, c], (T_BANK, L_BANKS[1], L_BANKS[0])[b][:, 0:Z_W[b]],
                                          plain(pt_r[0][:, c]), SUB).then_inc(pt_lo, 1)
                    unit(4)
                    if hh == 1 and more:
                        v_split(j + 1, 0)
                    unit(5)
                    project_out(2)
                    out_lo(1, "fox_group_g")

            dve.wait_ge(gains_t, 1)
            dve.tensor_copy(gains[:, :], bank[0][:, 0:GAIN_ROWS]).then_inc(gains_ready, 1)
            dve.wait_ge(gains_ready, 1)
            post = gains[:, GAIN_AT["ffn1_post_g"]:GAIN_AT["ffn1_post_g"] + DC]
            dve.tensor_scalar(post, post, 0.5, None, MUL)
            post = gains[:, GAIN_AT["ffn2_post_g"]:GAIN_AT["ffn2_post_g"] + DC]
            dve.tensor_scalar(post, post, 0.5, None, MUL).then_inc(gains_ready, 1)
            for u in range(SLOTS):
                lo_of(u + 1, u)
            first_units = early(U_UP[0], STEP_UNITS)
            for k in range(DC + 1):
                if k < DC:
                    dve.wait_ge(x_t, k + 1)
                    dve.tensor_copy(xT[:, k, :], bank[k][:, :]).then_inc(x_ready, 1)
                if k:
                    low(0, k - 1, "ffn1_pre_g")
                    first_units(k - 1)
            up(0)
            down(0)
            into_x(1, N_FFN1_POST, "ffn1_post_g", lambda m: y_low[:, m, :] if m < 4 else bank[m - 4][:, :],
                   "mix_pre_g", early(U_MIX, TILE_UNITS))
            mixer_start()
            dve.sem_inc(o_out, 1)
            with dve.Fori(0, TILES - 1) as j:
                mixer_tile(j, True)
            mixer_tile(TILES - 1, False)
            zero_acc(N_MIX_POST, 0)

            def out_pair(i, st):
                banks = bank[4 * st:4 * st + 4]
                for half in range(2):
                    for q in (2 * half, 2 * half + 1):
                        ahead(U_OUT, i, 4, q)
                    if half == 1 and isinstance(i, int) and i == 0:
                        dve.wait_ge(rms_ready, N_FOX + 1)
                        for a in range(2):
                            dve.tensor_tensor(gu[2 * a], banks[a][:, :], rms[:, 0, :], MUL).then_inc(y_half, 1)
                    if half == 1 or not (isinstance(i, int) and i == 0):
                        dve.wait_ge(w_used, U_OUT + 2 + 2 * half + 4 * i)
                        for a in range(2):
                            dve.tensor_tensor(gu[2 * a + half], banks[2 * half + a][:, :], rms[:, half, :], MUL).then_inc(y_half, 1)
                for a in range(2):
                    dve.wait_ge(y_half, 4 * i + (3 + a))
                    dve.tensor_tensor(y_sb[:, ds(2 * i + a, 1), :].squeeze(1), gu[2 * a], gu[2 * a + 1], ADD).then_inc(y_out, 1)
                for a in range(2):
                    add(N_MIX_POST + 1, 8 * N_MIX_POST + 2 * i + a, par=a)
            out_pair(0, 0)
            with dve.Fori(0, 1) as i:
                out_pair(2 * i + 1, 1)
                out_pair(2 * i + 2, 0)
            out_pair(3, 1)
            into_x(2, N_MIX_POST, "mix_post_g", lambda m: y_sb[:, m, :], "ffn2_pre_g", early(U_UP[1], STEP_UNITS))
            up(1)
            down(1)
            into_x(3, N_FFN2_POST, "ffn2_post_g", lambda m: y_low[:, m, :] if m < 4 else bank[m - 4][:, :],
                   "ple_pre_g")

            dve.wait_ge(g_post_loaded, 16)
            dve.wait_ge(e_copied, 2 * TB)
            for b in range(TB):
                for half in range(2):
                    r = 2 * b + half
                    dve.wait_ge(sig_done, r + 1)
                    dve.tensor_tensor(e_tok[TB * half + b], e_tok[TB * half + b], sig[r % 4], MUL).then_inc(e_out, 1)
                    dve.wait_ge(e_out, r + 1)
                    dve.tensor_tensor(sig[r % 4], e_tok[TB * half + b], g_post[:, 512 * half:512 * half + 512], MUL)\
                       .then_inc(eg_out, 1)
                dve.wait_ge(e_squared, 2 * b + 2)
                dve.tensor_tensor(cols[:, 3, b:b + 1], cols[:, 1, b:b + 1], cols[:, 2, b:b + 1], ADD).then_inc(post_sum, 1)
                dve.wait_ge(eg_out, 2 * b + 2)
                dve.wait_ge(post_ready, b + 1)
                for half in range(2):
                    r = 2 * b + half
                    dve.wait_ge(xt_done, r + 1)
                    dve.scalar_tensor_tensor(sig[r % 4], sig[r % 4], cols[:, 3, b:b + 1], bank[XT_BANK[r]][:, :], MUL, ADD)\
                       .then_inc(out_ready, 1)

        @block.tensor
        def _(pe):
            def product(dst, w_hi_ap, w_lo_ap, m_hi, m_lo, start, stop):
                pe.matmul(dst, w_hi_ap, m_hi, start=start, stop=False, skip_group_check=True)
                pe.matmul(dst, w_lo_ap, m_hi, start=False, stop=False, skip_group_check=True)
                return pe.matmul(dst, w_hi_ap, m_lo, start=False, stop=stop, skip_group_check=True)

            def blocks(dst, slot, col, m_hi, m_lo, start, stop):
                return product(dst, w_slot(0, slot, col), w_slot(1, slot, col), m_hi, m_lo, start, stop)

            def sum_rows(n, s_bank, slot=0):
                pe.wait_ge(added, 8 * n + 8)
                pe.matmul(s_bank[:, :], ones[:, :], acc[:, slot, :], start=True, stop=True).then_inc(summed, 1)

            def up(f, stage):
                n = N_FFN1_PRE if f == 0 else N_FFN2_PRE

                def step(s, st, number):
                    for q in range(4):
                        for kind in range(2):
                            j = 2 * q + kind
                            pe.wait_ge(w_lo, U_UP[f] + j + 1 + STEP_UNITS * s)
                            if number == 0 and j == 0 and f == 0:
                                pe.wait_ge(x_ready, 4)
                            if number == 1 and j == 1:
                                pe.wait_ge(ln_done, n + 1)
                            if number >= 2 and q == 0:
                                pe.wait_ge(up_out, 2 * STEPS * f + 2 * s - 2)
                            for kk in range(2):
                                k = 2 * q + kk
                                if number == 0:
                                    pe.wait_ge(xg_lo, DC * stage + k + 1)
                                for a in range(2):
                                    last = blocks(bank[4 * st + 2 * kind + a][:, :], j % SLOTS, 256 * kk + P * a,
                                                  xg[:, 0, k, :], xg[:, 1, k, :], k == 0, k == DC - 1)
                            last.then_inc(w_used, 1)
                            if number == 0 and j == 6:
                                sum_rows(n, bank[7])
                            if number == 3 and f == 1 and j == 3:
                                pe.wait_ge(p_loaded, 16)
                                pe.wait_ge(up_out, 4 * STEPS - 2)
                                for c in range(2):
                                    for b in range(TB):
                                        tr = pe.transpose(bank[6 + c][:, b * P:(b + 1) * P], p_in[:, b, c * P:(c + 1) * P],
                                                          ident[:, :])
                                    tr.then_inc(p_t, 1)
                step(0, 0, 0)
                step(1, 1, 1)
                with pe.Fori(0, STEPS // 2 - 1) as s2:
                    step(2 * s2 + 2, 0, 2)
                    step(2 * s2 + 3, 1, 2)
                step(STEPS - 1, 0, 3)

            def down(f):
                n = N_FFN1_POST if f == 0 else N_FFN2_POST

                def unit(u, slot, chunk, half, start=False, stop=False):
                    pe.wait_ge(w_lo, u + 1)
                    pe.wait_ge(h_lo_s, 2 * STEPS * f + 1 + chunk)
                    hid = [x[:, ds(chunk, 1), :].squeeze(1) for x in H]
                    for mm in range(4):
                        last = blocks(bank[(4 * half + mm + 4) % 8][:, :], slot, P * mm, hid[0], hid[1], start, stop)
                        if stop and mm < 3:
                            last.then_inc(y_done, 1)
                    last.then_inc(w_used, 1)
                if f == 1:
                    pe.wait_ge(p_copied, 2)
                for j in range(4):
                    if j < 2:
                        pe.wait_ge(up_out, 2 * STEPS * f + 20 + 2 * j)
                    unit(U_DOWN[f] + j, j, j // 2, j % 2, start=j < 2)
                with pe.Fori(1, BODY_STEPS) as s:
                    for j in range(4):
                        unit(U_DOWN[f] + j + 4 * s, j, 2 * s + j // 2, j % 2)
                for j in range(TAIL_UNITS):
                    half, c = divmod(j, 2 * TAIL_STEPS)
                    u = U_DOWN[f] + 4 * BODY_STEPS + j
                    unit(u, u % SLOTS, 2 * BODY_STEPS + c, half, stop=c == 2 * TAIL_STEPS - 1)
                pe.wait_ge(y_copied, 4 * f + 1)
                sum_rows(n, bank[4])

            def mixer_start():
                started = set()
                pe.wait_ge(y_copied, 4)
                for j, (kp, cp) in enumerate(MIX_FIRST):
                    pe.wait_ge(w_lo, U_MIX + j + 1)
                    for kk in range(2):
                        k = 2 * kp + kk
                        pe.wait_ge(xg_lo, DC + k + 1)
                        for cc in range(2):
                            c = 2 * cp + cc
                            if c not in started:
                                started.add(c)
                                if MIX_BANK[c] == 4:
                                    pe.wait_ge(ln_done, N_FFN1_POST + 1)
                                if MIX_BANK[c] < 4:
                                    pe.wait_ge(x_ready, DC + MIX_BANK[c] + 5)
                            last = blocks(bank[MIX_BANK[c]][:, :], (U_MIX + j) % SLOTS, 256 * kk + P * cc,
                                          xg[:, 0, k, :], xg[:, 1, k, :], k == 0, k == DC - 1)
                    last.then_inc(w_used, 1)
                    if j == 8:
                        sum_rows(N_MIX_PRE, bank[2])
                        pe.wait_ge(xg_lo, 2 * DC)
                        pe.wait_ge(wf_lo, 1)
                        wf = [w.rearrange("p a (k n) -> p (a k) n", n=P) for w in wf_r]
                        for k in range(DC):
                            last = product(bank[3][:, :], wf[0][:, k, :], wf[1][:, k, :], xg[:, 0, k, :], xg[:, 1, k, :],
                                           k == 0, k == DC - 1)
                        last.then_inc(f_done, 1)
                pe.wait_ge(hold_ready, 3)
                v_transpose(0)
                pe.wait_ge(hold_ready, 6)
                pe.wait_ge(f4_ready, 1)

            def v_transpose(kind):
                c, b = ((2, T_BANK), (5, O_BANK))[kind]
                for s in range(TB):
                    last = pe.transpose(b[:, s * P:(s + 1) * P], hold[:, c, s * P:(s + 1) * P], ident[:, :])
                last.then_inc(v_t, 1)

            def mixer_tile(j, more):
                for hh in range(2):
                    hd = 2 * j + hh
                    rows = slice(HD * hh, HD * hh + HD)

                    def project(g, halves=(0, 1)):
                        if not more:
                            return
                        for kh in halves:
                            x = 6 * hh + 2 * g + kh
                            pe.wait_ge(w_lo, U_MIX + TILE_UNITS + x + 1 + TILE_UNITS * j)
                            if kh == 0:
                                pe.wait_ge(hold_ready, 6 + 3 * hh + g + 6 * j)
                            for kk in range(4):
                                k = 4 * kh + kk
                                last = blocks(G_BANK[:, :], x % SLOTS, P * kk, xg[:, 0, k, :], xg[:, 1, k, :],
                                              k == 0, k == DC - 1)
                            last.then_inc(w_used, 1)

                    if hh == 0:
                        pe.wait_ge(qk_lo, 4 * j + 2)
                    pe.wait_ge(a_exp, 3 * hd + 1)
                    kt, qt = qk["k_sb"], qk["q_sb"]
                    for b in range(3):
                        for c in Z_BANKS[b]:
                            _, at, w = Z_AT[c]
                            dst = Z[b][:, at:at + w]
                            product(dst, kt[0][rows, c * P:(c + 1) * P], kt[1][rows, c * P:(c + 1) * P],
                                    qt[0][rows, c * P:SEQ], qt[1][rows, c * P:SEQ], at == 0, False)
                            last = pe.matmul(Z[b][:, at:at + P], ident_r, mask_sb, start=False, stop=True, skip_group_check=True)
                        last.then_inc(z_done, 1)
                    if hh == 0:
                        pe.wait_ge(hold_ready, 6 * j + 6)
                        pe.wait_ge(o_out, 2 * hd + 1)
                        v_transpose(1)
                        pe.wait_ge(qk_lo, 4 * j + 4)

                    def logits(b):
                        lb, at, w = L_AT[b]
                        lbank = L_BANKS[lb % 2]
                        dst = lbank[:, at:at + w]
                        qf, kf = qk["q_fx"], qk["k_fx"]
                        product(dst, qf[0][rows, b * P:(b + 1) * P], qf[1][rows, b * P:(b + 1) * P],
                                kf[0][rows, 0:w], kf[1][rows, 0:w], at == 0, False)
                        pe.matmul(dst, aug[0][:, b * P:(b + 1) * P], aug[1][:, 0:w], start=False, stop=False, skip_group_check=True)
                        return pe.matmul(lbank[:, at + b * P:at + (b + 1) * P], ident_r, mask_fx, start=False, stop=True,
                                         skip_group_check=True)
                    pe.wait_ge(aug_ready, 2 * hd + 2)
                    logits(3).then_inc(l_done, 1)
                    logits(2)
                    logits(0).then_inc(l_done, 1)
                    project(0)
                    pe.wait_ge(sp_lo, 3 * hd + 3)
                    for c in range(TB):
                        b, at, w = Z_AT[c]
                        for jc in range(c, TB):
                            jb, jat, jw = Z_AT[jc]
                            off = at + (jc - c) * P
                            lhs = tri_r if jc == c else full_r
                            for part in range(2):
                                last = pe.matmul(Z[b][:, off:off + jw], lhs, sp_r[part][:, 512 * jb + jat:512 * jb + jat + jw],
                                                 start=False, stop=(jc == TB - 1 and part == 1), skip_group_check=True)
                    last.then_inc(tri_done, 1)

                    pe.wait_ge(p_exp, 4 * hd + 1)
                    logits(1).then_inc(l_done, 1)
                    project(1)

                    def weigh(v, a):
                        for c in range(TB):
                            b, at, w = Z_AT[c]
                            first = 512 * b + at
                            last = product(O_BANK[:, c * P:SEQ], v[0][:, c * P:(c + 1) * P], v[1][:, c * P:(c + 1) * P],
                                           a[0][:, first:first + w], a[1][:, first:first + w], c == 0, c == TB - 1)
                        last.then_inc(o_done, 1)
                    pe.wait_ge(a_lo, 3 * hd + 3)
                    pe.wait_ge(o_out, 2 * hd + 1)
                    if hh == 0:
                        pe.wait_ge(v_lo, 2 * j + 2)
                    weigh(v_r["v_sb"], sp_r)
                    pe.wait_ge(p_scaled, 4 * hd + 4)
                    for b in range(3):
                        tbank = (T_BANK, L_BANKS[1], L_BANKS[0])[b]
                        for c in Z_BANKS[b]:
                            _, at, w = Z_AT[c]
                            for q in range(c, TB):
                                lb, lat, _ = L_AT[q]
                                first = 512 * lb + lat + c * P
                                last = pe.transpose(tbank[:, at + (q - c) * P:at + (q - c + 1) * P],
                                                    pr[:, first:first + P], ident[:, :])
                        last.then_inc(pt_done, 1)
                    project(2)
                    if hh == 1 and more:
                        pe.wait_ge(pt_lo, 3 * hd + 1)
                        pe.wait_ge(hold_ready, 6 * j + 9)
                        v_transpose(0)
                    pe.wait_ge(pt_lo, 3 * hd + 3)
                    pe.wait_ge(o_out, 2 * hd + 2)
                    weigh(v_r["v_fx"], pt_r)

            pe.wait_ge(consts, CONSTS)
            pe.wait_ge(gains_loaded, 16 * len(GAINS))
            pe.transpose(bank[0][:, 0:GAIN_ROWS], gains_in, ident[0:GAIN_ROWS, 0:GAIN_ROWS]).then_inc(gains_t, 1)
            for k in range(DC):
                if k == 0:
                    pe.wait_ge(gains_ready, 1)
                if k % 4 == 0:
                    pe.wait_ge(x_loaded[k // 4], 16)
                for b in range(TB):
                    last = pe.transpose(bank[k][:, b * P:(b + 1) * P], x_in[:, b, k * P:(k + 1) * P], ident[:, :])
                last.then_inc(x_t, 1)
            pe.wait_ge(const_hi, 1)
            up(0, 0)
            down(0)
            mixer_start()
            pe.sem_inc(o_done, 1)
            with pe.Fori(0, TILES - 1) as j:
                mixer_tile(j, True)
            mixer_tile(TILES - 1, False)

            def out_pair(i, st, number):
                for q in range(4):
                    pe.wait_ge(w_lo, U_OUT + q + 1 + 4 * i)
                    if number >= 2 and q == 0:
                        pe.wait_ge(y_out, 2 * i - 2)
                    if number == 1 and q == 0:
                        pe.wait_ge(ln_done, N_FOX + 1)
                    for kk in range(2):
                        k = 2 * q + kk
                        for a in range(2):
                            last = blocks(bank[4 * st + 2 * (q // 2) + a][:, :], q, 256 * kk + P * a,
                                          oT[0][:, k, :], oT[1][:, k, :], k % 4 == 0, k % 4 == 3)
                    last.then_inc(w_used, 1)
                    if number == 0 and q == 2:
                        pe.wait_ge(added, 8 * N_FOX + 8)
                        pe.matmul(bank[6][:, :], ones[:, :], acc[:, 0, :], start=True, stop=True).then_inc(summed, 1)
                        pe.matmul(bank[7][:, :], ones[:, :], acc[:, 1, :], start=True, stop=True).then_inc(summed, 1)
            pe.wait_ge(o_out, 2 * HEADS + 1)
            for i in range(4):
                out_pair(i, i % 2, i)
            sum_rows(N_MIX_POST, bank[0])
            up(1, 2)
            down(1)

            pe.wait_ge(y_copied, 8)
            pe.wait_ge(p_lo, 2)
            for r in range(2 * TB):
                half, b = divmod(r, TB)
                tok = slice(b * P, (b + 1) * P)
                pe.wait_ge(ple_lo, 2 * half + 2)
                if r == 3:
                    pe.wait_ge(ln_done, N_FFN2_POST + 1)
                if r >= 4:
                    pe.wait_ge(e_copied, r - 3)
                for k in range(2):
                    last = product(bank[PROJ_BANK[r]][:, :], pT_r[0][:, k, tok], pT_r[1][:, k, tok],
                                   w_ple[0][:, 2 * half + k, :], w_ple[1][:, 2 * half + k, :], k == 0, k == 1)
                last.then_inc(e_done, 1)

            def gate(r, k):
                b, half = divmod(r, 2)
                tok = slice(b * P, (b + 1) * P)
                row = 4 + 2 * k + half
                last = product(bank[GATE_BANK[r]][:, :], xg[:, 0, k, tok], xg[:, 1, k, tok], w_ple[0][:, row, :],
                               w_ple[1][:, row, :], k == 0, k == DC - 1)
                if k == DC - 1:
                    last.then_inc(gate_done, 1)

            def x_transpose(r):
                b, half = divmod(r, 2)
                for k in range(4):
                    last = pe.transpose(bank[XT_BANK[r]][:, k * P:(k + 1) * P], xT[:, 4 * half + k, b * P:(b + 1) * P],
                                        ident[:, :])
                last.then_inc(xt_done, 1)
            pe.wait_ge(e_copied, 2 * TB)
            for k in range(DC):
                pe.wait_ge(xg_lo, 3 * DC + k + 1)
                pe.wait_ge(ple_lo, 4 + 2 * k + 2)
                for r in range(4):
                    gate(r, k)
            pe.wait_ge(added, 8 * N_PLE_PRE + 8)
            for b in range(TB):
                last = pe.matmul(bank[0][:, b:b + 1], acc[:, 0, b * P:(b + 1) * P], ones[:, 0:1], start=True, stop=True)
            last.then_inc(summed, 1)
            for r in range(4):
                if XT_BANK[r] == 0:
                    pe.wait_ge(pre_ln, 1)
                x_transpose(r)
            for r in range(4, 8):
                pe.wait_ge(sig_done, r - 3)
                for k in range(DC):
                    gate(r, k)
                for x in {5: (4, 5), 6: (6, 7)}.get(r, ()):
                    pe.wait_ge(out_ready, x - 3)
                    x_transpose(x)


NAMES = ["x", "p", "ffn1_pre_g", "ffn1_w_gate", "ffn1_w_up", "ffn1_w_down", "ffn1_post_g", "mix_pre_g", "w_in",
         "b_forget", "sb_group_g", "fox_group_g", "w_out", "mix_post_g", "ffn2_pre_g", "ffn2_w_gate", "ffn2_w_up",
         "ffn2_w_down", "ffn2_post_g", "ple_pre_g", "w_ple_gate", "w_ple_proj", "ple_post_g"]


def kernel(**inputs):
    import numpy as np
    import concourse.bacc as bacc
    from concourse.bass_utils import run_bass_kernel_spmd

    nc = bacc.Bacc("TRN2", target_bir_lowering=False, num_devices=1)
    arrays, tensors = {}, {}
    for name in NAMES:
        arrays[f"in_{name}"] = np.ascontiguousarray(inputs[name])
        tensors[name] = nc.dram_tensor(f"in_{name}", arrays[f"in_{name}"].shape, mybir.dt.float32, kind="ExternalInput").ap()
    out = nc.dram_tensor("out_x", (1, SEQ, D), mybir.dt.float32, kind="ExternalOutput").ap()
    build(nc, tensors, out)
    result = run_bass_kernel_spmd(nc, [arrays], core_ids=[0])
    return result.results[0]["out_x"]
```

```python
import concourse.bass as bass
from concourse import mybir
from contextlib import ExitStack

P = 128
SEQ = 512
D = 1024
DC = D // P
FF = 2816
FC = FF // P
HEADS = 8
HD = 64
TILES = HEADS // 2
D_PLE = 256
TB = SEQ // P
EPS = 1e-6
MASKED = -1e30

GAINS = [("ffn1_pre_g", 8), ("ffn1_post_g", 8), ("mix_pre_g", 8), ("sb_group_g", 4), ("fox_group_g", 4),
         ("mix_post_g", 8), ("ffn2_pre_g", 8), ("ffn2_post_g", 8), ("ple_pre_g", 8)]
GAIN_AT = {}
GAIN_ROWS = 0
for _name, _rows in GAINS:
    GAIN_AT[_name] = GAIN_ROWS
    GAIN_ROWS += _rows

SLOTS = 4
STEP_UNITS = 8
STEPS = FC // 2
UP_UNITS = STEPS * STEP_UNITS
DOWN_UNITS = 2 * FC
TILE_UNITS = 12
PARTS = DC
PAIR_UNITS = 3
OUT_UNITS = PARTS + PAIR_UNITS * (DC // 2)
EARLY = 6
FIRST_AHEAD = [(), (), (), (), (0,), (1,), (2, 3), (4, 5)]
TAIL_STEPS = 2
BODY_STEPS = STEPS - TAIL_STEPS
TAIL_UNITS = 4 * TAIL_STEPS
PLE_UNITS = 20
U_UP = [0, UP_UNITS + DOWN_UNITS + TILES * TILE_UNITS + OUT_UNITS]
U_DOWN = [u + UP_UNITS for u in U_UP]
U_MIX = U_DOWN[0] + DOWN_UNITS
U_OUT = U_MIX + TILES * TILE_UNITS
U_PAIR = U_OUT + PARTS
UNITS = U_DOWN[1] + DOWN_UNITS
MIX_PAIRS = [(0, 1), (2, 5), (3, 4)]
MIX_FIRST = [(0, 0), (0, 1), (1, 0), (1, 1), (0, 2), (1, 2), (2, 0), (2, 1), (3, 0), (2, 2), (3, 2), (3, 1)]
MIX_BANK = [5, 6, 7, 0, 1, 4]

Z_AT = {0: (0, 0, 512), 1: (1, 0, 384), 3: (1, 384, 128), 2: (2, 0, 256)}
Z_BANKS = [[0], [1, 3], [2]]
Z_W = [512, 512, 256]
Z_COLS = sum(Z_W)
PART_BANKS = [[(4, 7), (4,), (1,)], [(7,), (4, 0), (1,)]]
PART_AT = [[(0, 1), (2,), (3,)], [(4,), (5, 6), (7,)]]
L_AT = {3: (0, 0, 512), 2: (1, 0, 384), 0: (1, 384, 128), 1: (2, 0, 256)}

PROJ_BANK = [5, 6, 7, 4] * 2
GATE_BANK = [4, 5, 6, 7] * 2
XT_BANK = [1, 2, 3, 0] * 2

N_FFN1_PRE, N_FFN1_POST, N_MIX_PRE, N_SB, N_FOX, N_MIX_POST, N_FFN2_PRE, N_FFN2_POST, N_PLE_PRE = range(9)


def build(nc, t, out):
    f32, f32r = mybir.dt.float32, mybir.dt.float32r
    ALU, ACT, AX = mybir.AluOpType, mybir.ActivationFunctionType, mybir.AxisListType.X
    MUL, ADD, SUB, MAX, MIN = ALU.mult, ALU.add, ALU.subtract, ALU.max, ALU.min

    def ds(start, size):
        return bass.ds(start, size)

    with ExitStack() as ctx:
        def sb(name, shape, dt=f32):
            return ctx.enter_context(nc.sbuf_tensor(name, shape, dt))

        def sem(name):
            return ctx.enter_context(nc.semaphore(name))

        def plain(ap):
            return ap.bitcast(f32)

        xT = sb("xT", [P, DC, SEQ])
        xg = sb("xg", [P, 2, DC, SEQ], f32r)
        big = sb("big", [P, 2 * FC, SEQ], f32r)
        w_raw = sb("w_raw", [P, SLOTS, 4 * P])
        w_r = sb("w_r", [P, 2, SLOTS, 4 * P], f32r)
        scratch = sb("scratch", [P, 6912])
        acc = sb("acc", [P, 2, SEQ])
        sq = sb("sq", [P, 2, SEQ])
        rms = sb("rms", [P, 2, SEQ])
        gains = sb("gains", [P, GAIN_ROWS])
        ident = sb("ident", [P, P])
        ones = sb("ones", [P, P])
        const_r = sb("const_r", [P, 5, P], f32r)
        f4 = sb("f4", [P, SEQ], f32r)
        pick = sb("pick", [P, 2, HEADS])
        b_col = sb("b_col", [HEADS, 1])
        eps_col = sb("eps_col", [P, 1])
        stat = sb("stat", [P, 4, TB])
        cols = sb("cols", [P, 4, TB])

        ident_r, tri_r, full_r, mask_sb, mask_fx = (const_r[:, i, :] for i in range(5))
        H = [big[:, 0:FC, :], big[:, FC:2 * FC, :]]
        qk = {n: [big[:, 2 * i + p, :] for p in range(2)] for i, n in enumerate(["q_sb", "k_sb", "q_fx", "k_fx"])}
        v_r = {n: [big[:, 8 + 2 * i + p, :] for p in range(2)] for i, n in enumerate(["v_sb", "v_fx"])}
        aug = [big[:, 12 + i, :] for i in range(2)]
        wf_r = [big[:, 14:16, :], big[:, 16:18, :]]
        oT = [big[:, 18:26, :], big[:, 26:34, :]]

        wide = big[:, 34:44, :].rearrange("p r n -> p (r n)").rearrange("p (i n) -> p i n", n=Z_COLS)
        sp_r = [wide[:, i, :] for i in range(2)]
        pt_r = [wide[:, 2 + i, :] for i in range(2)]
        w_ple = [big[:, 0:PLE_UNITS, :], big[:, FC:FC + PLE_UNITS, :]]
        pT_r = [xg[:, i, DC - 2:DC, :] for i in range(2)]
        gu = [scratch[:, i * SEQ:(i + 1) * SEQ] for i in range(4)]
        y_low = scratch[:, 2048:4096].rearrange("p (c n) -> p c n", n=SEQ)
        ple_raw = gu[0:2]
        sig = gu
        g_post = scratch[:, 2048:3072]
        p_in = scratch[:, 5120:6144].rearrange("p (b n) -> p b n", n=D_PLE)
        pT = [scratch[:, 4096 + i * SEQ:4096 + (i + 1) * SEQ] for i in range(2)]
        e_tok = [w_raw[:, i, :] for i in range(TB)] + [scratch[:, 4096 + i * SEQ:4096 + (i + 1) * SEQ] for i in range(TB)]
        y_sb = scratch[:, 2560:6656].rearrange("p (c n) -> p c n", n=SEQ)
        x_in = scratch[:, 2560:6656].rearrange("p (b n) -> p b n", n=D)
        hold = scratch[:, 0:3072].rearrange("p (c n) -> p c n", n=SEQ)
        el = scratch[:, 3072:4352]
        spf = scratch[:, 4352:5632]
        pr = scratch[:, 5632:6912]
        wf_raw = scratch[:, 6656:6720].rearrange("p (k n) -> p k n", n=HEADS)
        gains_in = scratch[0:GAIN_ROWS, 1536:1536 + P]
        const_in = scratch[:, 0:5 * P].rearrange("p (i n) -> p i n", n=P)
        scan_ones = el[0:HEADS, 0:SEQ]
        fz, fa, fl = (spf[0:HEADS, 0:SEQ], spf[0:HEADS, SEQ:2 * SEQ], pr[0:HEADS, 0:SEQ])

        bank = [ctx.enter_context(nc.psum_tensor(f"bank{i}", [P, SEQ], f32)) for i in range(8)]
        Z, O_BANK, G_BANK, L_BANKS, T_BANK = bank[0:3], bank[3], bank[4], [bank[5], bank[6]], bank[7]

        gains_loaded, b_loaded, wf_loaded, p_loaded = map(sem, ("gains_loaded", "b_loaded", "wf_loaded", "p_loaded"))
        first_gains_loaded = sem("first_gains_loaded")
        x_loaded = [sem(f"x_loaded{i}") for i in range(2)]
        raw_loaded = [sem(f"raw_loaded{i}") for i in range(SLOTS)]
        raw_loaded_2nd = [sem(f"raw_loaded_2nd{i}") for i in range(SLOTS)]
        w_hi, w_lo, w_used = sem("w_hi"), sem("w_lo"), sem("w_used")
        zeroed, consts, const_hi = sem("zeroed"), sem("consts"), sem("const_hi")
        gains_t, gains_ready, x_t = sem("gains_t"), sem("gains_ready"), sem("x_t")
        x_ready, xg_hi, xg_lo = sem("x_ready"), sem("xg_hi"), sem("xg_lo")
        squared, acc_zero, added, summed, ln_done, rms_ready = map(sem, (
            "squared", "acc_zero", "added", "summed", "ln_done", "rms_ready"))
        gate_out, up_out, silu_done, h_f, h_hi_s, h_lo_s = map(sem, (
            "gate_out", "up_out", "silu_done", "h_full", "h_hi", "h_lo"))
        y_done, y_copied, y_scaled = sem("y_done"), sem("y_copied"), sem("y_scaled")
        wf_zero, wf_hi, wf_lo, f_done, f_step, f_act, f4_ready = map(sem, (
            "wf_zero", "wf_hi", "wf_lo", "f_done", "f_step", "f_act", "f4_ready"))
        hold_ready, qk_hi, qk_lo, v_t, v_hi, v_lo = map(sem, (
            "hold_ready", "qk_hi", "qk_lo", "v_t", "v_hi", "v_lo"))
        z_done, absz, exp_z, lnz, sp_full, sp_hi, sp_lo, tri_done, a_exp, a_hi, a_lo = map(sem, (
            "z_done", "absz", "exp_z", "lnz", "sp_full", "sp_hi", "sp_lo", "tri_done", "a_exp", "a_hi", "a_lo"))
        aug_ready, l_done, neg_max, p_exp, rcp, p_scaled, pt_done, pt_hi, pt_lo = map(sem, (
            "aug_ready", "l_done", "neg_max", "p_exp", "rcp", "p_scaled", "pt_done", "pt_hi", "pt_lo"))
        o_done, o_hi, o_out = sem("o_done"), sem("o_hi"), sem("o_out")
        part_hi, part_lo = sem("part_hi"), sem("part_lo")
        fox_done, y_half, y_out = sem("fox_done"), sem("y_half"), sem("y_out")
        p_t, p_copied, p_hi, p_lo = sem("p_t"), sem("p_copied"), sem("p_hi"), sem("p_lo")
        ple_loaded = [sem(f"ple_loaded{i}") for i in range(2)]
        ple_hi, ple_lo, g_post_loaded = sem("ple_hi"), sem("ple_lo"), sem("g_post_loaded")
        e_done, e_copied, gate_done, sig_done, e_out, e_squared, eg_out = map(sem, (
            "e_done", "e_copied", "gate_done", "sig_done", "e_out", "e_squared", "eg_out"))
        pre_ln, pre_ready, post_sum, post_ln, post_ready = map(sem, (
            "pre_ln", "pre_ready", "post_sum", "post_ln", "post_ready"))
        xt_done, out_ready = sem("xt_done"), sem("out_ready")
        out_stored = [sem(f"out_stored{i}") for i in range(4)]

        block = ctx.enter_context(nc.Block())

        @block.sync
        def _(sp):
            def load_gains(names, loaded):
                for name, rows in names:
                    sp.dma_start(gains_in[GAIN_AT[name]:GAIN_AT[name] + rows, :],
                                 t[name][0].rearrange("(c p) -> c p", p=P)).then_inc(loaded, 16)
            load_gains(GAINS[:1], first_gains_loaded)
            x_rows = t["x"][0].rearrange("(b p) d -> p b d", p=P)

            def load_x(half):
                c = slice(512 * half, 512 * half + 512)
                sp.dma_start(x_in[:, :, c], x_rows[:, :, c]).then_inc(x_loaded[half], 16)
            load_x(0)
            w_in = t["w_in"][0].rearrange("(k p) n -> p k n", p=P)
            def load_unit(u, slot, src, k, size=4 * P):
                if not isinstance(u, int) or u >= SLOTS:
                    sp.wait_ge(w_lo, u - SLOTS + 1)
                dst = w_raw[:, slot, 0:size].rearrange("p (k n) -> p k n", k=k)
                sp.dma_start(dst, src).then_inc(raw_loaded[slot], 16)

            def load_up(f):
                w = [t[f"ffn{f + 1}_w_{kind}"][0].rearrange("(k p) n -> p k n", p=P) for kind in ("gate", "up")]

                def step_unit(s, j):
                    q, kind = divmod(j, 2)
                    load_unit(U_UP[f] + STEP_UNITS * s + j, j % SLOTS,
                              w[kind][:, 2 * q:2 * q + 2, ds(s * 256, 256)], 2)

                def step(s):
                    for j in range(STEP_UNITS):
                        step_unit(s, j)
                if f == 0:
                    for j in range(SLOTS):
                        if j == 2:
                            load_x(1)
                        step_unit(0, j)
                    load_gains(GAINS[1:], gains_loaded)
                    for j in range(SLOTS, STEP_UNITS):
                        step_unit(0, j)
                else:
                    step(0)
                with sp.Fori(1, STEPS) as s:
                    step(s)

            w_pg = t["w_ple_gate"][0].rearrange("(k p) n -> p k n", p=P)
            w_pp = t["w_ple_proj"][0].rearrange("(k p) n -> p k n", p=P)

            def load_ple(i, slot, src):
                if not isinstance(i, int) or i >= 2:
                    sp.wait_ge(ple_lo, i - 1)
                sp.dma_start(ple_raw[slot].unsqueeze(1), src).then_inc(ple_loaded[slot], 16)

            def load_gates(step):
                for i in range(2):
                    load_ple(2 * step + i, i, w_pg[:, ds(step - 2, 1), 512 * i:512 * i + 512])

            def load_down(f):
                w = t[f"ffn{f + 1}_w_down"][0].rearrange("(k p) n -> p k n", p=P)

                def step(s):
                    for j in range(4):
                        half, c = divmod(j, 2)
                        load_unit(U_DOWN[f] + 4 * s + j, j,
                                  w[:, ds(2 * s + c, 1), 512 * half:512 * half + 512], 1)
                if f == 0:
                    with sp.Fori(0, BODY_STEPS) as s:
                        step(s)
                else:
                    step(0)
                    step(1)
                    sp.wait_ge(h_lo_s, 4 * STEPS)
                    for s in range(1, 3):
                        if s > 1:
                            step(s)
                        for i in range(2):
                            load_ple(2 * s - 2 + i, i, w_pp[:, i:i + 1, 512 * (s - 1):512 * s])
                    with sp.Fori(3, BODY_STEPS) as s:
                        step(s)
                        load_gates(s - 1)
                for j in range(TAIL_UNITS):
                    if j == 2 * TAIL_STEPS and f == 1:
                        load_gates(BODY_STEPS - 1)
                    half, c = divmod(j, 2 * TAIL_STEPS)
                    u = U_DOWN[f] + 4 * BODY_STEPS + j
                    load_unit(u, u % SLOTS, w[:, 2 * BODY_STEPS + c:2 * BODY_STEPS + c + 1, 512 * half:512 * half + 512], 1)

            load_up(0)
            sp.dma_start(b_col[:, :], t["b_forget"][0].rearrange("(h o) -> h o", o=1)).then_inc(b_loaded, 16)
            sp.dma_start(wf_raw, w_in[:, :, 6 * 512:6 * 512 + HEADS]).then_inc(wf_loaded, 16)
            load_down(0)
            w_six = w_in[:, :, 0:6 * 512].rearrange("p k (c n) -> p k c n", n=512)
            for j, (kp, cp) in enumerate(MIX_FIRST):
                u = U_MIX + j
                sp.wait_ge(w_lo, u - SLOTS + 1)
                c0, c1 = MIX_PAIRS[cp]
                for k, loaded in enumerate((raw_loaded, raw_loaded_2nd)):
                    sp.dma_start(w_raw[:, u % SLOTS, 256 * k:256 * k + 256].rearrange("p (c n) -> p c n", c=2),
                                 w_six[:, 2 * kp + k, c0:c1 + 1:c1 - c0, 0:P]).then_inc(loaded[u % SLOTS], 16)
            with sp.Fori(1, TILES) as tile:
                for j in range(TILE_UNITS):
                    c, kh = divmod(j, 2)
                    load_unit(U_MIX + TILE_UNITS * tile + j, j % SLOTS,
                              w_in[:, 4 * kh:4 * kh + 4, ds(512 * c + tile * P, P)], 4)
            w_out = t["w_out"][0].rearrange("(k p) n -> p k n", p=P)
            for r in range(PARTS):
                load_unit(U_OUT + r, r % SLOTS, w_out[:, 0:TILES - 1, P * r:P * (r + 1)], TILES - 1, (TILES - 1) * P)
            for i in range(DC // 2):
                u = U_PAIR + PAIR_UNITS * i
                c = slice(2 * P * i, 2 * P * (i + 1))
                load_unit(u, u % SLOTS, w_out[:, TILES - 1:TILES, c], 1, 2 * P)
                for q in range(2):
                    load_unit(u + 1 + q, (u + 1 + q) % SLOTS, w_out[:, TILES + 2 * q:TILES + 2 * q + 2, c], 2)
            load_up(1)
            sp.wait_ge(x_ready, 3 * DC)
            sp.dma_start(p_in, t["p"][0, 0].rearrange("(b p) d -> p b d", p=P)).then_inc(p_loaded, 16)
            load_down(1)
            load_gates(BODY_STEPS)
            sp.wait_ge(x_ready, 4 * DC)
            sp.dma_start(g_post, t["ple_post_g"][0].partition_broadcast(P)).then_inc(g_post_loaded, 16)
            for r in range(2 * TB):
                b, half = divmod(r, 2)
                sp.wait_ge(out_ready, r + 1)
                sp.dma_start(out[0, b * P:(b + 1) * P, 512 * half:512 * half + 512], sig[r % 4]).then_inc(out_stored[r % 4], 16)
            for i in range(4):
                sp.wait_ge(out_stored[i], 32)

        @block.gpsimd
        def _(pool):
            n = [0]

            def settle(ins):
                n[0] += 1
                ins.then_inc(zeroed, 1)

            settle(pool.memset(ident[:, :], 0.0))
            settle(pool.memset(const_in[:, 0, :], 0.0))
            settle(pool.memset(const_in[:, 1, :], -1.0))
            settle(pool.memset(const_in[:, 3, :], 0.0))
            settle(pool.memset(const_in[:, 4, :], 0.0))
            settle(pool.memset(pick[:, :, :], 0.0))
            pool.memset(const_in[:, 2, :], -1.0).then_inc(consts, 1)
            pool.memset(ones[:, :], 1.0).then_inc(consts, 1)
            pool.memset(eps_col[:, :], EPS).then_inc(consts, 1)
            pool.memset(plain(f4[:, :]), 0.0).then_inc(consts, 1)
            pool.wait_ge(zeroed, n[0])

            def select(m, sign, op, fill, base=0):
                return pool.affine_select(out=m, in_=m, compare_op=op, fill=fill, base=base,
                                          pattern=[[-sign, m.shape[-1]]], channel_multiplier=sign)
            select(ident[:, :], 1, ALU.not_equal, 1.0).then_inc(consts, 1)
            select(const_in[:, 0, :], 1, ALU.not_equal, 1.0).then_inc(consts, 1)
            select(const_in[:, 1, :], 1, ALU.is_ge, 0.0).then_inc(consts, 1)
            select(const_in[:, 3, :], -1, ALU.is_gt, MASKED).then_inc(consts, 1)
            select(const_in[:, 4, :], 1, ALU.is_ge, MASKED).then_inc(consts, 1)
            for i in range(4):
                if i % 2:
                    pool.wait_ge(consts, 9 + i)
                select(pick[:, i // 2, :], 1, ALU.not_equal, 1.0, base=-32 * i).then_inc(consts, 1)

            def add_squares(n, chunks=DC):
                if n:
                    pool.wait_ge(summed, n)
                pool.memset(acc[:, 0, :], 0.0).then_inc(acc_zero, 1)
                pool.wait_ge(acc_zero, n + 1)
                for k in range(chunks):
                    at = 8 * n + k
                    pool.wait_ge(squared, at + 1)
                    if at:
                        pool.wait_ge(added, at)
                    pool.tensor_tensor(acc[:, 0, :], acc[:, 0, :], sq[:, k % 2, :], ADD).then_inc(added, 1)
            add_squares(N_FFN1_PRE)
            pool.wait_ge(w_used, U_MIX)
            for p in range(2):
                pool.memset(plain(wf_r[p]), 0.0).then_inc(wf_zero, 1)
            add_squares(N_MIX_PRE)
            add_squares(N_MIX_POST, DC - 2)
            add_squares(N_FFN2_PRE)
            add_squares(N_PLE_PRE)

        CONSTS = 13

        def w_slot(p, slot, first, size=P):
            return w_r[:, p, slot, first:first + size]

        @block.scalar
        def _(act):
            def split_hi(u, slot, after=None):
                if after is not None:
                    act.wait_ge(w_used, after)
                if isinstance(u, int):
                    act.wait_ge(raw_loaded[slot], 16 * (u // SLOTS + 1))
                    if U_MIX <= u < U_MIX + TILE_UNITS:
                        act.wait_ge(raw_loaded_2nd[slot], 16 * ((u - U_MIX) // SLOTS + 1))
                else:
                    act.wait_ge(raw_loaded[slot], u)
                act.activation(w_slot(0, slot, 0, 4 * P), w_raw[:, slot, :], ACT.Copy).then_inc(w_hi, 1)

            def ahead(base, i, stride, j):
                slot = (base + j) % SLOTS
                if isinstance(i, int):
                    u = base + stride * i + j
                    if u + SLOTS < UNITS:
                        split_hi(u + SLOTS, u % SLOTS, after=u + 1)
                else:
                    split_hi(16 * ((base + j) // SLOTS + 2) + i * (4 * stride), slot, after=base + j + 1 + stride * i)

            def squares(at, src, rows=slice(0, P), par=0):
                if not isinstance(at, int) or at >= 2:
                    act.wait_ge(added, at - 1)
                act.activation(sq[rows, par, :], src, ACT.Square).then_inc(squared, 1)

            def factor(n, slot, s_bank, count):
                act.wait_ge(summed, n + 1)
                act.activation(rms[:, slot, :], s_bank[:, :], ACT.Ln, bias=eps_col[:, :], scale=1.0 / count).then_inc(ln_done, 1)
                act.wait_ge(ln_done, n + 1)
                act.activation(rms[:, slot, :], rms[:, slot, :], ACT.Exp, scale=-0.5).then_inc(rms_ready, 1)

            def prep(stage, n, gain, used, between=None):
                g = GAIN_AT[gain]
                if used:
                    act.wait_ge(w_used, used)
                for k in range(DC):
                    act.wait_ge(x_ready, DC * stage + k + 1)
                    act.activation(xg[:, 0, k, :], xT[:, k, :], ACT.Copy, scale=gains[:, g + k:g + k + 1]).then_inc(xg_hi, 1)
                    squares(8 * n + k, xT[:, k, :], par=k % 2)
                    if between:
                        between(k)

            def up(f, pre_bank):
                n = N_FFN1_PRE if f == 0 else N_FFN2_PRE

                def step(s, first=False, p_copy=False):
                    for j in range(EARLY if first else 0, STEP_UNITS):
                        ahead(U_UP[f], s, STEP_UNITS, j)
                        if p_copy and j == 5:
                            for c in range(2):
                                act.wait_ge(p_t, c + 1)
                                act.activation(pT[c], bank[6 + c][:, :], ACT.Copy).then_inc(p_copied, 1)
                        if first and j == 6:
                            factor(n, 0, pre_bank, D)
                    for a in range(2):
                        at = 2 * s + (2 * STEPS * f + a + 1)
                        act.wait_ge(gate_out, at)
                        act.activation(gu[a], gu[a], ACT.Silu).then_inc(silu_done, 1)
                    for a in range(2):
                        at = 2 * s + (2 * STEPS * f + a + 1)
                        act.wait_ge(h_f, at)
                        act.activation(H[0][:, ds(2 * s + a, 1), :], gu[2 + a].unsqueeze(1), ACT.Copy).then_inc(h_hi_s, 1)
                step(0, first=True)
                with act.Fori(1, STEPS - 1) as s:
                    step(s)
                step(STEPS - 1, p_copy=f == 1)

            def split_ple(i, slot, used):
                act.wait_ge(w_used, used)
                act.wait_ge(ple_loaded[slot], 8 * (i - slot) + 16)
                act.activation(w_ple[0][:, ds(i, 1), :], ple_raw[slot].unsqueeze(1), ACT.Copy).then_inc(ple_hi, 1)

            def down(f):
                n = N_FFN1_POST if f == 0 else N_FFN2_POST
                base = U_DOWN[f] + 4 * BODY_STEPS
                act.preload_act_table_set("natural_log_exp_and_others")

                def step(s):
                    if f == 1:
                        for i in range(2):
                            split_ple(2 * s - 2 + i, i, U_DOWN[f] + 4 * s)
                    for j in range(4):
                        ahead(U_DOWN[f], s, 4, j)
                for j in range(4):
                    ahead(U_DOWN[f], 0, 4, j)
                if f == 1:
                    act.wait_ge(p_copied, 2)
                    act.wait_ge(w_used, U_DOWN[1])
                    for c in range(2):
                        act.activation(pT_r[0][:, c, :], pT[c], ACT.Copy).then_inc(p_hi, 1)
                with act.Fori(1, BODY_STEPS) as s:
                    step(s)
                if f == 1:
                    for i in range(2):
                        split_ple(2 * BODY_STEPS - 2 + i, i, base)
                for j in range(4):
                    ahead(base, 0, 4, j)
                for m in range(4):
                    if m == 3:
                        act.wait_ge(w_used, base + 4)
                    else:
                        act.wait_ge(y_done, 6 * f + m + 1)
                    squares(8 * n + m, bank[m + 4][:, :], par=m % 2)
                for j in range(4, 7):
                    ahead(base, 0, 4, j)
                if f == 1:
                    for i in range(2):
                        split_ple(PLE_UNITS - 2 + i, i, base + 6)
                for m in range(4, 8):
                    if m == 7:
                        act.wait_ge(w_used, base + 8)
                    else:
                        act.wait_ge(y_done, 6 * f + m)
                    squares(8 * n + m, bank[m - 4][:, :], par=m % 2)
                ahead(base, 0, 4, 7)
                factor(n, 0, bank[4], D)

            def qk_split(tile, kind):
                first = isinstance(tile, int) and tile == 0
                act.wait_ge(hold_ready, (2, 4)[kind] if first else 6 * tile + 3 * kind + 2)
                for name, c in ((("q_sb", 0), ("k_sb", 1)), (("q_fx", 3), ("k_fx", 4)))[kind]:
                    act.activation(qk[name][0], hold[:, c, :], ACT.Copy).then_inc(qk_hi, 1)

            def v_split(tile, kind):
                act.wait_ge(v_t, 2 * tile + kind + 1)
                act.activation(v_r[("v_sb", "v_fx")[kind]][0], (T_BANK, O_BANK)[kind][:, :], ACT.Copy).then_inc(v_hi, 1)

            def mixer_start():
                for j in range(EARLY, 9):
                    ahead(U_MIX, 0, TILE_UNITS, j)
                    if j == EARLY:
                        act.wait_ge(wf_zero, 2)
                        act.wait_ge(wf_loaded, 16)
                        act.activation(wf_r[0].rearrange("p a (k n) -> p (a k) n", n=P)[:, :, 0:HEADS], wf_raw,
                                       ACT.Copy).then_inc(wf_hi, 1)
                factor(N_MIX_PRE, 0, bank[2], D)
                qk_split(0, 0)
                act.wait_ge(f4_ready, 1)
                act.wait_ge(b_loaded, 16)
                act.activation(fa, fz, ACT.Abs, bias=b_col[:, :]).then_inc(f_act, 1)
                act.wait_ge(f_act, 1)
                act.activation(fa, fa, ACT.Exp, scale=-1.0).then_inc(f_act, 1)
                act.wait_ge(f_act, 2)
                act.activation(fa, fa, ACT.Ln, bias=1.0).then_inc(f_act, 1)
                ahead(U_MIX, 0, TILE_UNITS, 9)
                act.wait_ge(f_step, 4)
                act.activation(f4[0:HEADS, :], fl, ACT.Copy).then_inc(f_act, 1)
                act.wait_ge(f_act, 4)
                act.activation(f4[64:64 + HEADS, :], plain(f4[0:HEADS, :]), ACT.Copy, scale=-1.0).then_inc(f_act, 1)
                qk_split(0, 1)
                act.wait_ge(f_step, 5)
                act.activation(f4[96:96 + HEADS, :], plain(f4[32:32 + HEADS, :]), ACT.Copy, scale=-1.0).then_inc(f_act, 1)
                ahead(U_MIX, 0, TILE_UNITS, 10)
                v_split(0, 0)
                ahead(U_MIX, 0, TILE_UNITS, 11)

            def mixer_tile(j, more):
                for hh in range(2):
                    hd = 2 * j + hh
                    rows = slice(HD * hh, HD * hh + HD)

                    def unit(x):
                        if more:
                            ahead(U_MIX + TILE_UNITS, j, TILE_UNITS, 6 * hh + x)
                        elif x % 2 == 0:
                            for r, b in zip(PART_AT[hh][x // 2], PART_BANKS[hh][x // 2]):
                                act.wait_ge(w_used, U_OUT + r + 1)
                                act.activation(xg[:, 0, r, :], bank[b][:, :], ACT.Copy).then_inc(part_hi, 1)
                                ahead(U_OUT, 0, 0, r)
                    for b in range(3):
                        e = el[:, 512 * b:512 * b + Z_W[b]]
                        act.wait_ge(z_done, 3 * hd + b + 1)
                        act.activation(e, Z[b][:, 0:Z_W[b]], ACT.Abs).then_inc(absz, 1)
                        act.wait_ge(absz, 3 * hd + b + 1)
                        act.activation(e, e, ACT.Exp, scale=-1.0).then_inc(exp_z, 1)
                        act.wait_ge(exp_z, 3 * hd + b + 1)
                        act.activation(e, e, ACT.Ln, bias=1.0).then_inc(lnz, 1)
                    for b in range(3):
                        c = slice(512 * b, 512 * b + Z_W[b])
                        act.wait_ge(sp_full, 3 * hd + b + 1)
                        act.activation(sp_r[0][:, c], spf[:, c], ACT.Copy).then_inc(sp_hi, 1)
                    if hh == 0:
                        v_split(j, 1)

                    def softmax_exp(i, b):
                        lb, at, w = L_AT[b]
                        src = L_BANKS[lb % 2][:, at:at + w]
                        first = 512 * lb + at
                        act.wait_ge(neg_max, 4 * hd + (1, 3, 3, 4)[i])
                        act.activation(pr[:, first:first + w], src, ACT.Exp, bias=stat[:, 0, b:b + 1],
                                       accum_out=stat[:, 1, b:b + 1]).then_inc(p_exp, 1)
                    for i, b in enumerate((3, 2, 0)):
                        softmax_exp(i, b)
                    unit(0)
                    unit(1)
                    act.wait_ge(tri_done, hd + 1)
                    for b in range(3):
                        c = slice(512 * b, 512 * b + Z_W[b])
                        act.activation(el[:, c], Z[b][:, 0:Z_W[b]], ACT.Exp).then_inc(a_exp, 1)
                        act.wait_ge(a_exp, 3 * hd + b + 2)
                        act.activation(sp_r[0][:, c], el[:, c], ACT.Copy).then_inc(a_hi, 1)
                    softmax_exp(3, 1)
                    unit(2)
                    unit(3)
                    if hh == 1 and more:
                        qk_split(j + 1, 0)
                        qk_split(j + 1, 1)

                    def out_hi(kind, gain):
                        act.wait_ge(o_done, 2 * hd + kind + 2)
                        g = gains[rows, ds(GAIN_AT[gain] + j, 1)]
                        act.activation(oT[0][rows, ds(j + 4 * kind, 1), :], O_BANK[rows, :].unsqueeze(1), ACT.Copy,
                                       scale=g).then_inc(o_hi, 1)
                        squares(8 * N_SB + 2 * hd + kind, O_BANK[rows, :], rows, kind)
                    out_hi(0, "sb_group_g")
                    for b in range(3):
                        c = slice(512 * b, 512 * b + Z_W[b])
                        act.wait_ge(pt_done, 3 * hd + b + 1)
                        act.activation(pt_r[0][:, c], (T_BANK, L_BANKS[1], L_BANKS[0])[b][:, 0:Z_W[b]],
                                       ACT.Copy).then_inc(pt_hi, 1)
                    unit(4)
                    if hh == 1 and more:
                        v_split(j + 1, 0)
                    unit(5)
                    out_hi(1, "fox_group_g")

            act.wait_ge(consts, CONSTS)
            act.activation(const_r[:, :, :], const_in, ACT.Copy).then_inc(const_hi, 1)
            act.wait_ge(gains_ready, 1)

            def early(base, stride):
                def between(k):
                    if k >= 2:
                        ahead(base, 0, stride, k - 2)
                return between

            def first_units(k):
                if k < SLOTS:
                    split_hi(k, k)
                for j in FIRST_AHEAD[k]:
                    ahead(U_UP[0], 0, STEP_UNITS, j)
            prep(0, N_FFN1_PRE, "ffn1_pre_g", None, first_units)
            up(0, bank[7])
            down(0)
            prep(1, N_MIX_PRE, "mix_pre_g", U_DOWN[0], early(U_MIX, TILE_UNITS))
            mixer_start()
            act.sem_inc(a_exp, 1)
            with act.Fori(0, TILES - 1) as j:
                mixer_tile(j, True)
            mixer_tile(TILES - 1, False)

            for i in range(DC // 2):
                base = U_PAIR + PAIR_UNITS * i
                ahead(base, 0, 0, 0)
                ahead(base, 0, 0, 1)
                if i == 0:
                    factor(N_SB, 0, bank[6], D // 2)
                    factor(N_FOX, 1, bank[7], D // 2)
                for a in range(2):
                    act.wait_ge(y_out, 2 * i + a + 1)
                    squares(8 * N_MIX_POST + 2 * i + a, y_sb[:, 2 * i + a, :], par=a)
                ahead(base, 0, 0, 2)
            factor(N_MIX_POST, 0, bank[0], D)
            prep(2, N_FFN2_PRE, "ffn2_pre_g", U_UP[1], early(U_UP[1], STEP_UNITS))
            up(1, bank[7])
            down(1)

            def e_copy(r):
                act.wait_ge(e_done, r + 1)
                half, b = divmod(r, TB)
                act.activation(e_tok[TB * half + b], bank[PROJ_BANK[r]][:, :], ACT.Copy).then_inc(e_copied, 1)

            def e_copies(k):
                for r in (2 * k + 1, 2 * k + 2):
                    if r < 2 * TB:
                        e_copy(r)
                if k == 5:
                    act.wait_ge(e_done, 2 * TB)
            act.wait_ge(w_lo, UNITS)
            e_copy(0)
            prep(3, N_PLE_PRE, "ple_pre_g", None, e_copies)
            act.wait_ge(summed, N_PLE_PRE + 1)
            act.activation(cols[:, 0, :], bank[0][:, 0:TB], ACT.Ln, bias=eps_col[:, :], scale=1.0 / D).then_inc(pre_ln, 1)
            act.wait_ge(pre_ln, 1)
            act.activation(cols[:, 0, :], cols[:, 0, :], ACT.Exp, scale=-0.5).then_inc(pre_ready, 1)
            act.wait_ge(pre_ready, 1)
            act.wait_ge(x_ready, 4 * DC)
            act.wait_ge(ple_lo, PLE_UNITS)
            act.wait_ge(added, 8 * N_PLE_PRE + 8)
            for b in range(TB):
                for half in range(2):
                    r = 2 * b + half
                    act.wait_ge(gate_done, r + 1)
                    if r >= 4:
                        act.wait_ge(out_stored[r % 4], 16)
                    act.activation(sig[r % 4], bank[GATE_BANK[r]][:, :], ACT.Sigmoid, scale=cols[:, 0, b:b + 1]).then_inc(sig_done, 1)
                act.preload_act_table_set("natural_log_exp_and_others")
                for half in range(2):
                    r = 2 * b + half
                    act.wait_ge(e_out, r + 1)
                    if r >= 2:
                        act.wait_ge(e_squared, r - 1)
                    act.activation(sq[:, half, :], e_tok[TB * half + b], ACT.Square,
                                   accum_out=cols[:, 1 + half, b:b + 1]).then_inc(e_squared, 1)
                act.wait_ge(post_sum, b + 1)
                act.activation(cols[:, 3, b:b + 1], cols[:, 3, b:b + 1], ACT.Ln, bias=eps_col[:, :], scale=1.0 / D).then_inc(post_ln, 1)
                act.wait_ge(post_ln, b + 1)
                act.activation(cols[:, 3, b:b + 1], cols[:, 3, b:b + 1], ACT.Exp, scale=-0.5).then_inc(post_ready, 1)

        @block.vector
        def _(dve):
            def lo_of(at, slot):
                dve.wait_ge(w_hi, at)
                dve.tensor_tensor(w_slot(1, slot, 0, 4 * P), w_raw[:, slot, :], plain(w_slot(0, slot, 0, 4 * P)),
                                  SUB).then_inc(w_lo, 1)

            def ahead(base, i, stride, j):
                if isinstance(i, int) and base + stride * i + j + SLOTS >= UNITS:
                    return
                slot = (base + j + (stride * i if isinstance(i, int) else 0)) % SLOTS
                lo_of(base + j + SLOTS + 1 + stride * i, slot)

            def zero_acc(n, slot):
                if n:
                    dve.wait_ge(summed, n)
                dve.memset(acc[:, slot, :], 0.0).then_inc(acc_zero, 1)

            def add(n_zero, at, slot=0, rows=slice(0, P), par=0):
                dve.wait_ge(acc_zero, n_zero)
                dve.wait_ge(squared, at + 1)
                if not isinstance(at, int) or at:
                    dve.wait_ge(added, at)
                dve.tensor_tensor(acc[rows, slot, :], acc[rows, slot, :], sq[rows, par, :], ADD).then_inc(added, 1)

            def low(stage, k, gain):
                g = GAIN_AT[gain]
                dve.wait_ge(xg_hi, DC * stage + k + 1)
                dve.scalar_tensor_tensor(xg[:, 1, k, :], xT[:, k, :], gains[:, g + k:g + k + 1],
                                         plain(xg[:, 0, k, :]), MUL, SUB).then_inc(xg_lo, 1)

            def into_x(stage, n, gain, source, pre_gain, between=None):
                g = GAIN_AT[gain]
                dve.wait_ge(rms_ready, n + 1)

                for m in range(DC):
                    tmp = gu[2 + m % 2]
                    at = DC * (stage - 1) + m + 1
                    dve.scalar_tensor_tensor(tmp, source(m), gains[:, g + m:g + m + 1], rms[:, 0, :], MUL, MUL)\
                       .then_inc(y_scaled, 1)
                    if m:
                        low(stage, m - 1, pre_gain)
                    dve.wait_ge(y_scaled, at)
                    dve.tensor_tensor(xT[:, m, :], xT[:, m, :], tmp, ADD).then_inc(x_ready, 1)
                    if m and between:
                        between(m - 1)
                low(stage, DC - 1, pre_gain)
                if between:
                    between(DC - 1)

            def early(base, stride):
                def between(k):
                    if k >= 2:
                        ahead(base, 0, stride, k - 2)
                return between

            def up(f):
                n = N_FFN1_PRE if f == 0 else N_FFN2_PRE

                def step(s, st, first=False):
                    for j in range(EARLY if first else 0, STEP_UNITS):
                        ahead(U_UP[f], s, STEP_UNITS, j)
                    banks = bank[4 * st:4 * st + 4]
                    if first:
                        dve.wait_ge(rms_ready, n + 1)
                    done = U_UP[f] + STEP_UNITS + STEP_UNITS * s
                    dve.wait_ge(w_used, done)
                    for a in range(2):
                        dve.tensor_tensor(gu[a], banks[a][:, :], rms[:, 0, :], MUL).then_inc(gate_out, 1)
                    for a in range(2):
                        dve.tensor_tensor(gu[2 + a], banks[2 + a][:, :], rms[:, 0, :], MUL).then_inc(up_out, 1)
                    for a in range(2):
                        at = 2 * s + (2 * STEPS * f + a + 1)
                        dve.wait_ge(silu_done, at)
                        dve.wait_ge(up_out, at)
                        dve.tensor_tensor(gu[2 + a], gu[a], gu[2 + a], MUL).then_inc(h_f, 1)
                    for a in range(2):
                        at = 2 * s + (2 * STEPS * f + a + 1)
                        dve.wait_ge(h_hi_s, at)
                        dve.tensor_tensor(H[1][:, ds(2 * s + a, 1), :], gu[2 + a].unsqueeze(1),
                                          plain(H[0][:, ds(2 * s + a, 1), :]), SUB).then_inc(h_lo_s, 1)
                step(0, 0, first=True)
                with dve.Fori(0, STEPS // 2) as s2:
                    step(2 * s2 + 1, 1)
                    step(2 * s2 + 2, 0)

            def ple_lo_row(i, slot):
                dve.wait_ge(ple_hi, i + 1)
                dve.tensor_tensor(w_ple[1][:, ds(i, 1), :], ple_raw[slot].unsqueeze(1), plain(w_ple[0][:, ds(i, 1), :]),
                                  SUB).then_inc(ple_lo, 1)

            def down(f):
                n = N_FFN1_POST if f == 0 else N_FFN2_POST
                base = U_DOWN[f] + 4 * BODY_STEPS
                for j in range(4):
                    ahead(U_DOWN[f], 0, 4, j)
                if f == 1:
                    for c in range(2):
                        dve.wait_ge(p_hi, c + 1)
                        dve.tensor_tensor(pT_r[1][:, c, :], pT[c], plain(pT_r[0][:, c, :]), SUB).then_inc(p_lo, 1)
                with dve.Fori(1, BODY_STEPS) as s:
                    if f == 1:
                        for i in range(2):
                            ple_lo_row(2 * s - 2 + i, i)
                    for j in range(4):
                        ahead(U_DOWN[f], s, 4, j)
                zero_acc(n, 0)
                if f == 1:
                    for i in range(2):
                        ple_lo_row(2 * BODY_STEPS - 2 + i, i)
                for j in range(4):
                    ahead(base, 0, 4, j)
                for m in range(4):
                    add(n + 1, 8 * n + m, par=m % 2)
                    dve.tensor_copy(y_low[:, m, :], bank[m + 4][:, :]).then_inc(y_copied, 1)
                for j in range(4, 7):
                    ahead(base, 0, 4, j)
                if f == 1:
                    for i in range(2):
                        ple_lo_row(PLE_UNITS - 2 + i, i)
                for m in range(4, 8):
                    add(n + 1, 8 * n + m, par=m % 2)
                ahead(base, 0, 4, 7)

            def hold_tile_column(c, src):
                scale = HD ** -0.5 if c in (0, 3) else 1.0
                dve.scalar_tensor_tensor(hold[:, c, :], src, scale, rms[:, 0, :], MUL, MUL).then_inc(hold_ready, 1)

            def qk_split(tile, kind):
                for i, (name, c) in enumerate(((("q_sb", 0), ("k_sb", 1)), (("q_fx", 3), ("k_fx", 4)))[kind]):
                    dve.wait_ge(qk_hi, 4 * tile + (2 * kind + i + 1))
                    dve.tensor_tensor(qk[name][1], hold[:, c, :], plain(qk[name][0]), SUB).then_inc(qk_lo, 1)

            def v_split(tile, kind):
                name = ("v_sb", "v_fx")[kind]
                dve.wait_ge(v_hi, 2 * tile + kind + 1)
                dve.tensor_tensor(v_r[name][1], (T_BANK, O_BANK)[kind][:, :], plain(v_r[name][0]), SUB).then_inc(v_lo, 1)

            def aug_rows(hd):
                for i in range(2):
                    dve.tensor_scalar(aug[i], plain(f4[:, :]), pick[:, i, ds(hd, 1)], pick[:, 1 - i, ds(hd, 1)],
                                      MUL, ADD).then_inc(aug_ready, 1)

            def mixer_start():
                for j in range(EARLY, 9):
                    ahead(U_MIX, 0, TILE_UNITS, j)
                    if j == EARLY:
                        dve.wait_ge(wf_hi, 1)
                        cols = [w.rearrange("p a (k n) -> p (a k) n", n=P)[:, :, 0:HEADS] for w in wf_r]
                        dve.tensor_tensor(cols[1], wf_raw, plain(cols[0]), SUB).then_inc(wf_lo, 1)
                dve.memset(scan_ones, 1.0).then_inc(f_step, 1)
                dve.wait_ge(rms_ready, N_MIX_PRE + 1)
                dve.memset(acc[:, 0, :], 0.0).then_inc(acc_zero, 1)
                dve.memset(acc[:, 1, :], 0.0).then_inc(acc_zero, 1)

                def hold_pair(cp):
                    dve.wait_ge(w_used, U_MIX + MIX_FIRST.index((3, cp)) + 1)
                    for c in MIX_PAIRS[cp]:
                        hold_tile_column(c, bank[MIX_BANK[c]][:, :])
                hold_pair(0)
                qk_split(0, 0)
                dve.wait_ge(f_done, 1)
                dve.tensor_tensor(fz, bank[3][0:HEADS, :], rms[0:HEADS, 0, :], MUL).then_inc(f4_ready, 1)
                dve.wait_ge(f4_ready, 1)
                dve.wait_ge(f_act, 3)
                dve.tensor_scalar(fz, fz, b_col[:, :], 0.0, ADD, MIN).then_inc(f_step, 1)
                dve.wait_ge(f_step, 2)
                dve.tensor_tensor(fz, fz, fa, SUB).then_inc(f_step, 1)
                dve.wait_ge(f_step, 3)
                dve.tensor_tensor_scan(fl, scan_ones, fz, 0.0, MUL, ADD).then_inc(f_step, 1)
                hold_pair(2)
                dve.wait_ge(f_act, 4)
                dve.wait_ge(f_step, 4)
                dve.tensor_tensor(f4[32:32 + HEADS, :], fl, plain(f4[0:HEADS, :]), SUB).then_inc(f_step, 1)
                ahead(U_MIX, 0, TILE_UNITS, 9)
                hold_pair(1)
                qk_split(0, 1)
                dve.wait_ge(f_act, 6)
                aug_rows(0)
                ahead(U_MIX, 0, TILE_UNITS, 10)
                v_split(0, 0)
                ahead(U_MIX, 0, TILE_UNITS, 11)

            def mixer_tile(j, more):
                for hh in range(2):
                    hd = 2 * j + hh
                    rows = slice(HD * hh, HD * hh + HD)

                    def unit(x):
                        if more:
                            ahead(U_MIX + TILE_UNITS, j, TILE_UNITS, 6 * hh + x)
                        elif x % 2 == 0:
                            for r, b in zip(PART_AT[hh][x // 2], PART_BANKS[hh][x // 2]):
                                dve.wait_ge(part_hi, r + 1)
                                dve.tensor_tensor(xg[:, 1, r, :], bank[b][:, :], plain(xg[:, 0, r, :]), SUB).then_inc(part_lo, 1)
                                ahead(U_OUT, 0, 0, r)

                    def project_out(g):
                        if more:
                            dve.wait_ge(w_used, U_MIX + TILE_UNITS + 6 * hh + 2 * g + 2 + TILE_UNITS * j)
                            hold_tile_column(3 * hh + g, G_BANK[:, :])
                    for b in range(3):
                        c = slice(512 * b, 512 * b + Z_W[b])
                        dve.wait_ge(lnz, 3 * hd + b + 1)
                        dve.scalar_tensor_tensor(spf[:, c], Z[b][:, 0:Z_W[b]], 0.0, el[:, c], MAX, ADD).then_inc(sp_full, 1)
                    for b in range(3):
                        c = slice(512 * b, 512 * b + Z_W[b])
                        dve.wait_ge(sp_hi, 3 * hd + b + 1)
                        dve.tensor_tensor(sp_r[1][:, c], spf[:, c], plain(sp_r[0][:, c]), SUB).then_inc(sp_lo, 1)
                    if hh == 0:
                        v_split(j, 1)

                    def softmax_max(b):
                        lb, at, w = L_AT[b]
                        dve.reduce_max(stat[:, 0, b:b + 1], L_BANKS[lb % 2][:, at:at + w], AX, negate=True).then_inc(neg_max, 1)
                    dve.wait_ge(l_done, 3 * hd + 1)
                    softmax_max(3)
                    dve.wait_ge(l_done, 3 * hd + 2)
                    softmax_max(2)
                    softmax_max(0)

                    def normalise(i, b):
                        lb, at, w = L_AT[b]
                        c = slice(512 * lb + at, 512 * lb + at + w)
                        dve.wait_ge(p_exp, 4 * hd + i + 1)
                        dve.reciprocal(stat[:, 2, b:b + 1], stat[:, 1, b:b + 1]).then_inc(rcp, 1)
                        dve.wait_ge(rcp, 4 * hd + i + 1)
                        dve.tensor_scalar(pr[:, c], pr[:, c], stat[:, 2, b:b + 1], None, MUL).then_inc(p_scaled, 1)
                    project_out(0)
                    for i, b in enumerate((3, 2, 0)):
                        normalise(i, b)
                    unit(0)
                    unit(1)
                    dve.wait_ge(l_done, 3 * hd + 3)
                    softmax_max(1)
                    for b in range(3):
                        c = slice(512 * b, 512 * b + Z_W[b])
                        dve.wait_ge(a_hi, 3 * hd + b + 1)
                        dve.tensor_tensor(sp_r[1][:, c], el[:, c], plain(sp_r[0][:, c]), SUB).then_inc(a_lo, 1)
                    normalise(3, 1)
                    if more or hh == 0:
                        aug_rows(hd + 1)
                    unit(2)
                    project_out(1)
                    unit(3)
                    if hh == 1 and more:
                        qk_split(j + 1, 0)
                        qk_split(j + 1, 1)

                    def out_lo(kind, gain):
                        at = 8 * N_SB + 2 * hd + kind
                        dve.wait_ge(o_hi, 2 * hd + kind + 1)
                        dve.wait_ge(squared, at + 1)
                        dve.scalar_tensor_tensor(oT[1][rows, ds(j + 4 * kind, 1), :].squeeze(1), O_BANK[rows, :],
                                                 gains[rows, ds(GAIN_AT[gain] + j, 1)],
                                                 plain(oT[0][rows, ds(j + 4 * kind, 1), :].squeeze(1)), MUL, SUB).then_inc(o_out, 1)
                        add(N_FOX + 1, at, slot=kind, rows=rows, par=kind)
                    out_lo(0, "sb_group_g")
                    for b in range(3):
                        c = slice(512 * b, 512 * b + Z_W[b])
                        dve.wait_ge(pt_hi, 3 * hd + b + 1)
                        dve.tensor_tensor(pt_r[1][:, c], (T_BANK, L_BANKS[1], L_BANKS[0])[b][:, 0:Z_W[b]],
                                          plain(pt_r[0][:, c]), SUB).then_inc(pt_lo, 1)
                    unit(4)
                    if hh == 1 and more:
                        v_split(j + 1, 0)
                    project_out(2)
                    unit(5)
                    out_lo(1, "fox_group_g")

            first = GAINS[0][1]
            dve.wait_ge(gains_t, 1)
            dve.tensor_copy(gains[:, 0:first], bank[7][:, 0:first]).then_inc(gains_ready, 1)
            for k in range(DC + 1):
                if k < DC:
                    dve.wait_ge(x_t, k + 1)
                    dve.tensor_copy(xT[:, k, :], bank[k][:, :]).then_inc(x_ready, 1)
                if k:
                    low(0, k - 1, "ffn1_pre_g")
                    if k - 1 < SLOTS:
                        lo_of(k, k - 1)
                    for j in FIRST_AHEAD[k - 1]:
                        ahead(U_UP[0], 0, STEP_UNITS, j)
            dve.wait_ge(gains_t, 2)
            dve.tensor_copy(gains[:, first:GAIN_ROWS], bank[4][:, first:GAIN_ROWS]).then_inc(gains_ready, 1)
            dve.wait_ge(gains_ready, 2)
            for name in ("ffn1_post_g", "ffn2_post_g"):
                post = gains[:, GAIN_AT[name]:GAIN_AT[name] + DC]
                dve.tensor_scalar(post, post, 0.5, None, MUL).then_inc(gains_ready, 1)
            up(0)
            down(0)
            into_x(1, N_FFN1_POST, "ffn1_post_g", lambda m: y_low[:, m, :] if m < 4 else bank[m - 4][:, :],
                   "mix_pre_g", early(U_MIX, TILE_UNITS))
            mixer_start()
            dve.sem_inc(o_out, 1)
            with dve.Fori(0, TILES - 1) as j:
                mixer_tile(j, True)
            mixer_tile(TILES - 1, False)

            for i in range(DC // 2):
                base = U_PAIR + PAIR_UNITS * i
                banks = bank[4 * (i % 2):4 * (i % 2) + 4]

                def out_half(half, a):
                    dve.tensor_tensor(gu[2 * a + half], banks[2 * half + a][:, :], rms[:, half, :], MUL).then_inc(y_half, 1)
                ahead(base, 0, 0, 0)
                if i == 0:
                    ahead(base, 0, 0, 1)
                    dve.wait_ge(rms_ready, N_FOX + 1)
                dve.wait_ge(w_used, base + 1)
                for a in range(2):
                    out_half(0, a)
                if i:
                    ahead(base, 0, 0, 1)
                for a in range(2):
                    if a == 0:
                        dve.wait_ge(fox_done, i + 1)
                    else:
                        dve.wait_ge(w_used, base + 3)
                    out_half(1, a)
                    dve.wait_ge(y_half, 4 * i + 3 + a)
                    dve.tensor_tensor(y_sb[:, 2 * i + a, :], gu[2 * a], gu[2 * a + 1], ADD).then_inc(y_out, 1)
                if i == DC // 2 - 1:
                    for a in range(2):
                        add(N_MIX_POST + 1, 8 * N_MIX_POST + 2 * i + a, par=a)
                ahead(base, 0, 0, 2)
            into_x(2, N_MIX_POST, "mix_post_g", lambda m: y_sb[:, m, :], "ffn2_pre_g", early(U_UP[1], STEP_UNITS))
            up(1)
            down(1)
            into_x(3, N_FFN2_POST, "ffn2_post_g", lambda m: y_low[:, m, :] if m < 4 else bank[m - 4][:, :],
                   "ple_pre_g")

            dve.wait_ge(g_post_loaded, 16)
            dve.wait_ge(e_copied, 2 * TB)
            for b in range(TB):
                for half in range(2):
                    r = 2 * b + half
                    dve.wait_ge(sig_done, r + 1)
                    dve.tensor_tensor(e_tok[TB * half + b], e_tok[TB * half + b], sig[r % 4], MUL).then_inc(e_out, 1)
                    dve.wait_ge(e_out, r + 1)
                    dve.tensor_tensor(sig[r % 4], e_tok[TB * half + b], g_post[:, 512 * half:512 * half + 512], MUL)\
                       .then_inc(eg_out, 1)
                dve.wait_ge(e_squared, 2 * b + 2)
                dve.tensor_tensor(cols[:, 3, b:b + 1], cols[:, 1, b:b + 1], cols[:, 2, b:b + 1], ADD).then_inc(post_sum, 1)
                dve.wait_ge(eg_out, 2 * b + 2)
                dve.wait_ge(post_ready, b + 1)
                for half in range(2):
                    r = 2 * b + half
                    dve.wait_ge(xt_done, r + 1)
                    dve.scalar_tensor_tensor(sig[r % 4], sig[r % 4], cols[:, 3, b:b + 1], bank[XT_BANK[r]][:, :], MUL, ADD)\
                       .then_inc(out_ready, 1)

        @block.tensor
        def _(pe):
            def product(dst, w_hi_ap, w_lo_ap, m_hi, m_lo, start, stop):
                pe.matmul(dst, w_hi_ap, m_hi, start=start, stop=False, skip_group_check=True)
                pe.matmul(dst, w_lo_ap, m_hi, start=False, stop=False, skip_group_check=True)
                return pe.matmul(dst, w_hi_ap, m_lo, start=False, stop=stop, skip_group_check=True)

            def blocks(dst, slot, col, m_hi, m_lo, start, stop):
                return product(dst, w_slot(0, slot, col), w_slot(1, slot, col), m_hi, m_lo, start, stop)

            def first_blocks(k_at, dsts, slot, cols):
                pe.wait_ge(xg_hi, k_at + 1)
                for dst, col in zip(dsts, cols):
                    pe.matmul(dst, w_slot(0, slot, col), xg[:, 0, 0, :], start=True, stop=False, skip_group_check=True)
                    pe.matmul(dst, w_slot(1, slot, col), xg[:, 0, 0, :], start=False, stop=False, skip_group_check=True)
                pe.wait_ge(xg_lo, k_at + 1)
                for dst, col in zip(dsts, cols):
                    pe.matmul(dst, w_slot(0, slot, col), xg[:, 1, 0, :], start=False, stop=False, skip_group_check=True)

            def sum_rows(n, s_bank, slot=0):
                pe.wait_ge(added, 8 * n + 8)
                pe.matmul(s_bank[:, :], ones[:, :], acc[:, slot, :], start=True, stop=True).then_inc(summed, 1)

            def x_in_transpose(half):
                pe.wait_ge(x_loaded[half], 16)
                for k in range(4 * half, 4 * half + 4):
                    if k == 7:
                        pe.wait_ge(gains_ready, 1)
                    for b in range(TB):
                        last = pe.transpose(bank[k][:, b * P:(b + 1) * P], x_in[:, b, k * P:(k + 1) * P], ident[:, :])
                    last.then_inc(x_t, 1)

            def up(f, stage):
                n = N_FFN1_PRE if f == 0 else N_FFN2_PRE

                def step(s, st, number):
                    for q in range(4):
                        for kind in range(2):
                            j = 2 * q + kind
                            pe.wait_ge(w_lo, U_UP[f] + j + 1 + STEP_UNITS * s)
                            if number == 0 and j < 2 and f == 0:
                                pe.wait_ge(x_ready, 2 * j + 2)
                            if number == 1 and j == 0 and f == 0:
                                pe.wait_ge(gains_ready, 4)
                            if number == 1 and j == 1:
                                pe.wait_ge(ln_done, n + 1)
                            if number >= 2 and q == 0:
                                pe.wait_ge(up_out, 2 * STEPS * f + 2 * s - 2)
                            for kk in range(2):
                                k = 2 * q + kk
                                if number == 0 and j == 0 and k == 0:
                                    first_blocks(DC * stage, [bank[a][:, :] for a in range(2)], 0, [0, P])
                                    continue
                                if number == 0:
                                    pe.wait_ge(xg_lo, DC * stage + k + 1)
                                for a in range(2):
                                    last = blocks(bank[4 * st + 2 * kind + a][:, :], j % SLOTS, 256 * kk + P * a,
                                                  xg[:, 0, k, :], xg[:, 1, k, :], k == 0, k == DC - 1)
                            last.then_inc(w_used, 1)
                            if number == 0 and f == 0 and j == 0:
                                x_in_transpose(1)
                            if number == 0 and f == 0 and j == 4:
                                pe.wait_ge(gains_loaded, 16 * (len(GAINS) - 1))
                                pe.wait_ge(x_ready, 5)
                                pe.transpose(bank[4][:, 0:GAIN_ROWS], gains_in, ident[0:GAIN_ROWS, 0:GAIN_ROWS])\
                                  .then_inc(gains_t, 1)
                            if number == 0 and j == 6:
                                sum_rows(n, bank[7])
                            if number == 3 and f == 1 and j == 3:
                                pe.wait_ge(p_loaded, 16)
                                pe.wait_ge(up_out, 4 * STEPS - 2)
                                for c in range(2):
                                    for b in range(TB):
                                        tr = pe.transpose(bank[6 + c][:, b * P:(b + 1) * P], p_in[:, b, c * P:(c + 1) * P],
                                                          ident[:, :])
                                    tr.then_inc(p_t, 1)
                step(0, 0, 0)
                step(1, 1, 1)
                with pe.Fori(0, STEPS // 2 - 1) as s2:
                    step(2 * s2 + 2, 0, 2)
                    step(2 * s2 + 3, 1, 2)
                step(STEPS - 1, 0, 3)

            def down(f):
                n = N_FFN1_POST if f == 0 else N_FFN2_POST

                def unit(u, slot, chunk, half, start=False, stop=False):
                    pe.wait_ge(w_lo, u + 1)
                    pe.wait_ge(h_lo_s, 2 * STEPS * f + 1 + chunk)
                    hid = [x[:, ds(chunk, 1), :].squeeze(1) for x in H]
                    for mm in range(4):
                        last = blocks(bank[(4 * half + mm + 4) % 8][:, :], slot, P * mm, hid[0], hid[1], start, stop)
                        if stop and mm < 3:
                            last.then_inc(y_done, 1)
                    last.then_inc(w_used, 1)
                if f == 1:
                    pe.wait_ge(p_copied, 2)
                for j in range(4):
                    half, c = divmod(j, 2)
                    if c == 0:
                        pe.wait_ge(up_out, 2 * STEPS * f + 20 + 2 * half)
                    unit(U_DOWN[f] + j, j, c, half, start=c == 0)
                with pe.Fori(1, BODY_STEPS) as s:
                    for j in range(4):
                        unit(U_DOWN[f] + j + 4 * s, j, 2 * s + j % 2, j // 2)
                for j in range(TAIL_UNITS):
                    half, c = divmod(j, 2 * TAIL_STEPS)
                    u = U_DOWN[f] + 4 * BODY_STEPS + j
                    unit(u, u % SLOTS, 2 * BODY_STEPS + c, half, stop=c == 2 * TAIL_STEPS - 1)
                pe.wait_ge(y_copied, 4 * f + 1)
                sum_rows(n, bank[4])

            def mixer_start():
                started = set()
                pe.wait_ge(y_copied, 4)
                for j, (kp, cp) in enumerate(MIX_FIRST):
                    pe.wait_ge(w_lo, U_MIX + j + 1)
                    for kk in range(2):
                        k = 2 * kp + kk
                        if j == 0 and k == 0:
                            started.update((0, 1))
                            first_blocks(DC, [bank[MIX_BANK[c]][:, :] for c in range(2)], U_MIX % SLOTS, [0, P])
                            continue
                        pe.wait_ge(xg_lo, DC + k + 1)
                        for cc in range(2):
                            c = MIX_PAIRS[cp][cc]
                            if c not in started:
                                started.add(c)
                                if MIX_BANK[c] == 4:
                                    pe.wait_ge(ln_done, N_FFN1_POST + 1)
                                if MIX_BANK[c] < 4:
                                    pe.wait_ge(x_ready, DC + MIX_BANK[c] + 5)
                            last = blocks(bank[MIX_BANK[c]][:, :], (U_MIX + j) % SLOTS, 256 * kk + P * cc,
                                          xg[:, 0, k, :], xg[:, 1, k, :], k == 0, k == DC - 1)
                    last.then_inc(w_used, 1)
                    if j == 8:
                        sum_rows(N_MIX_PRE, bank[2])
                        pe.wait_ge(xg_lo, 2 * DC)
                        pe.wait_ge(wf_lo, 1)
                        wf = [w.rearrange("p a (k n) -> p (a k) n", n=P) for w in wf_r]
                        for k in range(DC):
                            last = product(bank[3][:, :], wf[0][:, k, :], wf[1][:, k, :], xg[:, 0, k, :], xg[:, 1, k, :],
                                           k == 0, k == DC - 1)
                        last.then_inc(f_done, 1)
                pe.wait_ge(f4_ready, 1)
                pe.wait_ge(hold_ready, 5)
                v_transpose(0)

            def v_transpose(kind):
                c, b = ((2, T_BANK), (5, O_BANK))[kind]
                for s in range(TB):
                    last = pe.transpose(b[:, s * P:(s + 1) * P], hold[:, c, s * P:(s + 1) * P], ident[:, :])
                last.then_inc(v_t, 1)

            def mixer_tile(j, more):
                for hh in range(2):
                    hd = 2 * j + hh
                    rows = slice(HD * hh, HD * hh + HD)

                    def project(g, halves=(0, 1)):
                        if not more:
                            return
                        for kh in halves:
                            x = 6 * hh + 2 * g + kh
                            pe.wait_ge(w_lo, U_MIX + TILE_UNITS + x + 1 + TILE_UNITS * j)
                            if kh == 0:
                                pe.wait_ge(hold_ready, 6 + 3 * hh + g + 6 * j)
                            for kk in range(4):
                                k = 4 * kh + kk
                                last = blocks(G_BANK[:, :], x % SLOTS, P * kk, xg[:, 0, k, :], xg[:, 1, k, :],
                                              k == 0, k == DC - 1)
                            last.then_inc(w_used, 1)

                    def parts(x):
                        if more:
                            return
                        for r, b in zip(PART_AT[hh][x], PART_BANKS[hh][x]):
                            pe.wait_ge(w_lo, U_OUT + r + 1)
                            if b == 7:
                                pe.wait_ge(v_lo, 2 * TILES - 1)
                            if b == 0:
                                pe.wait_ge(a_exp, 3 * hd + 2)
                            if b == 4 and r:
                                pe.wait_ge(part_lo, r - 1)
                            for k in range(TILES - 1):
                                last = blocks(bank[b][:, :], (U_OUT + r) % SLOTS, P * k, oT[0][:, k, :], oT[1][:, k, :],
                                              k == 0, k == TILES - 2)
                            last.then_inc(w_used, 1)

                    if hh == 0:
                        pe.wait_ge(qk_lo, 4 * j + 2)
                    pe.wait_ge(a_exp, 3 * hd + 1)
                    if not more and hh == 1:
                        pe.wait_ge(part_lo, PART_AT[1][0][0])
                    kt, qt = qk["k_sb"], qk["q_sb"]
                    for b in range(3):
                        for c in Z_BANKS[b]:
                            _, at, w = Z_AT[c]
                            dst = Z[b][:, at:at + w]
                            product(dst, kt[0][rows, c * P:(c + 1) * P], kt[1][rows, c * P:(c + 1) * P],
                                    qt[0][rows, c * P:SEQ], qt[1][rows, c * P:SEQ], at == 0, False)
                            last = pe.matmul(Z[b][:, at:at + P], ident_r, mask_sb, start=False, stop=True, skip_group_check=True)
                        last.then_inc(z_done, 1)
                    if hh == 0:
                        pe.wait_ge(qk_lo, 4 * j + 4)

                    def logits(b):
                        lb, at, w = L_AT[b]
                        lbank = L_BANKS[lb % 2]
                        dst = lbank[:, at:at + w]
                        qf, kf = qk["q_fx"], qk["k_fx"]
                        product(dst, qf[0][rows, b * P:(b + 1) * P], qf[1][rows, b * P:(b + 1) * P],
                                kf[0][rows, 0:w], kf[1][rows, 0:w], at == 0, False)
                        pe.matmul(dst, aug[0][:, b * P:(b + 1) * P], aug[1][:, 0:w], start=False, stop=False, skip_group_check=True)
                        return pe.matmul(lbank[:, at + b * P:at + (b + 1) * P], ident_r, mask_fx, start=False, stop=True,
                                         skip_group_check=True)
                    pe.wait_ge(aug_ready, 2 * hd + 2)
                    logits(3).then_inc(l_done, 1)
                    logits(2)
                    logits(0).then_inc(l_done, 1)
                    if hh == 0:
                        pe.wait_ge(hold_ready, 6 * j + 6)
                        pe.wait_ge(o_out, 2 * hd + 1)
                        v_transpose(1)
                    project(0)
                    parts(0)
                    pe.wait_ge(sp_lo, 3 * hd + 3)
                    for c in range(TB):
                        b, at, w = Z_AT[c]
                        for jc in range(c, TB):
                            jb, jat, jw = Z_AT[jc]
                            off = at + (jc - c) * P
                            lhs = tri_r if jc == c else full_r
                            for part in range(2):
                                last = pe.matmul(Z[b][:, off:off + jw], lhs, sp_r[part][:, 512 * jb + jat:512 * jb + jat + jw],
                                                 start=False, stop=(jc == TB - 1 and part == 1), skip_group_check=True)
                    last.then_inc(tri_done, 1)

                    pe.wait_ge(p_exp, 4 * hd + 1)
                    logits(1).then_inc(l_done, 1)
                    project(1)
                    parts(1)

                    def weigh(v, a):
                        for c in range(TB):
                            b, at, w = Z_AT[c]
                            first = 512 * b + at
                            last = product(O_BANK[:, c * P:SEQ], v[0][:, c * P:(c + 1) * P], v[1][:, c * P:(c + 1) * P],
                                           a[0][:, first:first + w], a[1][:, first:first + w], c == 0, c == TB - 1)
                        last.then_inc(o_done, 1)
                    pe.wait_ge(a_lo, 3 * hd + 3)
                    pe.wait_ge(o_out, 2 * hd + 1)
                    if hh == 0:
                        pe.wait_ge(v_lo, 2 * j + 2)
                    weigh(v_r["v_sb"], sp_r)
                    pe.wait_ge(p_scaled, 4 * hd + 4)
                    if not more:
                        pe.wait_ge(part_lo, PART_AT[hh][0][-1] + 1)
                    for b in range(3):
                        tbank = (T_BANK, L_BANKS[1], L_BANKS[0])[b]
                        for c in Z_BANKS[b]:
                            _, at, w = Z_AT[c]
                            for q in range(c, TB):
                                lb, lat, _ = L_AT[q]
                                first = 512 * lb + lat + c * P
                                last = pe.transpose(tbank[:, at + (q - c) * P:at + (q - c + 1) * P],
                                                    pr[:, first:first + P], ident[:, :])
                        last.then_inc(pt_done, 1)
                    project(2)
                    parts(2)
                    if hh == 1 and more:
                        pe.wait_ge(pt_lo, 3 * hd + 1)
                        pe.wait_ge(hold_ready, 6 * j + 9)
                        v_transpose(0)
                    pe.wait_ge(pt_lo, 3 * hd + 3)
                    pe.wait_ge(o_out, 2 * hd + 2)
                    weigh(v_r["v_fx"], pt_r)

            pe.wait_ge(consts, CONSTS)
            pe.wait_ge(first_gains_loaded, 16)
            rows = GAINS[0][1]
            pe.transpose(bank[7][:, 0:rows], gains_in[0:rows, :], ident[0:rows, 0:rows]).then_inc(gains_t, 1)
            x_in_transpose(0)
            pe.wait_ge(const_hi, 1)
            up(0, 0)
            down(0)
            mixer_start()
            pe.sem_inc(o_done, 1)
            with pe.Fori(0, TILES - 1) as j:
                mixer_tile(j, True)
            mixer_tile(TILES - 1, False)

            pe.wait_ge(part_lo, PARTS)
            for i in range(DC // 2):
                base = U_PAIR + PAIR_UNITS * i
                banks = bank[4 * (i % 2):4 * (i % 2) + 4]
                if i == 0:
                    pe.wait_ge(o_out, 2 * HEADS)
                if i == 1:
                    pe.wait_ge(ln_done, N_FOX + 1)
                if i >= 2:
                    pe.wait_ge(y_out, 2 * i - 2)
                pe.wait_ge(w_lo, base + 1)
                for a in range(2):
                    for part in range(2):
                        pe.matmul(banks[a][:, :], ident_r, xg[:, part, 2 * i + a, :], start=part == 0, stop=False,
                                  skip_group_check=True)
                    last = blocks(banks[a][:, :], base % SLOTS, P * a, oT[0][:, TILES - 1, :], oT[1][:, TILES - 1, :],
                                  False, True)
                last.then_inc(w_used, 1)
                if i == 0:
                    pe.wait_ge(o_out, 2 * HEADS + 1)
                for q in range(2):
                    pe.wait_ge(w_lo, base + 2 + q)
                    for a, kk in ((0, 0), (0, 1), (1, 0), (1, 1)):
                        k = 2 * q + kk
                        last = blocks(banks[2 + a][:, :], (base + 1 + q) % SLOTS, 2 * P * kk + P * a,
                                      oT[0][:, TILES + k, :], oT[1][:, TILES + k, :], k == 0, k == TILES - 1)
                        if a == 0 and k == TILES - 1:
                            last.then_inc(fox_done, 1)
                    last.then_inc(w_used, 1)
                    if i == 0 and q == 0:
                        pe.wait_ge(added, 8 * N_FOX + 8)
                        pe.matmul(bank[6][:, :], ones[:, :], acc[:, 0, :], start=True, stop=True).then_inc(summed, 1)
                        pe.matmul(bank[7][:, :], ones[:, :], acc[:, 1, :], start=True, stop=True).then_inc(summed, 1)
            sum_rows(N_MIX_POST, bank[0])
            up(1, 2)
            down(1)

            pe.wait_ge(y_copied, 8)
            pe.wait_ge(p_lo, 2)
            for r in range(2 * TB):
                half, b = divmod(r, TB)
                tok = slice(b * P, (b + 1) * P)
                pe.wait_ge(ple_lo, 2 * half + 2)
                if r == 3:
                    pe.wait_ge(ln_done, N_FFN2_POST + 1)
                if r >= 4:
                    pe.wait_ge(e_copied, r - 3)
                for k in range(2):
                    last = product(bank[PROJ_BANK[r]][:, :], pT_r[0][:, k, tok], pT_r[1][:, k, tok],
                                   w_ple[0][:, 2 * half + k, :], w_ple[1][:, 2 * half + k, :], k == 0, k == 1)
                last.then_inc(e_done, 1)

            def gate(r, k):
                b, half = divmod(r, 2)
                tok = slice(b * P, (b + 1) * P)
                row = 4 + 2 * k + half
                last = product(bank[GATE_BANK[r]][:, :], xg[:, 0, k, tok], xg[:, 1, k, tok], w_ple[0][:, row, :],
                               w_ple[1][:, row, :], k == 0, k == DC - 1)
                if k == DC - 1:
                    last.then_inc(gate_done, 1)

            def x_transpose(r):
                b, half = divmod(r, 2)
                for k in range(4):
                    last = pe.transpose(bank[XT_BANK[r]][:, k * P:(k + 1) * P], xT[:, 4 * half + k, b * P:(b + 1) * P],
                                        ident[:, :])
                last.then_inc(xt_done, 1)
            pe.wait_ge(e_copied, 2 * TB)
            for k in range(DC):
                pe.wait_ge(xg_lo, 3 * DC + k + 1)
                pe.wait_ge(ple_lo, 4 + 2 * k + 2)
                for r in range(4):
                    gate(r, k)
            pe.wait_ge(added, 8 * N_PLE_PRE + 8)
            for b in range(TB):
                last = pe.matmul(bank[0][:, b:b + 1], acc[:, 0, b * P:(b + 1) * P], ones[:, 0:1], start=True, stop=True)
            last.then_inc(summed, 1)
            for r in range(4):
                if XT_BANK[r] == 0:
                    pe.wait_ge(pre_ln, 1)
                x_transpose(r)
            for r in range(4, 8):
                pe.wait_ge(sig_done, r - 3)
                for k in range(DC):
                    gate(r, k)
                for x in {5: (4, 5), 6: (6, 7)}.get(r, ()):
                    pe.wait_ge(out_ready, x - 3)
                    x_transpose(x)


NAMES = ["x", "p", "ffn1_pre_g", "ffn1_w_gate", "ffn1_w_up", "ffn1_w_down", "ffn1_post_g", "mix_pre_g", "w_in",
         "b_forget", "sb_group_g", "fox_group_g", "w_out", "mix_post_g", "ffn2_pre_g", "ffn2_w_gate", "ffn2_w_up",
         "ffn2_w_down", "ffn2_post_g", "ple_pre_g", "w_ple_gate", "w_ple_proj", "ple_post_g"]


def kernel(**inputs):
    import numpy as np
    import concourse.bacc as bacc
    from concourse.bass_utils import run_bass_kernel_spmd

    nc = bacc.Bacc("TRN2", target_bir_lowering=False, num_devices=1)
    arrays, tensors = {}, {}
    for name in NAMES:
        arrays[f"in_{name}"] = np.ascontiguousarray(inputs[name])
        tensors[name] = nc.dram_tensor(f"in_{name}", arrays[f"in_{name}"].shape, mybir.dt.float32, kind="ExternalInput").ap()
    out = nc.dram_tensor("out_x", (1, SEQ, D), mybir.dt.float32, kind="ExternalOutput").ap()
    build(nc, tensors, out)
    result = run_bass_kernel_spmd(nc, [arrays], core_ids=[0])
    return result.results[0]["out_x"]
```
